# Optimizing a Trainium2 kernel written in Bass

```python
import jax, jax.numpy as jnp
from jax import lax
import numpy as np
import math

D_MODEL = 1024
BATCH = 1
SEQ = 512
DEPTH = 2

N_MIXERS = 2
N_RG_LAYERS = (DEPTH + 1) // 2
N_NSA_LAYERS = DEPTH // 2
RMS_EPS = 1e-6
D_FF = 4 * D_MODEL
D_RNN = D_MODEL
RG_BLOCKS = 4
RG_BLOCK_W = D_RNN // RG_BLOCKS
CONV_W = 4
RG_C = 8.0
N_HEADS = 16
HEAD_DIM = D_MODEL // N_HEADS
N_KV_GROUPS = 4
HEADS_PER_GROUP = N_HEADS // N_KV_GROUPS
CMP_LEN = 32
CMP_STRIDE = 16
CMP_RATIO = CMP_LEN // CMP_STRIDE
SLC_LEN = 64
N_SELECT = 16
WINDOW = 512
Q_BLOCK = 128
Q_COLS = N_HEADS * HEAD_DIM
KV_COLS = N_KV_GROUPS * HEAD_DIM
GATE_COLS = 3 * N_HEADS
NSA_IN_COLS = Q_COLS + 6 * KV_COLS + GATE_COLS
ALIBI_MAX = 8.0
NEG_INF = -1e30
FORCE_BONUS = 1e4


def _rmsnorm(x, g):
    xf = x.astype(jnp.float32)
    y = xf * lax.rsqrt(jnp.mean(xf * xf, axis=-1, keepdims=True) + RMS_EPS)
    return (y * g.astype(jnp.float32)).astype(x.dtype)

def _masked_softmax(s, mask):
    s = jnp.where(mask, s, NEG_INF)
    m = jnp.max(s, axis=-1, keepdims=True)
    p = jnp.where(mask, jnp.exp(s - m), 0.0)
    return p / jnp.maximum(jnp.sum(p, axis=-1, keepdims=True), 1e-30)

def _alibi_slopes():
    h = jnp.arange(1, N_HEADS + 1, dtype=jnp.float32)
    return jnp.exp2(-ALIBI_MAX * h / N_HEADS).reshape(N_KV_GROUPS, HEADS_PER_GROUP)

def _sq_relu_mlp(h, w_up, w_down):
    u = jax.nn.relu(h @ w_up)
    return (u * u) @ w_down

def _causal_depthwise_conv(x, w, b):
    y = lax.conv_general_dilated(
        x, w[:, None, :].astype(x.dtype), window_strides=(1,),
        padding=[(CONV_W - 1, 0)], dimension_numbers=('NWC', 'WIO', 'NWC'),
        feature_group_count=x.shape[-1])
    return y + b

def _lru_combine(left, right):
    a_l, b_l = left
    a_r, b_r = right
    return a_l * a_r, a_r * b_l + b_r

def _rglru_mixer(h, w_in, conv_w, conv_b, w_a, b_a, w_x, b_x, lam, w_out):
    B, S, _ = h.shape
    proj = h @ w_in
    y = jax.nn.gelu(proj[..., :D_RNN], approximate=True)
    xb = _causal_depthwise_conv(proj[..., D_RNN:], conv_w, conv_b)
    xr = xb.reshape(B, S, RG_BLOCKS, RG_BLOCK_W)
    r = jax.nn.sigmoid(jnp.einsum('bsnc,ncd->bsnd', xr, w_a).reshape(B, S, D_RNN) + b_a)
    i = jax.nn.sigmoid(jnp.einsum('bsnc,ncd->bsnd', xr, w_x).reshape(B, S, D_RNN) + b_x)
    log_a = -RG_C * r.astype(jnp.float32) * jax.nn.softplus(-lam.astype(jnp.float32))
    a = jnp.exp(log_a)
    u = jnp.sqrt(-jnp.expm1(2.0 * log_a)) * (i * xb).astype(jnp.float32)
    _, hs = lax.associative_scan(_lru_combine, (a, u), axis=1)
    return (hs.astype(h.dtype) * y) @ w_out

def _compress(z, pe, w1, w2):
    B, S, G, DH = z.shape
    n_chunk = S // CMP_STRIDE
    nc = n_chunk - CMP_RATIO + 1
    chunks = z.reshape(B, n_chunk, CMP_STRIDE, G, DH)
    blocks = jnp.concatenate([chunks[:, r:r + nc] for r in range(CMP_RATIO)], axis=2)
    blocks = blocks + pe[None, None, :, None, :]
    flat = jnp.transpose(blocks, (0, 1, 3, 2, 4)).reshape(B, nc, G, CMP_LEN * DH)
    return jax.nn.gelu(flat @ w1, approximate=True) @ w2

def _cmp_to_slc_map(nc, nb):
    cs = jnp.arange(nc) * CMP_STRIDE
    ss = jnp.arange(nb) * SLC_LEN
    ov = jnp.minimum(cs[:, None] + CMP_LEN, ss[None, :] + SLC_LEN) - jnp.maximum(cs[:, None], ss[None, :])
    return (jnp.maximum(ov, 0) / CMP_STRIDE).astype(jnp.float32)

def _nsa_attend(q, gates, k_c, v_c, k_s, v_s, k_w, v_w):
    B, S = q.shape[0], q.shape[1]
    nqb = S // Q_BLOCK
    nc = k_c.shape[1]
    nb = k_s.shape[2]
    n_sel = min(N_SELECT, nb)
    G, Hg, DH = N_KV_GROUPS, HEADS_PER_GROUP, HEAD_DIM
    qx = q.reshape(B * nqb, Q_BLOCK, G, Hg, DH)
    gx = gates.reshape(B * nqb, Q_BLOCK, G, Hg, 3)
    slopes = _alibi_slopes()[:, :, None, None]
    cmp_map = _cmp_to_slc_map(nc, nb)
    cmp_end = jnp.arange(nc) * CMP_STRIDE + (CMP_LEN - 1)
    blk_ids = jnp.arange(nb)
    key_off = jnp.arange(SLC_LEN)
    win_off = jnp.arange(WINDOW + Q_BLOCK)
    gi = jnp.arange(G)[:, None, None]
    scale = HEAD_DIM ** -0.5
    zero = jnp.zeros((), jnp.int32)

    def step(args):
        idx, q_blk, g_blk = args
        b = idx // nqb
        qb = idx % nqb
        t = qb * Q_BLOCK + jnp.arange(Q_BLOCK)
        qf = q_blk.astype(jnp.float32) * scale

        kc = lax.dynamic_index_in_dim(k_c, b, 0, keepdims=False).astype(jnp.float32)
        vc = lax.dynamic_index_in_dim(v_c, b, 0, keepdims=False).astype(jnp.float32)
        d_c = t[:, None] - cmp_end[None, :]
        s_c = jnp.einsum('qghd,ngd->ghqn', qf, kc) - slopes * d_c.astype(jnp.float32)
        p_c = _masked_softmax(s_c, d_c >= 0)
        o_c = jnp.einsum('ghqn,ngd->qghd', p_c, vc)

        imp = jnp.einsum('ghqn,nj->gqj', p_c, cmp_map)
        cur = t // SLC_LEN
        forced = (blk_ids[None, :] == 0) | (blk_ids[None, :] == cur[:, None]) | (blk_ids[None, :] == cur[:, None] - 1)
        score = jnp.where(blk_ids[None, :] <= cur[:, None], imp + FORCE_BONUS * forced, -1.0)
        sel = lax.top_k(score, n_sel)[1]
        sel_ok = sel <= cur[None, :, None]

        ks = lax.dynamic_index_in_dim(k_s, b, 0, keepdims=False)
        vs = lax.dynamic_index_in_dim(v_s, b, 0, keepdims=False)
        k_sel = ks[gi, sel].astype(jnp.float32).reshape(G, Q_BLOCK, n_sel * SLC_LEN, DH)
        v_sel = vs[gi, sel].astype(jnp.float32).reshape(G, Q_BLOCK, n_sel * SLC_LEN, DH)
        pos = (sel[..., None] * SLC_LEN + key_off).reshape(G, Q_BLOCK, n_sel * SLC_LEN)
        d_s = t[None, :, None] - pos
        m_s = (d_s >= 0) & jnp.repeat(sel_ok, SLC_LEN, axis=-1)
        s_s = jnp.einsum('qghd,gqkd->ghqk', qf, k_sel) - slopes * d_s[:, None].astype(jnp.float32)
        p_s = _masked_softmax(s_s, m_s[:, None])
        o_s = jnp.einsum('ghqk,gqkd->qghd', p_s, v_sel)

        kw = lax.dynamic_slice(k_w, (b, qb * Q_BLOCK, zero, zero), (1, WINDOW + Q_BLOCK, G, DH))[0].astype(jnp.float32)
        vw = lax.dynamic_slice(v_w, (b, qb * Q_BLOCK, zero, zero), (1, WINDOW + Q_BLOCK, G, DH))[0].astype(jnp.float32)
        s_pos = qb * Q_BLOCK - WINDOW + win_off
        d_w = t[:, None] - s_pos[None, :]
        m_w = (d_w >= 0) & (d_w < WINDOW) & (s_pos[None, :] >= 0)
        s_w = jnp.einsum('qghd,kgd->ghqk', qf, kw) - slopes * d_w.astype(jnp.float32)
        p_w = _masked_softmax(s_w, m_w)
        o_w = jnp.einsum('ghqk,kgd->qghd', p_w, vw)

        g = g_blk.astype(jnp.float32)
        o = g[..., 0:1] * o_c + g[..., 1:2] * o_s + g[..., 2:3] * o_w
        return o.reshape(Q_BLOCK, N_HEADS * HEAD_DIM)

    out = lax.map(step, (jnp.arange(B * nqb, dtype=jnp.int32), qx, gx))
    return out.reshape(B, S, N_HEADS * HEAD_DIM)

def _nsa_mixer(h, w_in, b_gate, pe_k, pe_v, w1_k, w2_k, w1_v, w2_v, w_out):
    B, S, _ = h.shape
    proj = h @ w_in
    q = proj[..., :Q_COLS].reshape(B, S, N_KV_GROUPS, HEADS_PER_GROUP, HEAD_DIM)
    kv = proj[..., Q_COLS:Q_COLS + 6 * KV_COLS].reshape(B, S, 6, N_KV_GROUPS, HEAD_DIM)
    gates = jax.nn.sigmoid(proj[..., Q_COLS + 6 * KV_COLS:] + b_gate).reshape(B, S, N_HEADS, 3)
    k_c = _compress(kv[:, :, 0], pe_k, w1_k, w2_k)
    v_c = _compress(kv[:, :, 1], pe_v, w1_v, w2_v)
    nb = S // SLC_LEN
    k_s = jnp.transpose(kv[:, :, 2].reshape(B, nb, SLC_LEN, N_KV_GROUPS, HEAD_DIM), (0, 3, 1, 2, 4))
    v_s = jnp.transpose(kv[:, :, 3].reshape(B, nb, SLC_LEN, N_KV_GROUPS, HEAD_DIM), (0, 3, 1, 2, 4))
    pad = ((0, 0), (WINDOW, 0), (0, 0), (0, 0))
    k_w = jnp.pad(kv[:, :, 4], pad)
    v_w = jnp.pad(kv[:, :, 5], pad)
    o = _nsa_attend(q, gates, k_c, v_c, k_s, v_s, k_w, v_w)
    return o.astype(h.dtype) @ w_out

def first_inputs(seed: int = 0) -> dict:
    key = jax.random.key(seed)
    ks = jax.random.split(key, 24)
    f32 = jnp.float32
    nrm = lambda k, shape, s: jax.random.normal(k, shape, f32) * s
    u = jax.random.uniform(ks[11], (N_RG_LAYERS, D_RNN), f32, minval=0.9, maxval=0.999)
    sig = u ** (1.0 / RG_C)
    return {
        'x': nrm(ks[0], (BATCH, SEQ, D_MODEL), 1.0),
        'norm_mix': 1.0 + nrm(ks[1], (DEPTH, D_MODEL), 0.02),
        'norm_ffn': 1.0 + nrm(ks[2], (DEPTH, D_MODEL), 0.02),
        'norm_final': 1.0 + nrm(ks[3], (D_MODEL,), 0.02),
        'rg_w_in': nrm(ks[4], (N_RG_LAYERS, D_MODEL, 2 * D_RNN), D_MODEL ** -0.5),
        'rg_conv_w': nrm(ks[5], (N_RG_LAYERS, CONV_W, D_RNN), CONV_W ** -0.5),
        'rg_conv_b': nrm(ks[6], (N_RG_LAYERS, D_RNN), 0.01),
        'rg_w_a': nrm(ks[7], (N_RG_LAYERS, RG_BLOCKS, RG_BLOCK_W, RG_BLOCK_W), RG_BLOCK_W ** -0.5),
        'rg_b_a': nrm(ks[8], (N_RG_LAYERS, D_RNN), 0.01),
        'rg_w_x': nrm(ks[9], (N_RG_LAYERS, RG_BLOCKS, RG_BLOCK_W, RG_BLOCK_W), RG_BLOCK_W ** -0.5),
        'rg_b_x': nrm(ks[10], (N_RG_LAYERS, D_RNN), 0.01),
        'rg_lambda': jnp.log(sig) - jnp.log1p(-sig),
        'rg_w_out': nrm(ks[12], (N_RG_LAYERS, D_RNN, D_MODEL), D_RNN ** -0.5),
        'nsa_w_in': nrm(ks[13], (N_NSA_LAYERS, D_MODEL, NSA_IN_COLS), D_MODEL ** -0.5),
        'nsa_b_gate': nrm(ks[14], (N_NSA_LAYERS, GATE_COLS), 0.01),
        'nsa_pe_k': nrm(ks[15], (N_NSA_LAYERS, CMP_LEN, HEAD_DIM), 0.02),
        'nsa_pe_v': nrm(ks[16], (N_NSA_LAYERS, CMP_LEN, HEAD_DIM), 0.02),
        'nsa_w1_k': nrm(ks[17], (N_NSA_LAYERS, CMP_LEN * HEAD_DIM, HEAD_DIM), (CMP_LEN * HEAD_DIM) ** -0.5),
        'nsa_w2_k': nrm(ks[18], (N_NSA_LAYERS, HEAD_DIM, HEAD_DIM), HEAD_DIM ** -0.5),
        'nsa_w1_v': nrm(ks[19], (N_NSA_LAYERS, CMP_LEN * HEAD_DIM, HEAD_DIM), (CMP_LEN * HEAD_DIM) ** -0.5),
        'nsa_w2_v': nrm(ks[20], (N_NSA_LAYERS, HEAD_DIM, HEAD_DIM), HEAD_DIM ** -0.5),
        'nsa_w_out': nrm(ks[21], (N_NSA_LAYERS, N_HEADS * HEAD_DIM, D_MODEL), (N_HEADS * HEAD_DIM) ** -0.5),
        'mlp_w_up': nrm(ks[22], (DEPTH, D_MODEL, D_FF), D_MODEL ** -0.5),
        'mlp_w_down': nrm(ks[23], (DEPTH, D_FF, D_MODEL), D_FF ** -0.5),
    }

def first_block(x, norm_mix, norm_ffn, norm_final,
              rg_w_in, rg_conv_w, rg_conv_b, rg_w_a, rg_b_a, rg_w_x, rg_b_x, rg_lambda, rg_w_out,
              nsa_w_in, nsa_b_gate, nsa_pe_k, nsa_pe_v, nsa_w1_k, nsa_w2_k, nsa_w1_v, nsa_w2_v, nsa_w_out,
              mlp_w_up, mlp_w_down):
    for i in range(DEPTH):
        h = _rmsnorm(x, norm_mix[i])
        j = i // N_MIXERS
        if i % N_MIXERS == 0:
            x = x + _rglru_mixer(h, rg_w_in[j], rg_conv_w[j], rg_conv_b[j], rg_w_a[j], rg_b_a[j],
                                 rg_w_x[j], rg_b_x[j], rg_lambda[j], rg_w_out[j])
        else:
            x = x + _nsa_mixer(h, nsa_w_in[j], nsa_b_gate[j], nsa_pe_k[j], nsa_pe_v[j],
                               nsa_w1_k[j], nsa_w2_k[j], nsa_w1_v[j], nsa_w2_v[j], nsa_w_out[j])
        h = _rmsnorm(x, norm_ffn[i])
        x = x + _sq_relu_mlp(h, mlp_w_up[i], mlp_w_down[i])
    return _rmsnorm(x, norm_final)


CHUNK = 64
D_FF_2 = 2816
NORM_EPS = 1e-6

A_HEADS = 4
A_QK_DIM = 64
A_V_DIM = 2 * A_QK_DIM
A_WIDTH = A_HEADS * A_V_DIM
A_COLS = 3 * A_WIDTH

B_HEAD_DIM = 64
B_WIDTH = D_MODEL - A_WIDTH
B_HEADS = B_WIDTH // B_HEAD_DIM
B_DECAY_RANK = 64
B_A_RANK = 64
B_GATE_RANK = 128
B_VRES_RANK = 32
B_LN_EPS = 64e-5
B_COLS = 3 * B_WIDTH + B_DECAY_RANK + B_A_RANK + B_GATE_RANK
B_SPLITS = [B_WIDTH, 2 * B_WIDTH, 3 * B_WIDTH, 3 * B_WIDTH + B_DECAY_RANK,
            3 * B_WIDTH + B_DECAY_RANK + B_A_RANK]
EVEN_IN = A_COLS + B_COLS

C_HEADS = 4
C_QK_DIM = D_MODEL // C_HEADS
C_V_DIM = 2 * C_QK_DIM
C_QK_WIDTH = C_HEADS * C_QK_DIM
C_V_WIDTH = C_HEADS * C_V_DIM
ODD_IN = 2 * C_QK_WIDTH + 2 * C_V_WIDTH

N_EVEN = (DEPTH + 1) // 2
N_ODD = DEPTH // 2


def rms_norm(x, g, eps=NORM_EPS):
    xf = x.astype(jnp.float32)
    y = xf * lax.rsqrt(jnp.mean(xf * xf, axis=-1, keepdims=True) + eps)
    return (y * g.astype(jnp.float32)).astype(x.dtype)

def swiglu(x, w_gu, w_d):
    gate, up = jnp.split(x @ w_gu, 2, axis=-1)
    return (jax.nn.silu(gate) * up) @ w_d

def token_shift(z, mu):
    z_prev = jnp.pad(z, ((0, 0), (1, 0), (0, 0)))[:, :-1]
    return z + (z_prev - z) * mu

def diff_attention(q, k, v, lam):
    S_ = q.shape[1]
    q = q * (A_QK_DIM ** -0.5)
    slopes = 2.0 ** (-8.0 / A_HEADS * jnp.arange(1, A_HEADS + 1, dtype=jnp.float32))
    pos = jnp.arange(S_)
    chunk_id = pos // CHUNK
    outs = []
    for s0 in range(0, S_, Q_BLOCK):
        kend = s0 + Q_BLOCK
        scores = jnp.einsum('bqhmd,bkhmd->bhmqk', q[:, s0:kend], k[:, :kend]).astype(jnp.float32)
        dist = jnp.abs(pos[s0:kend][:, None] - pos[:kend][None, :]).astype(jnp.float32)
        bias = -slopes[:, None, None, None] * dist
        allowed = chunk_id[:kend][None, :] <= chunk_id[s0:kend][:, None]
        scores = jnp.where(allowed, scores + bias, -jnp.inf)
        p = jax.nn.softmax(scores, axis=-1)
        p = p[:, :, 0] - lam * p[:, :, 1]
        outs.append(jnp.einsum('bhqk,bkhe->bqhe', p.astype(v.dtype), v[:, :kend]))
    return jnp.concatenate(outs, axis=1)

def rwkv7_recurrence(r, w, k, v, kk, a):
    Bn, _, H, N = r.shape

    def step(state, inp):
        r_t, w_t, k_t, v_t, kk_t, a_t = inp
        sa = jnp.einsum('bhvk,bhk->bhv', state, -kk_t)
        state = (state * w_t[:, :, None, :]
                 + sa[..., None] * (kk_t * a_t)[:, :, None, :]
                 + v_t[..., None] * k_t[:, :, None, :])
        return state, jnp.einsum('bhvk,bhk->bhv', state, r_t)

    xs = tuple(jnp.moveaxis(t, 1, 0) for t in (r, w, k, v, kk, a))
    state0 = jnp.zeros((Bn, H, N, N), jnp.float32)
    _, y = lax.scan(step, state0, xs)
    return jnp.moveaxis(y, 0, 1)

def head_group_norm(y, w, b):
    Bn, S_ = y.shape[:2]
    mean = jnp.mean(y, axis=-1, keepdims=True)
    var = jnp.mean(jnp.square(y - mean), axis=-1, keepdims=True)
    yn = (y - mean) * lax.rsqrt(var + B_LN_EPS)
    return yn.reshape(Bn, S_, -1) * w + b

def rwkv7_time_mix(zb, mu, vec, w_up, a_up, g_up, v_first, vres):
    Bn, S_, _ = zb.shape
    f32 = jnp.float32
    zs = token_shift(zb.astype(f32), mu.astype(f32))
    r, k, v, xw, xa, xg = jnp.split(zs, B_SPLITS, axis=-1)
    w0, a0, k_k, k_a, r_k, ln_w, ln_b = vec.astype(f32)
    w = -jax.nn.softplus(-(w0 + jnp.tanh(xw) @ w_up.astype(f32))) - 0.5
    decay = jnp.exp(-jnp.exp(w))
    if vres is not None:
        v0, v_down, v_up = vres
        v = v + (v_first - v) * jax.nn.sigmoid(v0.astype(f32) + (v @ v_down.astype(f32)) @ v_up.astype(f32))
    a = jax.nn.sigmoid(a0 + xa @ a_up.astype(f32))
    g = jax.nn.sigmoid(xg) @ g_up.astype(f32)
    heads = lambda t: t.reshape(Bn, S_, B_HEADS, B_HEAD_DIM)
    kk = heads(k * k_k)
    kk = kk / jnp.maximum(jnp.sqrt(jnp.sum(kk * kk, axis=-1, keepdims=True)), 1e-12)
    k = k * (1.0 + (a - 1.0) * k_a)
    rh, kh, vh = heads(r), heads(k), heads(v)
    y = rwkv7_recurrence(rh, heads(decay), kh, vh, kk, heads(a))
    y = head_group_norm(y, ln_w, ln_b)
    r_k_h = r_k.reshape(B_HEADS, B_HEAD_DIM)
    bonus = jnp.sum(rh * kh * r_k_h, axis=-1, keepdims=True) * vh
    y = y + bonus.reshape(Bn, S_, B_WIDTH)
    return y * g, v

def diff_rwkv_mixer(h, w_in, w_out, lam_vecs, subln, lam_init, mu, vec, w_up, a_up, g_up, v_first, vres):
    Bn, S_, _ = h.shape
    z = h @ w_in
    za, zb = z[..., :A_COLS], z[..., A_COLS:]
    qa, ka, va = jnp.split(za, 3, axis=-1)
    qa = qa.reshape(Bn, S_, A_HEADS, 2, A_QK_DIM)
    ka = ka.reshape(Bn, S_, A_HEADS, 2, A_QK_DIM)
    va = va.reshape(Bn, S_, A_HEADS, A_V_DIM)
    lv = lam_vecs.astype(jnp.float32)
    lam = jnp.exp(jnp.sum(lv[0] * lv[1])) - jnp.exp(jnp.sum(lv[2] * lv[3])) + lam_init
    oa = diff_attention(qa, ka, va, lam)
    oa = rms_norm(oa, subln) * (1.0 - lam_init)
    ob, v_b = rwkv7_time_mix(zb, mu, vec, w_up, a_up, g_up, v_first, vres)
    mix = jnp.concatenate([oa.reshape(Bn, S_, A_WIDTH), ob.astype(h.dtype)], axis=-1)
    return mix @ w_out, v_b

def retention(q, k, v):
    Bn, S_, H, _ = q.shape
    dk, dv = q.shape[-1], v.shape[-1]
    n_chunks = S_ // CHUNK
    log_g = jnp.log(1.0 - 2.0 ** (-5.0 - jnp.arange(H, dtype=jnp.float32)))
    idx = jnp.arange(CHUNK, dtype=jnp.float32)
    intra = jnp.exp(log_g[:, None, None] * jnp.abs(idx[:, None] - idx[None, :]))
    q_decay = jnp.exp(log_g[:, None] * (idx + 1.0))
    k_decay = jnp.exp(log_g[:, None] * (CHUNK - 1.0 - idx))
    chunk_decay = jnp.exp(log_g * CHUNK)

    def to_chunks(t):
        return t.reshape(Bn, n_chunks, CHUNK, H, t.shape[-1]).transpose(1, 0, 3, 2, 4)

    def step(state, inp):
        qc, kc, vc = inp
        scores = jnp.einsum('bhid,bhjd->bhij', qc, kc) * intra
        y = (jnp.einsum('bhij,bhjv->bhiv', scores, vc)
             + jnp.einsum('bhid,bhdv->bhiv', qc, state) * q_decay[:, :, None])
        state = (state * chunk_decay[:, None, None]
                 + jnp.einsum('bhjd,bhjv->bhdv', kc * k_decay[:, :, None], vc))
        return state, y

    state0 = jnp.zeros((Bn, H, dk, dv), jnp.float32)
    _, y = lax.scan(step, state0, (to_chunks(q), to_chunks(k), to_chunks(v)))
    return y.transpose(1, 0, 3, 2, 4).reshape(Bn, S_, H, dv)

def retention_mixer(h, w_in, w_out):
    Bn, S_, _ = h.shape
    z = (h @ w_in).astype(jnp.float32)
    q, k, v, g = jnp.split(z, [C_QK_WIDTH, 2 * C_QK_WIDTH, 2 * C_QK_WIDTH + C_V_WIDTH], axis=-1)
    q = q.reshape(Bn, S_, C_HEADS, C_QK_DIM)
    k = k.reshape(Bn, S_, C_HEADS, C_QK_DIM) * (C_QK_DIM ** -0.5)
    v = v.reshape(Bn, S_, C_HEADS, C_V_DIM)
    y = retention(q, k, v)
    y = y * lax.rsqrt(jnp.mean(y * y, axis=-1, keepdims=True) + NORM_EPS)
    y = jax.nn.silu(g) * y.reshape(Bn, S_, C_V_WIDTH)
    return y.astype(h.dtype) @ w_out

def second_inputs(seed: int = 0) -> dict:
    key = jax.random.key(seed)
    ks = jax.random.split(key, 24)
    nrm = lambda k, shape, s: s * jax.random.normal(k, shape, jnp.float32)
    x = nrm(ks[0], (BATCH, SEQ, D_MODEL), 1.0)
    norms = 1.0 + nrm(ks[1], (DEPTH, 6, D_MODEL), 0.05)
    ffn_wgu = nrm(ks[2], (DEPTH, 2, D_MODEL, 2 * D_FF_2), D_MODEL ** -0.5)
    ffn_wd = nrm(ks[3], (DEPTH, 2, D_FF_2, D_MODEL), D_FF_2 ** -0.5)
    even_w_in = nrm(ks[4], (N_EVEN, D_MODEL, EVEN_IN), D_MODEL ** -0.5)
    even_w_out = nrm(ks[5], (N_EVEN, D_MODEL, D_MODEL), D_MODEL ** -0.5)
    diff_lam = nrm(ks[6], (N_EVEN, 4, A_QK_DIM), 0.1)
    diff_subln = 1.0 + nrm(ks[7], (N_EVEN, A_V_DIM), 0.05)
    rwkv_mu = jax.random.uniform(ks[8], (N_EVEN, B_COLS), jnp.float32)
    vshape = (N_EVEN, B_WIDTH)
    w0 = jnp.linspace(-6.0, -1.0, B_WIDTH, dtype=jnp.float32)[None, :] + nrm(ks[9], vshape, 0.1)
    a0 = nrm(ks[10], vshape, 0.1)
    k_k = 0.85 + nrm(ks[11], vshape, 0.05)
    k_a = 1.0 + nrm(ks[12], vshape, 0.05)
    r_k = nrm(ks[13], vshape, 0.1)
    ln_w = 1.0 + nrm(ks[14], vshape, 0.05)
    ln_b = nrm(ks[15], vshape, 0.02)
    rwkv_vec = jnp.stack([w0, a0, k_k, k_a, r_k, ln_w, ln_b], axis=1)
    rwkv_w_up = nrm(ks[16], (N_EVEN, B_DECAY_RANK, B_WIDTH), 0.1 * B_DECAY_RANK ** -0.5)
    rwkv_a_up = nrm(ks[17], (N_EVEN, B_A_RANK, B_WIDTH), 0.5 * B_A_RANK ** -0.5)
    rwkv_g_up = nrm(ks[18], (N_EVEN, B_GATE_RANK, B_WIDTH), B_GATE_RANK ** -0.5)
    rwkv_v0 = nrm(ks[19], (N_EVEN - 1, B_WIDTH), 0.1)
    rwkv_v_down = nrm(ks[20], (N_EVEN - 1, B_WIDTH, B_VRES_RANK), B_WIDTH ** -0.5)
    rwkv_v_up = nrm(ks[21], (N_EVEN - 1, B_VRES_RANK, B_WIDTH), 0.5 * B_VRES_RANK ** -0.5)
    odd_w_in = nrm(ks[22], (N_ODD, D_MODEL, ODD_IN), D_MODEL ** -0.5)
    odd_w_out = nrm(ks[23], (N_ODD, C_V_WIDTH, D_MODEL), C_V_WIDTH ** -0.5)
    return {'x': x, 'norms': norms, 'ffn_wgu': ffn_wgu, 'ffn_wd': ffn_wd,
            'even_w_in': even_w_in, 'even_w_out': even_w_out,
            'diff_lam': diff_lam, 'diff_subln': diff_subln,
            'rwkv_mu': rwkv_mu, 'rwkv_vec': rwkv_vec,
            'rwkv_w_up': rwkv_w_up, 'rwkv_a_up': rwkv_a_up, 'rwkv_g_up': rwkv_g_up,
            'rwkv_v0': rwkv_v0, 'rwkv_v_down': rwkv_v_down, 'rwkv_v_up': rwkv_v_up,
            'odd_w_in': odd_w_in, 'odd_w_out': odd_w_out}

def second_block(x, norms, ffn_wgu, ffn_wd, even_w_in, even_w_out, diff_lam, diff_subln,
              rwkv_mu, rwkv_vec, rwkv_w_up, rwkv_a_up, rwkv_g_up,
              rwkv_v0, rwkv_v_down, rwkv_v_up, odd_w_in, odd_w_out):
    v_first = None
    for i in range(DEPTH):
        g = norms[i]
        x = x + 0.5 * rms_norm(swiglu(rms_norm(x, g[0]), ffn_wgu[i, 0], ffn_wd[i, 0]), g[1])
        h = rms_norm(x, g[2])
        j = i // 2
        if i % 2 == 0:
            lam_init = 0.8 - 0.6 * math.exp(-0.3 * i)
            vres = None if j == 0 else (rwkv_v0[j - 1], rwkv_v_down[j - 1], rwkv_v_up[j - 1])
            mix, v_b = diff_rwkv_mixer(h, even_w_in[j], even_w_out[j], diff_lam[j], diff_subln[j],
                                       lam_init, rwkv_mu[j], rwkv_vec[j], rwkv_w_up[j],
                                       rwkv_a_up[j], rwkv_g_up[j], v_first, vres)
            if j == 0:
                v_first = v_b
        else:
            mix = retention_mixer(h, odd_w_in[j], odd_w_out[j])
        x = x + rms_norm(mix, g[3])
        x = x + 0.5 * rms_norm(swiglu(rms_norm(x, g[4]), ffn_wgu[i, 1], ffn_wd[i, 1]), g[5])
    return x


def setup_inputs(seed=0):
    out = dict(first_inputs(seed))
    for name, value in second_inputs(seed + 1).items():
        if name != "x":
            out[name + "_2"] = value
    return out


def reference(
    x, norm_mix, norm_ffn, norm_final, rg_w_in, rg_conv_w, rg_conv_b, rg_w_a, rg_b_a, rg_w_x,
    rg_b_x, rg_lambda, rg_w_out, nsa_w_in, nsa_b_gate, nsa_pe_k, nsa_pe_v, nsa_w1_k, nsa_w2_k,
    nsa_w1_v, nsa_w2_v, nsa_w_out, mlp_w_up, mlp_w_down, norms_2, ffn_wgu_2, ffn_wd_2,
    even_w_in_2, even_w_out_2, diff_lam_2, diff_subln_2, rwkv_mu_2, rwkv_vec_2, rwkv_w_up_2,
    rwkv_a_up_2, rwkv_g_up_2, rwkv_v0_2, rwkv_v_down_2, rwkv_v_up_2, odd_w_in_2, odd_w_out_2,
):
    x = first_block(
        x, norm_mix, norm_ffn, norm_final, rg_w_in, rg_conv_w, rg_conv_b, rg_w_a, rg_b_a,
        rg_w_x, rg_b_x, rg_lambda, rg_w_out, nsa_w_in, nsa_b_gate, nsa_pe_k, nsa_pe_v, nsa_w1_k,
        nsa_w2_k, nsa_w1_v, nsa_w2_v, nsa_w_out, mlp_w_up, mlp_w_down,
    )
    return second_block(
        x, norms_2, ffn_wgu_2, ffn_wd_2, even_w_in_2, even_w_out_2, diff_lam_2, diff_subln_2,
        rwkv_mu_2, rwkv_vec_2, rwkv_w_up_2, rwkv_a_up_2, rwkv_g_up_2, rwkv_v0_2, rwkv_v_down_2,
        rwkv_v_up_2, odd_w_in_2, odd_w_out_2,
    )


_drawn_inputs = setup_inputs


def setup_inputs(seed=0):
    import zlib

    import numpy as np

    out = dict(_drawn_inputs(seed))
    spreads = {}
    factors = {'rg_b_a': 34.253,
     'rg_b_x': 8.0,
     'nsa_b_gate': 8.0,
     'nsa_pe_k': 64.0,
     'nsa_pe_v': 5.154,
     'rwkv_w_up_2': 6.517}
    for name, (base, spread) in spreads.items():
        noise = np.random.default_rng([zlib.crc32(name.encode()), seed]).standard_normal(out[name].shape)
        drawn = base * np.exp(spread * noise) if base else spread * noise
        out[name] = __import__('jax').numpy.asarray(drawn.astype(out[name].dtype))
    for name, factor in factors.items():
        out[name] = (out[name] * factor).astype(out[name].dtype)
    return out
```

```python
from contextlib import ExitStack
import math

import concourse.bass as bass
from concourse import mybir

F32 = mybir.dt.float32
F32R = mybir.dt.float32r
ACT = mybir.ActivationFunctionType
ALU = mybir.AluOpType
AX = mybir.AxisListType

P = 128
S = 512
D = 1024
KT = D // P
QT = S // P
CH = 2048
BIG = -1e30
EPS = 1e-6

HEADS, HD, GROUPS = 16, 64, 4
CMP_LEN, CMP_STRIDE = 32, 16
NC = S // CMP_STRIDE - 1
DFF = 4 * D
RG_C = 8.0
DFF2 = 2816
RCH = 64


def build(nc, a, out):
    ctx = ExitStack()
    with ctx:
        def sb(name, shape, dt=F32):
            return ctx.enter_context(nc.sbuf_tensor(name, shape, dt))

        def sem(name):
            return ctx.enter_context(nc.semaphore(name))

        x = sb("x", [P, KT, S])
        raw = sb("raw", [P, 2, CH])
        whi = sb("whi", [P, 2, CH], F32R)
        wlo = sb("wlo", [P, 2, CH], F32R)
        split_zone = sb("split_zone", [P, 24 * S])
        zone = nc.sbuf_base - 24 * S * 4
        h_hi = nc.alloc_sbuf_tensor_at("h_hi", [P, KT, S], F32R, offset=zone)
        h_lo = nc.alloc_sbuf_tensor_at("h_lo", [P, KT, S], F32R, offset=zone + 8 * S * 4)
        u_hi = nc.alloc_sbuf_tensor_at("u_hi", [P, 4, S], F32R, offset=zone + 16 * S * 4)
        u_lo = nc.alloc_sbuf_tensor_at("u_lo", [P, 4, S], F32R, offset=zone + 20 * S * 4)
        fsum = sb("fsum", [P, KT, S])
        tmp = sb("tmp", [P, 8, S])
        ident = sb("ident", [P, P])
        ones = sb("ones", [P, P])
        par = sb("par", [P, 3, P])
        eps = sb("eps", [P, 4])
        AR = 14848
        arena = sb("arena", [P, AR])
        pbank = [ctx.enter_context(nc.psum_tensor(f"bank{i}", [P, S], F32)) for i in range(8)]

        def tiles(at, n, w=S):
            return arena[:, at:at + n * w].rearrange("p (t n) -> p t n", n=w)

        loaded = [sem("loaded0"), sem("loaded1")]
        hi_ready = sem("hi_ready")
        lo_ready = sem("lo_ready")
        tiles_out = sem("tiles_out")
        done = {k: sem(f"{k}_done") for k in ("pe", "act", "dve", "pool")}
        act_step = sem("act_step")
        dve_step = sem("dve_step")
        pool_step = sem("pool_step")
        const_in = sem("const_in")
        small_in = sem("small_in")
        stored = sem("stored")
        gate_done = sem("gate_done")
        prod_done = sem("prod_done")
        uhi_done = sem("uhi_done")
        ulo_done = sem("ulo_done")
        added = sem("added")
        n_sq = sem("n_sq")
        n_mm = sem("n_mm")
        n_rt = sem("n_rt")
        n_hn = sem("n_hn")
        n_hi = sem("n_hi")
        n_lo = sem("n_lo")
        s_pe = sem("s_pe")
        s_act = sem("s_act")
        s_dve = sem("s_dve")
        s_pool = sem("s_pool")

        def at(c, i, k):
            return c if i is None else i * k + c

        class Chain:

            def __init__(self, eng, own):
                self.eng, self.own, self.n = eng, own, 0

            def __call__(self, ins):
                ins.then_inc(self.own, 1)
                self.n += 1
                self.eng.wait_ge(self.own, self.n)

        stream = []
        where = {}

        def cols(w, c, n=256, kt=KT):
            return w.rearrange("(k p) n -> p k n", p=P)[:, :, c:c + n]

        def whole(k, n):
            return lambda slot: raw[:, slot, 0:k * n].rearrange("p (k n) -> p k n", k=k)

        def add_chunks(name, srcs, outs):
            where[name] = len(stream)
            for src in srcs:
                stream.append(([(whole(src.shape[1], src.shape[2]), src)], outs))

        def ffn_chunks(name, groups, gu):
            where[name] = len(stream)
            for g in range(groups):
                stream.extend([(None, 2)] * gu)
                if g > 0:
                    stream.append((None, 8))
            stream.append((None, 8))

        rg_in, rg_out = a["rg_w_in"][0], a["rg_w_out"][0]
        nsa_in, nsa_out = a["nsa_w_in"][0], a["nsa_w_out"][0]
        even_in, even_out = a["even_w_in_2"][0], a["even_w_out_2"][0]
        odd_in, odd_out = a["odd_w_in_2"][0], a["odd_w_out_2"][0]
        NG1 = DFF // 256
        NG2 = DFF2 // 256
        FFN = {}

        def mlp(i):
            up = a["mlp_w_up"][i].rearrange("(k p) (c n) -> c p k n", p=P, n=256)
            down = a["mlp_w_down"][i].rearrange("(c k p) n -> c p k n", k=2, p=P)
            return dict(gu=1, groups=NG1, w=[up], down=down, swiglu=False, dst=x)

        def swi(l, i):
            w = a["ffn_wgu_2"][l, i]
            g = w[:, 0:DFF2].rearrange("(k p) (c n) -> c p k n", p=P, n=256)
            u = w[:, DFF2:2 * DFF2].rearrange("(k p) (c n) -> c p k n", p=P, n=256)
            down = a["ffn_wd_2"][l, i].rearrange("(c k p) n -> c p k n", k=2, p=P)
            return dict(gu=2, groups=NG2, w=[g, u], down=down, swiglu=True, dst=fsum)

        PG = dict(mix=0, ffn=16, final=32, conv_w=40, conv_b=72, b_a=80, b_x=88, lam=96)
        PN2, PMU, PSUB, PVEC = 0, 96, 110, 0

        def gain(sec, i):
            return par[:, sec, i:i + 1]

        PLAN = [("setup",), ("norm", x, 0, PG["mix"]), ("rg",), ("norm", x, 0, PG["ffn"]), ("ffn", "f0")]
        FFN["f0"] = mlp(0)
        PLAN += [("norm", x, 0, PG["mix"] + KT), ("nsa",), ("norm", x, 0, PG["ffn"] + KT), ("ffn", "f1")]
        FFN["f1"] = mlp(1)
        PLAN += [("norm_x", 0, PG["final"])]
        for l in range(2):
            n2 = PN2 + l * 6 * KT
            for i in range(2):
                FFN[f"s{l}{i}"] = swi(l, i)
            PLAN += [("norm", x, 1, n2), ("ffn", f"s{l}0"), ("post", 1, n2 + KT, 0.5), ("norm", x, 1, n2 + 2 * KT),
                     (("even",), ("odd",))[l], ("post", 1, n2 + 3 * KT, 1.0), ("norm", x, 1, n2 + 4 * KT),
                     ("ffn", f"s{l}1"), ("post", 1, n2 + 5 * KT, 0.5)]
        PLAN += [("store",)]

        ends = []
        for step in PLAN:
            if step[0] == "rg":
                add_chunks("rg_in", [cols(rg_in, 256 * c) for c in range(8)], 2)
                where["rg_gates"] = len(stream)
                for w in (a["rg_w_a"][0], a["rg_w_x"][0]):
                    stream.append(([((lambda n: lambda slot: raw[:, slot, n * 512:(n + 1) * 512].rearrange(
                        "p (k n) -> p k n", k=2))(n), w[n].rearrange("(k p) n -> p k n", p=P)) for n in range(4)], 8))
                add_chunks("rg_out", [cols(rg_out, 256 * c) for c in range(4)], 2)
            elif step[0] == "ffn":
                ffn_chunks(step[1], FFN[step[1]]["groups"], FFN[step[1]]["gu"])
            elif step[0] == "nsa":
                q_src = nsa_in[:, 0:D].rearrange("(k p) (t h g d) -> t g p k h d", p=P, t=2, h=2, g=4)
                add_chunks("nsa_in", [cols(nsa_in, D), cols(nsa_in, D + 256)], 2)
                for c in range(4):
                    stream.append(([((lambda j: lambda slot: raw[:, slot, :].rearrange(
                        "p (k m h d) -> p k m h d", k=KT, m=2, h=2)[:, :, j // 2, j % 2])(j), q_src[c // 2, 2 * (c % 2) + j // 2][:, :, j % 2, :])
                        for j in range(4)], 2))
                for c in (2, 4):
                    stream.append(([(whole(8, 256), cols(nsa_in, D + 256 * c))], 2))
                for c in (3, 5):
                    stream.append(([(whole(8, 256), cols(nsa_in, D + 256 * c))], 4))
                add_chunks("nsa_out", [cols(nsa_out, 256 * c) for c in range(4)], 2)
            elif step[0] == "even":
                add_chunks("even_a", [cols(even_in, 256 * c) for c in range(4)], 2)
                add_chunks("even_v", [cols(even_in, 1024 + 256 * c) for c in range(2)], 4)
                add_chunks("even_b", [cols(even_in, 1536 + 256 * c) for c in range(7)], 2)
                add_chunks("even_out", [cols(even_out, 256 * c) for c in range(4)], 2)
            elif step[0] == "odd":
                for h in range(4):
                    add_chunks(f"odd{h}", [cols(odd_in, 256 * h), cols(odd_in, 1024 + 256 * h)], 2)
                    for c in range(2):
                        stream.append(([(whole(8, 256), cols(odd_in, 2048 + 512 * h + 256 * c))], 4))
                    for c in range(2):
                        stream.append(([(whole(8, 256), cols(odd_in, 4096 + 512 * h + 256 * c))], 2))
                    wo = odd_out.rearrange("(h k p) n -> h p k n", k=4, p=P)[h]
                    for c in range(2):
                        stream.append(([(whole(4, 512), wo[:, :, 512 * c:512 * c + 512])], 4))
            ends.append(len(stream))
        before = [0]
        landed = []
        for n, (parts, outs) in enumerate(stream):
            before.append(before[-1] + outs)
            landed.append((landed[n - 2] if n > 1 else 0) + 16 * (1 if parts is None else len(parts)))
        TOTAL = len(stream)
        ffn_base, k = {}, 0
        for step in PLAN:
            if step[0] == "ffn":
                ffn_base[step[1]] = k
                k += FFN[step[1]]["groups"]
        norm_base, k = {}, 0
        for i, step in enumerate(PLAN):
            if step[0] in ("norm", "norm_x", "post"):
                norm_base[i] = k
                k += KT

        def enter(e, stage):
            if stage:
                for k in ("pe", "act", "dve", "pool"):
                    e.wait_ge(done[k], stage)

        def leave(e, k):
            e.drain().then_inc(done[k], 1)

        def load_chunk(e, n, i, dn, dt, src=None):
            parts = stream[n][0] if src is None else [(whole(src.shape[1], src.shape[2]), src)]
            if n >= 2:
                e.wait_ge(lo_ready, at(n - 1, i, dn))
            for dst, s in parts:
                e.dma_start(dst(n % 2), s).then_inc(loaded[n % 2], 16)

        def act_hi(e, n, i=None, dn=0, dt=0):
            if i is None and n >= TOTAL:
                return
            e.wait_ge(loaded[n % 2], at(landed[n], i, dn * 8))
            if n >= 2:
                e.wait_ge(tiles_out, at(before[n - 1], i, dt))
            e.activation(whi[:, n % 2, :], raw[:, n % 2, :], ACT.Copy).then_inc(hi_ready, 1)

        def dve_lo(e, n, i=None, dn=0, dt=0):
            if i is None and n >= TOTAL:
                return
            e.wait_ge(hi_ready, at(n + 1, i, dn))
            e.tensor_tensor(wlo[:, n % 2, :], raw[:, n % 2, :], whi[:, n % 2, :].bitcast(F32),
                            ALU.subtract).then_inc(lo_ready, 1)

        def three(pe, o, w_hi, w_lo, r_hi, r_lo, first, last):
            pe.matmul(o, w_hi, r_hi, start=first, stop=False)
            pe.matmul(o, w_hi, r_lo, start=False, stop=False)
            return pe.matmul(o, w_lo, r_hi, start=False, stop=last)

        def pe_chunk(pe, n, kt, mt, hi, lo, outs, free=None, i=None, dn=0, k0=0, first=True, last=True, off=0, ready=True):
            s = n % 2
            if ready:
                pe.wait_ge(lo_ready, at(n + 1, i, dn))
            for m in range(mt):
                if free:
                    free(m)
                for k in range(kt):
                    c = off + k * mt * P + m * P
                    ins = three(pe, outs(m), whi[:, s, c:c + P], wlo[:, s, c:c + P], hi[:, k0 + k, :], lo[:, k0 + k, :],
                                first and k == 0, last and k == kt - 1)
                ins.then_inc(tiles_out, 1)

        def pe_rows(pe, n, outs, free=None):
            s = n % 2
            pe.wait_ge(lo_ready, n + 1)
            for t in range(QT):
                if free:
                    free(t)
                for k in range(KT):
                    c = slice(k * 256, k * 256 + 256)
                    q = slice(t * P, t * P + P)
                    pe.matmul(outs(t), h_hi[:, k, q], whi[:, s, c], start=k == 0, stop=False)
                    pe.matmul(outs(t), h_hi[:, k, q], wlo[:, s, c], start=False, stop=False)
                    ins = pe.matmul(outs(t), h_lo[:, k, q], whi[:, s, c], start=False, stop=k == KT - 1)
                ins.then_inc(tiles_out, 1)

        def ffn_walk(e, name, gu, dn):
            f = FFN[name]
            G, per = f["groups"], f["gu"] + 1
            n0 = where[name]

            def n_gu(g):
                return n0 if g == 0 else n0 + f["gu"] + (g - 1) * per

            def n_dn(g):
                return n0 + f["gu"] + g * per + f["gu"] if g < G - 1 else n0 + G * per - 1
            turns = (G - 1) // 2
            if n0 + G * per == TOTAL and 2 * turns == G - 1:
                turns -= 1
            dt = 2 * (2 * f["gu"] + 8)
            gu(0, n_gu(0), None, 0, 0)
            with e.Fori(0, turns) as i:
                for g in (1, 2):
                    gu(g, n_gu(g), i, 2 * per, dt)
                    dn(g - 1, n_dn(g - 1), i, 2 * per, dt)
            for g in range(2 * turns + 1, G):
                gu(g, n_gu(g), None, 0, 0)
                dn(g - 1, n_dn(g - 1), None, 0, 0)
            dn(G - 1, n_dn(G - 1), None, 0, 0)

        def after_down(name, g):
            gu = FFN[name]["gu"]
            return before[where[name]] + 2 * gu * (g + 2) + 8 * (g + 1)

        def sp_ffn(e, name):
            f = FFN[name]

            def gu(g, n, i, dn, dt):
                for c, w in enumerate(f["w"]):
                    load_chunk(e, n + c, i, dn, dt, w[at(g, i, 2)])

            def down(g, n, i, dn, dt):
                load_chunk(e, n, i, dn, dt, f["down"][at(g, i, 2)])
            ffn_walk(e, name, gu, down)

        def pe_ffn(pe, name):
            f, b = FFN[name], ffn_base[name]

            def gu(g, n, i, dn, dt):
                for c in range(f["gu"]):
                    def free(m):
                        if g > 0:
                            pe.wait_ge(prod_done, at(2 * (b + g - 1) + m + 1, i, 4))
                    pe_chunk(pe, n + c, KT, 2, h_hi, h_lo, lambda m: pbank[2 * c + m][:, :], free, i, dn)

            def down(g, n, i, dn, dt):
                pe.wait_ge(ulo_done, at(2 * (b + g) + 2, i, 4))

                def free(m):
                    pe.wait_ge(added, at(8 * (b + g) + m + 5, i, 16))
                pe_chunk(pe, n, 2, 8, u_hi, u_lo, lambda m: pbank[4 + m % 4][:, :], free, i, dn, k0=2 * (g % 2))
            ffn_walk(pe, name, gu, down)

        def act_ffn(e, name):
            f, b = FFN[name], ffn_base[name]

            def gu(g, n, i, dn, dt):
                for j in range(2):
                    e.wait_ge(tiles_out, at(before[n] + j + 1, i, dt))
                    if g > 0:
                        e.wait_ge(prod_done, at(2 * (b + g - 1) + j + 1, i, 4))
                    e.activation(tmp[:, j, :], pbank[j][:, :], ACT.Silu if f["swiglu"] else ACT.Relu)\
                        .then_inc(gate_done, 1)
                if f["swiglu"]:
                    act_hi(e, n + 2, i, dn, dt)
                for j in range(2):
                    e.wait_ge(prod_done, at(2 * (b + g) + j + 1, i, 4))
                    if g > 0:
                        e.wait_ge(tiles_out, at(after_down(name, g - 2), i, dt))
                    e.activation(u_hi[:, 2 * (g % 2) + j, :], tmp[:, 2 + j, :], ACT.Copy).then_inc(uhi_done, 1)
                act_hi(e, n + f["gu"] + 1, i, dn, dt)

            def down(g, n, i, dn, dt):
                act_hi(e, n + 2, i, dn, dt)
            ffn_walk(e, name, gu, down)

        def dve_ffn(e, name):
            f, b = FFN[name], ffn_base[name]
            dst = f["dst"]

            def gu(g, n, i, dn, dt):
                if f["swiglu"]:
                    dve_lo(e, n + 2, i, dn, dt)
                for j in range(2):
                    e.wait_ge(gate_done, at(2 * (b + g) + j + 1, i, 4))
                    if f["swiglu"]:
                        e.wait_ge(tiles_out, at(before[n + 1] + j + 1, i, dt))
                    if g > 0:
                        e.wait_ge(ulo_done, at(2 * (b + g - 1) + j + 1, i, 4))
                    if f["swiglu"]:
                        ins = e.tensor_tensor(tmp[:, 2 + j, :], pbank[2 + j][:, :], tmp[:, j, :], ALU.mult)
                    else:
                        ins = e.scalar_tensor_tensor(tmp[:, 2 + j, :], pbank[j][:, :], 0.0, tmp[:, j, :],
                                                     ALU.max, ALU.mult)
                    ins.then_inc(prod_done, 1)
                for j in range(2):
                    e.wait_ge(uhi_done, at(2 * (b + g) + j + 1, i, 4))
                    u = 2 * (g % 2) + j
                    e.tensor_tensor(u_lo[:, u, :], tmp[:, 2 + j, :], u_hi[:, u, :].bitcast(F32),
                                    ALU.subtract).then_inc(ulo_done, 1)
                if g == 0:
                    dve_lo(e, n + f["gu"] + 1, i, dn, dt)

            def down(g, n, i, dn, dt):
                final = i is None and g == f["groups"] - 1
                for m in range(8):
                    if m == 4 and not final:
                        dve_lo(e, n + 1, i, dn, dt)
                    e.wait_ge(tiles_out, at(before[n] + m + 1, i, dt))
                    if b + g > 0 or i is not None:
                        e.wait_ge(added, at(8 * (b + g) + m + 1, i, 16))
                    e.tensor_tensor(dst[:, m, :], dst[:, m, :], pbank[4 + m % 4][:, :], ALU.add)\
                        .then_inc(added, 1)
                dve_lo(e, n + 2, i, dn, dt)
            ffn_walk(e, name, gu, down)

        def pe_norm(pe, stage, src):
            b = norm_base[stage]
            for k in range(KT):
                pe.wait_ge(n_sq, b + k + 1)
                pe.matmul(pbank[7][:, :], ones[:, :], tmp[:, k % 4, :], start=k == 0, stop=k == KT - 1)\
                    .then_inc(n_mm, 1)

        def act_norm(e, stage, src, split):
            b = norm_base[stage]
            for k in range(KT):
                if k >= 4:
                    e.wait_ge(n_mm, b + k - 3)
                e.activation(tmp[:, k % 4, :], src[:, k, :], ACT.Square).then_inc(n_sq, 1)
            e.wait_ge(n_mm, b + KT)
            e.activation(tmp[:, 4, :], pbank[7][:, :], ACT.Sqrt, bias=eps[:, 0:1], scale=1.0 / D)\
                .then_inc(n_rt, 1)
            if split:
                for k in range(KT):
                    e.wait_ge(n_hn, b + k + 1)
                    e.activation(h_hi[:, k, :], tmp[:, k % 4, :], ACT.Copy).then_inc(n_hi, 1)

        def dve_norm(e, stage, src, sec, g0, split, chain):
            b = norm_base[stage]
            e.wait_ge(n_rt, b // KT + 1)
            chain(e.reciprocal(tmp[:, 5, :], tmp[:, 4, :]))

            def lo(k):
                e.wait_ge(n_hi, b_split(stage) + k + 1)
                e.tensor_tensor(h_lo[:, k, :], tmp[:, k % 4, :], h_hi[:, k, :].bitcast(F32), ALU.subtract)\
                    .then_inc(n_lo, 1)
            for k in range(KT):
                o = tmp[:, k % 4, :] if split else x[:, k, :]
                if split and k >= 4:
                    e.wait_ge(n_lo, b_split(stage) + k - 3)
                e.scalar_tensor_tensor(o, src[:, k, :], gain(sec, g0 + k), tmp[:, 5, :], ALU.mult, ALU.mult)\
                    .then_inc(n_hn, 1)
                if split and k > 0:
                    lo(k - 1)
            if split:
                lo(KT - 1)

        def b_split(stage):
            return KT * sum(1 for s in PLAN[:stage] if s[0] == "norm")

        def dve_post(e, stage, sec, g0, scale, chain):
            b = norm_base[stage]
            e.wait_ge(n_rt, b // KT + 1)
            chain(e.reciprocal(tmp[:, 5, :], tmp[:, 4, :]))
            for k in range(KT):
                chain(e.scalar_tensor_tensor(tmp[:, k % 4, :], fsum[:, k, :], gain(sec, g0 + k), tmp[:, 5, :],
                                             ALU.mult, ALU.mult))
                e.scalar_tensor_tensor(x[:, k, :], tmp[:, k % 4, :], scale, x[:, k, :], ALU.mult, ALU.add)\
                    .then_inc(n_hn, 1)

        xrows = fsum[:, :, :].rearrange("p t n -> p (t n)").rearrange("p (q c) -> p q c", q=QT)
        prow = tmp[:, 6, :].rearrange("p (r n) -> p r n", n=P)

        def vec(v, n):
            return v.rearrange("(r n) -> r n", n=P) if n == 1 else v.rearrange("l (r n) -> (l r) n", n=P)

        ROWS = [(0, PG["mix"], vec(a["norm_mix"], 2)), (0, PG["ffn"], vec(a["norm_ffn"], 2)),
                (0, PG["final"], vec(a["norm_final"], 1)), (0, PG["conv_w"], vec(a["rg_conv_w"][0], 2)),
                (0, PG["conv_b"], vec(a["rg_conv_b"][0], 1)), (0, PG["b_a"], vec(a["rg_b_a"][0], 1)),
                (0, PG["b_x"], vec(a["rg_b_x"][0], 1)), (0, PG["lam"], vec(a["rg_lambda"][0], 1)),
                (1, PN2, a["norms_2"].rearrange("l i (r n) -> (l i r) n", n=P)),
                (1, PMU, vec(a["rwkv_mu_2"][0], 1)), (1, PSUB, a["diff_subln_2"]),
                (2, PVEC, vec(a["rwkv_vec_2"][0], 2))]

        def sp_setup(e):
            e.wait_ge(pool_step, 1)
            for r, at0, src in ROWS:
                e.dma_start(prow[at0:at0 + src.shape[0], r, :], src).then_inc(const_in, 16)
            for q in range(QT):
                e.dma_start(xrows[:, q, :], a["x"][0].rearrange("(q p) c -> q p c", p=P)[q]).then_inc(const_in, 16)

        def pool_setup(e, chain):
            chain(e.memset(tmp[:, 6, :], 0.0))
            chain(e.memset(ident[:, :], 0.0))
            chain(e.affine_select(out=ident[:, :], in_=ident[:, :], compare_op=ALU.not_equal, fill=1.0, base=0,
                                  pattern=[[-1, P]], channel_multiplier=1))
            e.memset(ones[:, :], 1.0)
            for j, v in enumerate((EPS, 64e-5, 1.0, 0.0)):
                e.memset(eps[:, j:j + 1], v)

        def pe_setup(pe):
            pe.wait_ge(pool_step, 3)
            pe.wait_ge(const_in, 16 * (len(ROWS) + QT))
            for r in range(3):
                pe.transpose(pbank[0][:, r * P:r * P + P], prow[:, r, :], ident[:, :]).then_inc(setup_par, 1)
            for k in range(KT):
                if k == KT - 1:
                    pe.wait_ge(setup_out, 1)
                for q in range(QT):
                    ins = pe.transpose(pbank[(k + 1) % 8][:, q * P:q * P + P], xrows[:, q, k * P:k * P + P],
                                       ident[:, :])
                ins.then_inc(setup_pe, 1)

        def dve_setup(e):
            e.wait_ge(setup_par, 3)
            e.tensor_copy(par[:, :, :].rearrange("p r n -> p (r n)"), pbank[0][:, 0:3 * P]).then_inc(setup_out, 1)
            for k in range(KT):
                e.wait_ge(setup_pe, k + 1)
                e.tensor_copy(x[:, k, :], pbank[(k + 1) % 8][:, :]).then_inc(added, 1)

        def pe_store(pe):
            for t in range(2 * QT):
                q, half = t // 2, t % 2
                for j in range(4):
                    ins = pe.transpose(pbank[t][:, j * P:j * P + P], x[:, 4 * half + j, q * P:q * P + P], ident[:, :])
                ins.then_inc(store_pe, 1)

        def dve_store(e):
            for t in range(2 * QT):
                e.wait_ge(store_pe, t + 1)
                e.tensor_copy(xrows[:, t // 2, (t % 2) * 512:(t % 2) * 512 + 512], pbank[t][:, :])\
                    .then_inc(store_dve, 1)

        def sp_store(e, stage):
            enter(e, stage)
            for q in range(QT):
                e.wait_ge(store_dve, 2 * q + 2)
                e.dma_start(out.rearrange("b (q p) c -> (b q) p c", p=P)[q], xrows[:, q, :]).then_inc(stored, 16)
            e.wait_ge(stored, 16 * QT)

        setup_par = sem("setup_par")
        setup_pe, setup_out, store_pe, store_dve = sem("setup_pe"), sem("setup_out"), sem("store_pe"), sem("store_dve")

        def pe_out(pe, name):
            for c in range(4):
                pe_chunk(pe, where[name] + c, KT, 2, h_hi, h_lo, lambda m: pbank[2 * c + m][:, :])

        def act_out(e, name):
            for c in range(4):
                act_hi(e, where[name] + c + 2)

        def dve_out(e, name, add):
            n = where[name]
            for m in range(KT):
                e.wait_ge(tiles_out, before[n] + m + 1)
                if add:
                    ins = e.tensor_tensor(x[:, m, :], x[:, m, :], pbank[m][:, :], ALU.add)
                else:
                    ins = e.tensor_copy(fsum[:, m, :], pbank[m][:, :])
                ins.then_inc(out_taken, 1)
                if m % 2:
                    dve_lo(e, n + m // 2 + 2)

        out_taken = sem("out_taken")

        rg_act, rg_dve, rg_pool = sem("rg_act"), sem("rg_dve"), sem("rg_pool")
        Y, XB, RR = tiles(0, KT), tiles(8 * S, KT), tiles(16 * S, KT)
        PX = tiles(24 * S, 2, S + 4)
        small = arena[:, 24 * S + 2 * (S + 4):AR]
        GI = fsum
        RA_XH, RA_R, RA_I, RA_T, RA_A, RA_SQ, RA_YH, RA_END = 16, 24, 32, 40, 48, 56, 64, 72

        def pe_rg(pe):
            n0 = where["rg_in"]
            for c in range(8):
                def free(m):
                    if 2 * c + m >= 8:
                        pe.wait_ge(rg_act, 2 * c + m - 7)
                pe_chunk(pe, n0 + c, KT, 2, h_hi, h_lo, lambda m: pbank[(2 * c + m) % 8][:, :], free)
            for g in range(2):
                for b in range(4):
                    pe.wait_ge(rg_dve, 8 + 2 * b + 2)

                    def free(m):
                        if g:
                            pe.wait_ge(rg_act, RA_R + 2 * b + m + 1)
                    pe_chunk(pe, n0 + 8 + g, 2, 2, h_hi, h_lo, lambda m: pbank[2 * b + m][:, :], free, k0=2 * b,
                             off=512 * b)
            pe.wait_ge(rg_dve, RD_END)
            pe_out(pe, "rg_out")

        def act_rg(e, chain):
            n0 = where["rg_in"]
            c8 = small
            lam = par[:, 0, PG["lam"]:PG["lam"] + KT]
            chain(e.activation(c8[:, 0:8], lam, ACT.Abs))
            chain(e.activation(c8[:, 8:16], c8[:, 0:8], ACT.Exp, scale=-1.0))
            chain(e.activation(c8[:, 16:24], c8[:, 8:16], ACT.Ln, bias=eps[:, 2:3]))
            chain(e.activation(c8[:, 24:32], lam, ACT.Relu, scale=-1.0))
            for c in range(8):
                for m in range(2):
                    t = 2 * c + m
                    e.wait_ge(tiles_out, before[n0 + c] + m + 1)
                    if t < 8:
                        e.activation(Y[:, t, :], pbank[t % 8][:, :], ACT.Gelu_apprx_tanh).then_inc(rg_act, 1)
                    else:
                        if t >= 10:
                            e.wait_ge(rg_dve, t - 9)
                        if t == 8:
                            e.wait_ge(rg_pool, 1)
                        e.activation(PX[:, t % 2, 3:3 + S], pbank[t % 8][:, :], ACT.Copy).then_inc(rg_act, 1)
                act_hi(e, n0 + c + 2)
            e.wait_ge(tiles_out, before[n0 + 8])
            for t in range(8):
                e.wait_ge(rg_dve, t + 1)
                e.activation(h_hi[:, t, :], XB[:, t, :], ACT.Copy).then_inc(rg_act, 1)
            for g, (o, b) in enumerate(((RR, PG["b_a"]), (GI, PG["b_x"]))):
                for t in range(8):
                    e.wait_ge(tiles_out, before[n0 + 8 + g] + t + 1)
                    e.activation(o[:, t, :], pbank[t][:, :], ACT.Sigmoid, bias=gain(0, b + t)).then_inc(rg_act, 1)
                act_hi(e, n0 + 8 + g + 2)
            e.wait_ge(rg_dve, 18)
            for t in range(8):
                e.activation(tmp[:, t, :], RR[:, t, :], ACT.Tanh, scale=c8[:, 32 + t:33 + t]).then_inc(rg_act, 1)
            for t in range(8):
                chain(e.activation(RR[:, t, :], RR[:, t, :], ACT.Exp, scale=c8[:, 40 + t:41 + t]))
            for t in range(8):
                e.wait_ge(rg_dve, 18 + t + 1)
                e.activation(XB[:, t, :], XB[:, t, :], ACT.Sqrt).then_inc(rg_act, 1)
            for t in range(8):
                e.wait_ge(rg_dve, 26 + t + 1)
                e.activation(h_hi[:, t, :], Y[:, t, :], ACT.Copy).then_inc(rg_act, 1)
            act_out(e, "rg_out")

        RD_END = 42

        def dve_rg(e, chain):
            n0 = where["rg_in"]
            c8 = small
            for c in range(4):
                dve_lo(e, n0 + c + 2)
            for t in range(8):
                px = PX[:, t % 2, :]
                e.wait_ge(rg_act, 8 + t + 1)
                w = [gain(0, PG["conv_w"] + 8 * j + t) for j in range(4)]
                chain(e.tensor_scalar(XB[:, t, :], px[:, 0:S], w[0], gain(0, PG["conv_b"] + t), ALU.mult, ALU.add))
                for j in (1, 2):
                    chain(e.scalar_tensor_tensor(XB[:, t, :], px[:, j:j + S], w[j], XB[:, t, :], ALU.mult, ALU.add))
                e.scalar_tensor_tensor(XB[:, t, :], px[:, 3:3 + S], w[3], XB[:, t, :], ALU.mult, ALU.add)\
                    .then_inc(rg_dve, 1)
                if t % 2:
                    dve_lo(e, n0 + 4 + t // 2 + 2)
            for t in range(8):
                e.wait_ge(rg_act, RA_XH + t + 1)
                e.tensor_tensor(h_lo[:, t, :], XB[:, t, :], h_hi[:, t, :].bitcast(F32), ALU.subtract)\
                    .then_inc(rg_dve, 1)
            e.wait_ge(act_step, 4)
            chain(e.tensor_tensor(c8[:, 16:24], c8[:, 16:24], c8[:, 24:32], ALU.add))
            e.tensor_scalar(c8[:, 32:40], c8[:, 16:24], RG_C, None, ALU.mult).then_inc(rg_dve, 1)
            e.tensor_scalar(c8[:, 40:48], c8[:, 16:24], -RG_C, None, ALU.mult).then_inc(rg_dve, 1)
            for g in range(2):
                dve_lo(e, n0 + 8 + g + 2)
            for t in range(8):
                e.wait_ge(rg_pool, 1 + t + 1)
                e.wait_ge(rg_act, RA_T + t + 1)
                chain(e.tensor_scalar(XB[:, t, :], tmp[:, t, :], 1.0, None, ALU.add))
                chain(e.reciprocal(XB[:, t, :], XB[:, t, :]))
                e.scalar_tensor_tensor(XB[:, t, :], tmp[:, t, :], 2.0, XB[:, t, :], ALU.mult, ALU.mult)\
                    .then_inc(rg_dve, 1)
            for t in range(8):
                e.wait_ge(rg_act, RA_A + t + 1)
                chain(e.tensor_tensor(XB[:, t, :], XB[:, t, :], GI[:, t, :], ALU.mult))
                e.wait_ge(act_step, 4 + t + 1)
                chain(e.tensor_tensor_scan(tmp[:, t, :], RR[:, t, :], XB[:, t, :], 0.0, ALU.mult, ALU.add))
                e.tensor_tensor(Y[:, t, :], Y[:, t, :], tmp[:, t, :], ALU.mult).then_inc(rg_dve, 1)
            for t in range(8):
                e.wait_ge(rg_act, RA_A + 8 + t + 1)
                e.tensor_tensor(h_lo[:, t, :], Y[:, t, :], h_hi[:, t, :].bitcast(F32), ALU.subtract)\
                    .then_inc(rg_dve, 1)
            dve_out(e, "rg_out", True)

        def pool_rg(e):
            for j in range(2):
                ins = e.memset(PX[:, j, 0:3], 0.0)
            ins.then_inc(rg_pool, 1)
            for t in range(8):
                e.wait_ge(rg_act, RA_I + t + 1)
                e.wait_ge(rg_dve, 8 + t + 1)
                e.tensor_tensor(GI[:, t, :], GI[:, t, :], XB[:, t, :], ALU.mult).then_inc(rg_pool, 1)

        na_proj, na_act, na_dve, na_pool, na_pe = (sem("na_proj"), sem("na_act"), sem("na_dve"), sem("na_pool"),
                                                   sem("na_pe"))
        sc_pe, sc_dve, sc_act = sem("sc_pe"), sem("sc_dve"), sem("sc_act")
        tr_pe, tr_act, tr_dve = sem("tr_pe"), sem("tr_act"), sem("tr_dve")
        pv_pe, cb_dve = sem("pv_pe"), sem("cb_dve")
        cm_pe, cm_dve, cm_max, cm_act = sem("cm_pe"), sem("cm_dve"), sem("cm_max"), sem("cm_act")
        bias_pool = sem("bias_pool")
        o = 0
        qT = tiles(o, 8); o += 8 * S
        zc = tiles(o, 4); o += 4 * S
        ksT = tiles(o, 2); o += 2 * S
        kwT = tiles(o, 2); o += 2 * S
        vs = tiles(o, QT, 256); o += QT * 256
        vw = tiles(o, QT, 256); o += QT * 256
        gates = tiles(o, QT, 48); o += QT * 48
        gz = tiles(o, 2, NC + 1); o += 2 * (NC + 1)
        kcT = tiles(o, 2, NC + 1); o += 2 * (NC + 1)
        vcr = tiles(o, 2, P); o += 2 * P
        dist = arena[:, o:o + S]; o += S
        cdist = tiles(o, QT, NC + 1); o += QT * (NC + 1)
        gw = tiles(o, KT, 48); o += KT * 48
        w2bd = tiles(o, 2, P); o += 2 * P
        peT = tiles(o, 2, CMP_LEN); o += 2 * CMP_LEN
        pbias = arena[:, o:o + 2]; o += 2
        negm = tiles(o, 2, 4); o += 8
        sums = tiles(o, 2, 4); o += 8
        rr = tiles(o, 2, 4); o += 8
        bias_h = tiles(o, 2); o += 2 * S
        cb_h = tiles(o, 2, QT * (NC + 1)); o += 2 * QT * (NC + 1)
        cs = tiles(o, QT, NC + 1); o += QT * (NC + 1)
        csT = arena[:, o:o + S]; o += S
        cmx = arena[:, o:o + QT]; o += QT
        csum = arena[:, o:o + QT]; o += QT
        cout = tiles(o, QT, HD); o += QT * HD
        perow = cout.rearrange("p t n -> p (t n)").rearrange("p (z n) -> p z n", z=2)
        bgate = arena[0:1, o:o + 48]; o += 48
        assert o <= AR
        w1bd = [fsum[:, :, :].rearrange("p t n -> p (t n)").rearrange("p (l e) -> p l e", e=P),
                tmp[:, :, :].rearrange("p t n -> p (t n)").rearrange("p (l e) -> p l e", e=P)]
        orow = xrows
        UNITS = HEADS * QT

        def pool_nsa(e, chain):
            c0 = chain.n
            chain(e.memset(fsum[:, :, :], 0.0))
            chain(e.memset(tmp[:, :, :], 0.0))
            chain(e.memset(w2bd[:, :, :], 0.0))
            for z, (w1, w2, pe_) in enumerate(((a["nsa_w1_k"], a["nsa_w2_k"], a["nsa_pe_k"]),
                                               (a["nsa_w1_v"], a["nsa_w2_v"], a["nsa_pe_v"]))):
                for h in range(2):
                    r = slice(h * HD, h * HD + HD)
                    e.dma_start(w1bd[z][r, :, r], w1[0].rearrange("(l d) e -> d l e", d=HD)).then_inc(small_in, 16)
                    e.dma_start(w2bd[r, z, r], w2[0]).then_inc(small_in, 16)
                    e.dma_start(perow[0:CMP_LEN, z, r], pe_[0]).then_inc(small_in, 16)
            e.dma_start(gw[:, :, :], cols(nsa_in, D + 6 * 256, 48)).then_inc(small_in, 16)
            e.dma_start(bgate, a["nsa_b_gate"]).then_inc(small_in, 16)
            chain(e.iota(dist, pattern=[[1, S]], base=-3 * P, channel_multiplier=-1,
                         allow_small_or_imprecise_dtypes=True))
            chain(e.affine_select(out=dist, in_=dist, compare_op=ALU.is_ge, fill=BIG, base=3 * P,
                                  pattern=[[-1, S]], channel_multiplier=1))
            chain(e.iota(cdist[:, :, 0:NC], pattern=[[-P, QT], [CMP_STRIDE, NC]], base=CMP_LEN - 1,
                         channel_multiplier=-1, allow_small_or_imprecise_dtypes=True))
            chain(e.affine_select(out=cdist[:, :, 0:NC], in_=cdist[:, :, 0:NC], compare_op=ALU.is_ge, fill=BIG,
                                  base=1 - CMP_LEN, pattern=[[P, QT], [-CMP_STRIDE, NC]], channel_multiplier=1))
            for h in range(HEADS):
                slope = 2.0 ** (-8.0 * (h + 1) / HEADS)
                if h >= 2:
                    e.wait_ge(sc_dve, 4 * (h - 1))
                e.tensor_scalar(bias_h[:, h % 2, :], dist, slope, None, ALU.mult)
                e.tensor_scalar(cb_h[:, h % 2, :].rearrange("p (t n) -> p t n", t=QT)[:, :, 0:NC],
                                cdist[:, :, 0:NC], slope, None, ALU.mult).then_inc(bias_pool, 1)

        SMALL_NSA = 16 * 14

        def pe_nsa(pe):
            n0 = where["nsa_in"]
            t = 0
            for c in range(10):
                def free(m):
                    if t + m >= 8:
                        pe.wait_ge(na_proj, t + m - 7)
                if c < 8:
                    pe_chunk(pe, n0 + c, KT, 2, h_hi, h_lo, lambda m: pbank[(t + m) % 8][:, :], free)
                    t += 2
                else:
                    pe_rows(pe, n0 + c, lambda m: pbank[(t + m) % 8][:, 0:256], free)
                    t += 4
            pe.wait_ge(small_in, SMALL_NSA)
            pe.wait_ge(na_dve, 1)
            pe.wait_ge(na_proj, 24)
            for q in range(QT):
                og = pbank[0][:, q * 48:q * 48 + 48]
                pe.matmul(og, ones[0:1, :], bgate, start=True, stop=False)
                for k in range(KT):
                    hq = slice(q * P, q * P + P)
                    gk = slice(k * 48, k * 48 + 48)
                    pe.matmul(og, h_hi[:, k, hq], u_hi[:, 0, gk], start=False, stop=False)
                    pe.matmul(og, h_hi[:, k, hq], u_lo[:, 0, gk], start=False, stop=False)
                    ins = pe.matmul(og, h_lo[:, k, hq], u_hi[:, 0, gk], start=False, stop=k == KT - 1)
            ins.then_inc(na_pe, 1)
            for z in range(2):
                ins = pe.transpose(pbank[1][:, z * 32:z * 32 + 32], perow[0:CMP_LEN, z, :], ident[0:32, 0:32])
            ins.then_inc(na_pe, 1)
            pe.wait_ge(na_act, 2)
            for z in range(2):
                o62 = pbank[2 + z][:, 0:2 * NC].rearrange("p (t n) -> p t n", t=2)
                for l in range(CMP_LEN):
                    pe.matmul(o62, w1bd[z][:, l, :], zc[:, 2 * z:2 * z + 2, l:l + CMP_STRIDE * (NC - 1) + 1:CMP_STRIDE],
                              start=l == 0, stop=l == CMP_LEN - 1)
                for l in range(CMP_LEN):
                    ins = pe.matmul(pbank[2 + z][:, 64:65], w1bd[z][:, l, :], peT[:, z, l:l + 1], start=l == 0,
                                    stop=l == CMP_LEN - 1)
                ins.then_inc(na_pe, 1)
                pe.wait_ge(na_act, 4 + z)
                if z == 0:
                    pe.matmul(pbank[4][:, 0:2 * NC].rearrange("p (t n) -> p t n", t=2), w2bd[:, 0, :],
                              gz[:, :, 0:NC], start=True, stop=True).then_inc(na_pe, 1)
                else:
                    for t2 in range(2):
                        ins = pe.matmul(pbank[5][0:NC, t2 * P:t2 * P + P], gz[:, t2, 0:NC], w2bd[:, 1, :],
                                        start=True, stop=True)
                    ins.then_inc(na_pe, 1)
            pe.wait_ge(na_act, 7)

            def scores(u):
                h, q = u // QT, u % QT
                t2, half, g = h // 8, (h // 4) % 2, h % 4
                r = slice(half * HD, half * HD + HD)
                nk = (q + 1) * P
                lhs = qT[r, 4 * t2 + g, q * P:q * P + P]
                if u >= 2:
                    pe.wait_ge(sc_dve, u - 1)
                pe.matmul(pbank[u % 2][:, 0:nk], lhs, ksT[r, t2, 0:nk], start=True, stop=True)
                pe.matmul(pbank[2 + u % 2][:, 0:nk], lhs, kwT[r, t2, 0:nk], start=True, stop=True).then_inc(sc_pe, 1)

            def turn(u):
                q, p = u % QT, u % 2
                pe.wait_ge(sc_act, u + 1)
                if u >= 1:
                    pe.wait_ge(tr_act, u)
                    pe.wait_ge(tr_dve, u)
                for b in range(2):
                    for k in range(q + 1):
                        kk = slice(k * P, k * P + P)
                        ins = pe.transpose(pbank[4 + b][:, kk], tmp[:, 2 * b + p, kk], ident[:, :])
                ins.then_inc(tr_pe, 1)

            def values(u):
                h, q, p = u // QT, u % QT, u % 2
                t2, G = h // 8, h // 4
                pe.wait_ge(tr_act, u + 1)
                pe.wait_ge(tr_dve, u + 1)
                if u >= 1:
                    pe.wait_ge(cb_dve, u)
                for b, v in enumerate((vs, vw)):
                    for k in range(q + 1):
                        ins = pe.matmul(pbank[7][:, b * HD:b * HD + HD], tmp[:, 4 + 2 * b + p, k * P:k * P + P], v[:, k, G * HD:G * HD + HD],
                                        start=k == 0, stop=k == q)
                ins.then_inc(pv_pe, 1)
            def compressed(h, part):
                t2, half, g = h // 8, (h // 4) % 2, h % 4
                r = slice(half * HD, half * HD + HD)
                if part == 0:
                    if h:
                        pe.wait_ge(cm_dve, 3 * h)
                    for q in range(QT):
                        ins = pe.matmul(pbank[6][:, 32 * q:32 * q + NC], qT[r, 4 * t2 + g, q * P:q * P + P],
                                        kcT[r, t2, 0:NC], start=True, stop=True)
                elif part == 1:
                    pe.wait_ge(cm_dve, 3 * h + 1)
                    pe.wait_ge(cm_act, h + 1)
                    for q in range(QT):
                        ins = pe.transpose(pbank[6][0:NC, q * P:q * P + P], cs[:, q, 0:NC], ident[:, :])
                else:
                    pe.wait_ge(cm_dve, 3 * h + 2)
                    for q in range(QT):
                        ins = pe.matmul(pbank[6][:, q * HD:q * HD + HD], csT[0:NC, q * P:q * P + P],
                                        vcr[0:NC, t2, half * HD:half * HD + HD], start=True, stop=True)
                ins.then_inc(cm_pe, 1)
            for u in range(UNITS + 2):
                if u >= 5 and u % QT == 1:
                    compressed(u // QT - 1, 2)
                if u >= 4 and u % QT == 0:
                    compressed(u // QT - 1, 1)
                if u < UNITS:
                    scores(u)
                if u < UNITS and u % QT == 2:
                    compressed(u // QT, 0)
                if 1 <= u <= UNITS:
                    turn(u - 1)
                if u >= 2:
                    values(u - 2)
            pe.wait_ge(cb_dve, UNITS)
            pe.wait_ge(cm_dve, 3 * HEADS)
            for k in range(KT):
                for q in range(QT):
                    ins = pe.transpose(pbank[k][:, q * P:q * P + P], orow[:, q, k * P:k * P + P], ident[:, :])
                ins.then_inc(na_pe, 1)
            pe.wait_ge(na_dve, 1 + KT)
            pe_out(pe, "nsa_out")

        def act_nsa(e, chain):
            n0 = where["nsa_in"]
            dst = [zc[:, j, :] for j in range(4)] + [qT[:, j, :] for j in range(8)] + [ksT[:, 0, :], ksT[:, 1, :],
                   kwT[:, 0, :], kwT[:, 1, :]] + [vs[:, j, :] for j in range(4)] + [vw[:, j, :] for j in range(4)]
            t = 0
            for c in range(10):
                for m in range(2 if c < 8 else 4):
                    e.wait_ge(tiles_out, before[n0 + c] + m + 1)
                    e.activation(dst[t], pbank[t % 8][:, 0:256 if c >= 8 else S], ACT.Copy,
                                 scale=HD ** -0.5 if 4 <= t < 12 else 1.0).then_inc(na_proj, 1)
                    t += 1
                act_hi(e, n0 + c + 2)
            e.wait_ge(small_in, SMALL_NSA)
            e.activation(u_hi[:, 0, 0:KT * 48], gw[:, :, :].rearrange("p k n -> p (k n)"), ACT.Copy).then_inc(na_act, 1)
            e.wait_ge(na_pe, 2)
            e.activation(peT[:, :, :].rearrange("p z l -> p (z l)"), pbank[1][:, 0:64], ACT.Copy).then_inc(na_act, 1)
            e.activation(gates[:, :, :].rearrange("p q n -> p (q n)"), pbank[0][:, 0:QT * 48], ACT.Sigmoid)\
                .then_inc(na_act, 1)
            for z in range(2):
                e.wait_ge(na_pe, 3 + 2 * z)
                if z:
                    e.wait_ge(na_pe, 4)
                chain(e.activation(pbias[:, z:z + 1], pbank[2 + z][:, 64:65], ACT.Copy))
                e.activation(gz[:, :, 0:NC], pbank[2 + z][:, 0:2 * NC].rearrange("p (t n) -> p t n", t=2),
                             ACT.Gelu_apprx_tanh, bias=pbias[:, z:z + 1]).then_inc(na_act, 1)
            e.wait_ge(na_pe, 6)
            e.activation(kcT[:, :, 0:NC], pbank[4][:, 0:2 * NC].rearrange("p (t n) -> p t n", t=2), ACT.Copy)\
                .then_inc(na_act, 1)
            e.activation(vcr[0:NC, :, :].rearrange("p t n -> p (t n)"), pbank[5][0:NC, 0:2 * P], ACT.Copy)\
                .then_inc(na_act, 1)
            for u in range(UNITS + 1):
                if u < UNITS:
                    q, p = u % QT, u % 2
                    nk = (q + 1) * P
                    e.wait_ge(sc_dve, u + 1)
                    if u >= 2:
                        e.wait_ge(cb_dve, u - 1)
                    for b, s_ in enumerate((tmp[:, p, 0:nk], tmp[:, 2 + p, 0:nk])):
                        ins = e.activation(s_, s_, ACT.Exp, bias=negm[:, p, b:b + 1], scale=-1.0,
                                           accum_out=sums[:, p, b:b + 1])
                    ins.then_inc(sc_act, 1)
                if u < UNITS and u % QT == 2:
                    h = u // QT
                    e.wait_ge(cm_max, h + 1)
                    e.activation(cs[:, :, 0:NC], cs[:, :, 0:NC], ACT.Exp).then_inc(cm_act, 1)
                if u >= 1:
                    v = u - 1
                    nk = (v % QT + 1) * P
                    e.wait_ge(tr_pe, v + 1)
                    if v >= 2:
                        e.wait_ge(pv_pe, v - 1)
                    e.activation(tmp[:, 4 + v % 2, 0:nk], pbank[4][:, 0:nk], ACT.Copy).then_inc(tr_act, 1)
            for k in range(KT):
                e.wait_ge(na_pe, 7 + k)
                e.activation(h_hi[:, k, :], pbank[k][:, :], ACT.Copy).then_inc(na_act, 1)
            act_out(e, "nsa_out")

        def dve_nsa(e, chain):
            n0 = where["nsa_in"]
            for c in range(10):
                dve_lo(e, n0 + c + 2)
            e.wait_ge(na_act, 1)
            e.tensor_tensor(u_lo[:, 0, 0:KT * 48], gw[:, :, :].rearrange("p k n -> p (k n)"),
                            u_hi[:, 0, 0:KT * 48].bitcast(F32), ALU.subtract).then_inc(na_dve, 1)

            def masked(u):
                h, q, p = u // QT, u % QT, u % 2
                nk = (q + 1) * P
                e.wait_ge(sc_pe, u + 1)
                e.wait_ge(bias_pool, h + 1)
                if u >= 2:
                    e.wait_ge(tr_pe, u - 1)
                for b, (dst, src, bias) in enumerate((
                        (tmp[:, p, 0:nk], pbank[p][:, 0:nk], bias_h[:, h % 2, S - nk:S]),
                        (tmp[:, 2 + p, 0:nk], pbank[2 + p][:, 0:nk], bias_h[:, h % 2, S - nk:S]))):
                    ins = e.tensor_tensor_reduce(dst, src, bias, -1.0, -BIG, ALU.add, ALU.min,
                                                 negm[:, p, b:b + 1])
                ins.then_inc(sc_dve, 1)

            def take(v):
                q, p = v % QT, v % 2
                nk = (q + 1) * P
                e.wait_ge(tr_pe, v + 1)
                if v >= 2:
                    e.wait_ge(pv_pe, v - 1)
                e.tensor_copy(tmp[:, 6 + p, 0:nk], pbank[5][:, 0:nk]).then_inc(tr_dve, 1)

            def combine(v):
                h, q, p = v // QT, v % QT, v % 2
                e.wait_ge(sc_act, v + 1)
                chain(e.tensor_scalar(rr[:, p, 0:2], sums[:, p, 0:2], 1e-30, None, ALU.max))
                chain(e.reciprocal(rr[:, p, 0:2], rr[:, p, 0:2]))
                chain(e.tensor_tensor(rr[:, p, 0:2], rr[:, p, 0:2], gates[:, q, 3 * h + 1:3 * h + 3], ALU.mult))
                e.wait_ge(pv_pe, v + 1)
                dst = orow[:, q, h * HD:h * HD + HD]
                chain(e.tensor_scalar(dst, pbank[7][:, 0:HD], rr[:, p, 0:1], None, ALU.mult))
                e.scalar_tensor_tensor(dst, pbank[7][:, HD:2 * HD], rr[:, p, 1:2], dst, ALU.mult, ALU.add)\
                    .then_inc(cb_dve, 1)

            def compressed(h, part):
                cb = cb_h[:, h % 2, :].rearrange("p (t n) -> p t n", t=QT)[:, :, 0:NC]
                c = cs[:, :, 0:NC]
                if part == 0:
                    e.wait_ge(cm_pe, 3 * h + 1)
                    e.tensor_tensor(c, pbank[6][:, 0:P].rearrange("p (q n) -> p q n", q=QT)[:, :, 0:NC], cb,
                                    ALU.add).then_inc(cm_dve, 1)
                    e.wait_ge(cm_dve, 3 * h + 1)
                    chain(e.tensor_reduce(cmx, c, AX.X, ALU.max))
                    chain(e.tensor_scalar(cmx, cmx, BIG * 1e-10, None, ALU.max))
                    e.tensor_tensor(c, c, cmx.unsqueeze(2).broadcast_to([P, QT, NC]), ALU.subtract)\
                        .then_inc(cm_max, 1)
                elif part == 1:
                    e.wait_ge(cm_pe, 3 * h + 2)
                    e.tensor_copy(csT[0:NC, :], pbank[6][0:NC, :]).then_inc(cm_dve, 1)
                    chain(e.tensor_reduce(csum, c, AX.X, ALU.add))
                    chain(e.tensor_scalar(csum, csum, 1e-30, None, ALU.max))
                    chain(e.reciprocal(csum, csum))
                    chain(e.tensor_tensor(csum, csum, gates[:, :, 3 * h], ALU.mult))
                else:
                    e.wait_ge(cm_pe, 3 * h + 3)
                    chain(e.tensor_tensor(cout, pbank[6][:, 0:QT * HD].rearrange("p (q n) -> p q n", q=QT),
                                          csum.unsqueeze(2).broadcast_to([P, QT, HD]), ALU.mult))
                    e.wait_ge(cb_dve, QT * h + QT)
                    dst = orow[:, :, h * HD:h * HD + HD]
                    e.tensor_tensor(dst, dst, cout, ALU.add).then_inc(cm_dve, 1)
            for u in range(UNITS + 2):
                if u < UNITS:
                    masked(u)
                if 1 <= u <= UNITS:
                    take(u - 1)
                if u >= 2:
                    combine(u - 2)
                if u < UNITS and u % QT == 2:
                    compressed(u // QT, 0)
                if u >= 4 and u % QT == 0:
                    compressed(u // QT - 1, 1)
                if u >= 5 and u % QT == 1:
                    compressed(u // QT - 1, 2)
            for k in range(KT):
                e.wait_ge(na_act, 8 + k)
                e.tensor_tensor(h_lo[:, k, :], pbank[k][:, :], h_hi[:, k, :].bitcast(F32), ALU.subtract)\
                    .then_inc(na_dve, 1)
            dve_out(e, "nsa_out", True)

        class Steps:

            def __init__(self, name, names):
                self.sem, self.names, self.n = sem(name), names, 0
                self.index = {s: i for i, s in enumerate(names)}

            def done(self, ins, s):
                assert self.names[self.n % len(self.names)] == s, (s, self.names[self.n % len(self.names)])
                self.n += 1
                ins.then_inc(self.sem, 1)

            def wait(self, e, s, turn=0):
                e.wait_ge(self.sem, turn * len(self.names) + self.index[s] + 1)

        A_H = 4
        ev_proj, ev_dve, ev_act, ev_pe = sem("ev_proj"), sem("ev_dve"), sem("ev_act"), sem("ev_pe")
        dsc_pe, dsc_dve, dsc_act = sem("dsc_pe"), sem("dsc_dve"), sem("dsc_act")
        dtr_pe, dtr_act, dtr_dve, dpv_pe, dcb_dve = (sem("dtr_pe"), sem("dtr_act"), sem("dtr_dve"), sem("dpv_pe"),
                                                     sem("dcb_dve"))
        dbias_pool = sem("dbias_pool")
        qa, ka, va = tiles(0, 4), tiles(4 * S, 4), tiles(8 * S, QT)
        ddist, dbias = arena[:, 12 * S:13 * S], tiles(13 * S, 4)
        lamv = arena[:, 17 * S:17 * S + 4 * HD]
        o = 17 * S + 4 * HD
        lams = arena[:, o:o + 8]; o += 8
        dnegm, dsums, drr = tiles(o, 2, 2), tiles(o + 4, 2, 2), tiles(o + 8, 2, 2); o += 12
        dss = arena[:, o:o + 16]; o += 16
        DUNITS = A_H * QT

        zs = tiles(0, 14)
        o = 14 * S
        wa_up, g_up = arena[:, o:o + S], arena[:, o + S:o + 2 * S]; o += 2 * S
        cmask = arena[:, o:o + S]; o += S
        m_up, m_upd, m_low = arena[:, o:o + P], arena[:, o + P:o + 2 * P], arena[:, o + 2 * P:o + 3 * P]; o += 3 * P
        lmask = tiles(o, 6, P); o += 6 * P
        bones = arena[:, o:o + P]; o += P
        ident2 = arena[:, o:o + HD]; o += HD
        PAD = o
        X_ = tiles(o, 9); o += 9 * S
        assert o <= AR, o
        rz = nc.alloc_sbuf_tensor_at("rz", [P, 24, S], F32, offset=zone)
        MUL = ALU.mult

        def padded(j):
            return arena[:, PAD + j * (S + 8):PAD + j * (S + 8) + S + 1]

        def pool_even(e, chain):
            e.dma_start(lamv, a["diff_lam_2"].rearrange("a l d -> a (l d)").broadcast_to([P, 4 * HD]))\
                .then_inc(small_in, 16)
            chain(e.iota(ddist, pattern=[[1, S]], base=-3 * P, channel_multiplier=-1,
                         allow_small_or_imprecise_dtypes=True))
            chain(e.tensor_scalar(dbias[:, 0, :], ddist, 0.0, 2.0, ALU.min, MUL))
            chain(e.tensor_tensor(ddist, dbias[:, 0, :], ddist, ALU.subtract))
            chain(e.memset(ddist[0:RCH, S - RCH:S], BIG))
            for h in range(A_H):
                e.tensor_scalar(dbias[:, h, :], ddist, 2.0 ** (-8.0 / A_H * (h + 1)), None, MUL)\
                    .then_inc(dbias_pool, 1)
            e.wait_ge(ev_dve, 2)
            e.wait_ge(ev_proj, 20)
            e.dma_start(wa_up[0:HD, :], a["rwkv_w_up_2"][0]).then_inc(small_in, 16)
            e.dma_start(wa_up[HD:P, :], a["rwkv_a_up_2"][0]).then_inc(small_in, 16)
            e.dma_start(g_up, a["rwkv_g_up_2"][0]).then_inc(small_in, 16)
            for j in range(2):
                chain(e.memset(padded(j)[:, 0:1], 0.0))
            chain(e.memset(cmask, 1.0))
            chain(e.memset(cmask.rearrange("p (c t) -> p c t", t=RCH)[:, :, 0:1], 0.0))

            def block_ones(m, b):
                v = m.rearrange("p (c f) -> p c f", f=b)
                chain(e.memset(m, 1.0))
                chain(e.affine_select(out=v, in_=v, compare_op=ALU.is_ge, fill=0.0, base=0,
                                      pattern=[[-b, P // b], [0, b]], channel_multiplier=1))
                chain(e.affine_select(out=v, in_=v, compare_op=ALU.is_ge, fill=0.0, base=b - 1,
                                      pattern=[[b, P // b], [0, b]], channel_multiplier=-1))
            block_ones(bones, RCH)
            for j in range(6):
                block_ones(lmask[:, j, :], 2 << j)
            for j in range(5, 0, -1):
                chain(e.tensor_tensor(lmask[:, j, :], lmask[:, j, :], lmask[:, j - 1, :], ALU.subtract))
            chain(e.tensor_tensor(lmask[:, 0, :], lmask[:, 0, :], ident[:, :], ALU.subtract))
            chain(e.affine_select(out=m_up, in_=bones, compare_op=ALU.is_gt, fill=0.0, base=0, pattern=[[1, P]],
                                  channel_multiplier=-1))
            chain(e.affine_select(out=m_upd, in_=bones, compare_op=ALU.is_ge, fill=0.0, base=0, pattern=[[1, P]],
                                  channel_multiplier=-1))
            chain(e.affine_select(out=m_low, in_=bones, compare_op=ALU.is_gt, fill=0.0, base=0, pattern=[[-1, P]],
                                  channel_multiplier=1))
            for j in range(2):
                chain(e.tensor_copy(ident2[j * HD:j * HD + HD, :], ident[j * HD:j * HD + HD, j * HD:j * HD + HD]))
            e.tensor_copy(ident2[:, 0:1], ident2[:, 0:1]).then_inc(dbias_pool, 1)
            rwkv_pool(e)

        EV_SMALL = (SMALL_NSA if any(s[0] == "nsa" for s in PLAN) else 0)

        def pe_even(pe):
            n0 = where["even_a"]
            t = 0
            for c in range(6):
                def free(m):
                    if t + m >= 8:
                        pe.wait_ge(ev_proj, t + m - 7)
                if c < 4:
                    pe_chunk(pe, n0 + c, KT, 2, h_hi, h_lo, lambda m: pbank[(t + m) % 8][:, :], free)
                    t += 2
                else:
                    pe_rows(pe, n0 + c, lambda m: pbank[(t + m) % 8][:, 0:256], free)
                    t += 4
            pe.wait_ge(ev_proj, 16)

            def scores(u):
                h, q = u // QT, u % QT
                nk = (q + 1) * P
                if u >= 2:
                    pe.wait_ge(dsc_dve, u - 1)
                for m in range(2):
                    r = slice(m * HD, m * HD + HD)
                    ins = pe.matmul(pbank[2 * m + u % 2][:, 0:nk], qa[r, h, q * P:q * P + P], ka[r, h, 0:nk],
                                    start=True, stop=True)
                ins.then_inc(dsc_pe, 1)

            def turn(u):
                q, p = u % QT, u % 2
                pe.wait_ge(dsc_act, u + 1)
                if u >= 1:
                    pe.wait_ge(dtr_act, u)
                    pe.wait_ge(dtr_dve, u)
                for b in range(2):
                    for k in range(q + 1):
                        kk = slice(k * P, k * P + P)
                        ins = pe.transpose(pbank[4 + b][:, kk], tmp[:, 2 * b + p, kk], ident[:, :])
                ins.then_inc(dtr_pe, 1)

            def values(u):
                h, q, p = u // QT, u % QT, u % 2
                pe.wait_ge(dtr_act, u + 1)
                pe.wait_ge(dtr_dve, u + 1)
                if u >= 1:
                    pe.wait_ge(dcb_dve, u)
                for b in range(2):
                    for k in range(q + 1):
                        ins = pe.matmul(pbank[7][:, b * P:b * P + P], tmp[:, 4 + 2 * b + p, k * P:k * P + P],
                                        va[:, k, h * P:h * P + P], start=k == 0, stop=k == q)
                ins.then_inc(dpv_pe, 1)
            for u in range(DUNITS + 2):
                if u < DUNITS:
                    scores(u)
                if 1 <= u <= DUNITS:
                    turn(u - 1)
                if u >= 2:
                    values(u - 2)
            pe.wait_ge(ev_dve, 1)
            for h in range(A_H):
                for q in range(QT):
                    ins = pe.transpose(pbank[h][:, q * P:q * P + P], xrows[:, q, h * P:h * P + P], ident[:, :])
                ins.then_inc(ev_pe, 1)
            n1 = where["even_b"]
            for c in range(7):
                def free(m):
                    t = 2 * c + m
                    if t < 4:
                        pe.wait_ge(ev_proj, 17 + t)
                    if t >= 8:
                        pe.wait_ge(ev_proj, 20 + t - 7)
                pe_chunk(pe, n1 + c, KT, 2, h_hi, h_lo, lambda m: pbank[(2 * c + m) % 8][:, :], free)
            pe.wait_ge(small_in, EV_SMALL + 64)
            pe.wait_ge(dbias_pool, 5)
            pe.wait_ge(ev_proj, 34)
            rwkv_pe(pe)
            pe.wait_ge(ev_dve, 2 + 14 + KT)
            pe_out(pe, "even_out")

        def act_even(e, chain):
            n0 = where["even_a"]
            dst = [qa[:, j, :] for j in range(4)] + [ka[:, j, :] for j in range(4)] + \
                [va[:, j, 0:256] for j in range(4)] + [va[:, j, 256:512] for j in range(4)]
            t = 0
            for c in range(6):
                for m in range(2 if c < 4 else 4):
                    e.wait_ge(tiles_out, before[n0 + c] + m + 1)
                    e.activation(dst[t], pbank[t % 8][:, 0:256 if c >= 4 else S], ACT.Copy,
                                 scale=HD ** -0.5 if t < 4 else 1.0).then_inc(ev_proj, 1)
                    t += 1
                act_hi(e, n0 + c + 2)
            e.wait_ge(dve_even_l.sem, dve_even_l.index["dots"] + 1)
            e.activation(lams[:, 2:4], lams[:, 0:2], ACT.Exp).then_inc(ev_act, 1)
            for u in range(DUNITS + 1):
                if u < DUNITS:
                    q, p = u % QT, u % 2
                    nk = (q + 1) * P
                    e.wait_ge(dsc_dve, u + 1)
                    if u >= 2:
                        e.wait_ge(dcb_dve, u - 1)
                    for b in range(2):
                        s_ = tmp[:, 2 * b + p, 0:nk]
                        ins = e.activation(s_, s_, ACT.Exp, bias=dnegm[:, p, b:b + 1], scale=-1.0,
                                           accum_out=dsums[:, p, b:b + 1])
                    ins.then_inc(dsc_act, 1)
                if u >= 1:
                    v = u - 1
                    nk = (v % QT + 1) * P
                    e.wait_ge(dtr_pe, v + 1)
                    if v >= 2:
                        e.wait_ge(dpv_pe, v - 1)
                    e.activation(tmp[:, 4 + v % 2, 0:nk], pbank[4][:, 0:nk], ACT.Copy).then_inc(dtr_act, 1)
            e.wait_ge(dcb_dve, DUNITS)
            e.activation(dss, dss, ACT.Sqrt, bias=eps[:, 0:1], scale=1.0 / P).then_inc(ev_act, 1)
            for h in range(A_H):
                e.wait_ge(ev_pe, h + 1)
                e.activation(fsum[:, 2 * h + 1, :], pbank[h][:, :], ACT.Copy, scale=lams[:, 6:7]).then_inc(ev_proj, 1)
            n1 = where["even_b"]
            for c in range(7):
                for m in range(2):
                    t = 2 * c + m
                    e.wait_ge(tiles_out, before[n1 + c] + m + 1)
                    if t < 2:
                        e.wait_ge(dbias_pool, 5)
                    else:
                        e.wait_ge(ev_dve, 2 + t - 1)
                    e.activation(padded(t % 2)[:, 1:S + 1], pbank[t % 8][:, :], ACT.Copy).then_inc(ev_proj, 1)
                act_hi(e, n1 + c + 2)
            e.wait_ge(ev_dve, 2 + 14)
            e.activation(zs[0:HD, 12, :], zs[0:HD, 12, :], ACT.Tanh)
            e.activation(zs[:, 13, :], zs[:, 13, :], ACT.Sigmoid).then_inc(ev_act, 1)
            rwkv_act(e)
            w_dve.wait(e, "out", 3)
            for k in range(KT):
                src = fsum[:, 2 * k + 1, :] if k < 4 else zs[:, k - 4, :]
                e.activation(h_hi[:, k, :], src, ACT.Copy).then_inc(ev_act, 1)
            act_out(e, "even_out")

        dve_even_l = Steps("lam_dots", ["dots", "lam"])

        def dve_even(e, chain):
            n0 = where["even_a"]
            e.wait_ge(small_in, EV_SMALL + 16)
            for j in range(2):
                ins = e.tensor_tensor_reduce(lamv[:, 2 * j * HD:2 * j * HD + HD], lamv[:, 2 * j * HD:2 * j * HD + HD],
                                             lamv[:, (2 * j + 1) * HD:(2 * j + 2) * HD], 1.0, 0.0, ALU.mult, ALU.add,
                                             lams[:, j:j + 1])
            dve_even_l.done(ins, "dots")
            for c in range(6):
                dve_lo(e, n0 + c + 2)
            e.wait_ge(ev_act, 1)
            chain(e.tensor_tensor(lams[:, 4:5], lams[:, 3:4], lams[:, 2:3], ALU.subtract))
            chain(e.tensor_scalar(lams[:, 5:6], lams[:, 4:5], -(0.8 - 0.6), None, ALU.add))
            dve_even_l.done(e.tensor_scalar(lams[:, 6:7], gain(1, PSUB), 1.0 - (0.8 - 0.6), None, ALU.mult), "lam")

            def masked(u):
                h, q, p = u // QT, u % QT, u % 2
                nk = (q + 1) * P
                e.wait_ge(dsc_pe, u + 1)
                e.wait_ge(dbias_pool, h + 1)
                if u >= 2:
                    e.wait_ge(dtr_pe, u - 1)
                for b in range(2):
                    ins = e.tensor_tensor_reduce(tmp[:, 2 * b + p, 0:nk], pbank[2 * b + p][:, 0:nk],
                                                 dbias[:, h, S - nk:S], -1.0, -BIG, ALU.add, ALU.min,
                                                 dnegm[:, p, b:b + 1])
                ins.then_inc(dsc_dve, 1)

            def take(v):
                q, p = v % QT, v % 2
                nk = (q + 1) * P
                e.wait_ge(dtr_pe, v + 1)
                if v >= 2:
                    e.wait_ge(dpv_pe, v - 1)
                e.tensor_copy(tmp[:, 6 + p, 0:nk], pbank[5][:, 0:nk]).then_inc(dtr_dve, 1)

            def combine(v):
                h, q, p = v // QT, v % QT, v % 2
                e.wait_ge(dsc_act, v + 1)
                chain(e.reciprocal(drr[:, p, :], dsums[:, p, :]))
                chain(e.tensor_tensor(drr[:, p, 1:2], drr[:, p, 1:2], lams[:, 5:6], ALU.mult))
                e.wait_ge(dpv_pe, v + 1)
                dst = xrows[:, q, h * P:h * P + P]
                chain(e.tensor_scalar(dst, pbank[7][:, 0:P], drr[:, p, 0:1], None, ALU.mult))
                chain(e.scalar_tensor_tensor(dst, pbank[7][:, P:2 * P], drr[:, p, 1:2], dst, ALU.mult, ALU.add))
                chain(e.tensor_tensor(xrows[:, q, 512 + h * P:512 + h * P + P], dst, dst, ALU.mult))
                e.tensor_reduce(dss[:, v:v + 1], xrows[:, q, 512 + h * P:512 + h * P + P], AX.X, ALU.add)\
                    .then_inc(dcb_dve, 1)
            for u in range(DUNITS + 2):
                if u < DUNITS:
                    masked(u)
                if 1 <= u <= DUNITS:
                    take(u - 1)
                if u >= 2:
                    combine(u - 2)
            e.wait_ge(ev_act, 2)
            chain(e.reciprocal(dss, dss))
            for v in range(DUNITS):
                dst = xrows[:, v % QT, (v // QT) * P:(v // QT) * P + P]
                ins = e.tensor_scalar(dst, dst, dss[:, v:v + 1], None, ALU.mult)
            ins.then_inc(ev_dve, 1)
            e.wait_ge(ev_pe, A_H)
            e.drain().then_inc(ev_dve, 1)
            n1 = where["even_b"]
            for t in range(14):
                z = padded(t % 2)
                e.wait_ge(ev_proj, 21 + t)
                chain(e.tensor_tensor(tmp[:, t % 2, :], z[:, 0:S], z[:, 1:S + 1], ALU.subtract))
                e.scalar_tensor_tensor(zs[:, t, :], tmp[:, t % 2, :], gain(1, PMU + t), z[:, 1:S + 1],
                                       ALU.mult, ALU.add).then_inc(ev_dve, 1)
                if t % 2:
                    dve_lo(e, n1 + t // 2 + 2)
            rwkv_dve(e)
            for k in range(KT):
                src = fsum[:, 2 * k + 1, :] if k < 4 else zs[:, k - 4, :]
                e.wait_ge(ev_act, 3 + k + 1)
                e.tensor_tensor(h_lo[:, k, :], src, h_hi[:, k, :].bitcast(F32), ALU.subtract).then_inc(ev_dve, 1)
            dve_out(e, "even_out", False)

        LEV = range(1, 6)
        HH = range(2)
        w_pe = Steps("w_pe", ["w", "a", "g", "kk", "bonus", "t_al", "t_bh", "t_kh", "t_v"]
                     + [f"m{i}{h}" for h in HH for i in range(5)]
                     + ["rhs0", "rhs1"]
                     + [f"{x_}{l}{h}" for l in LEV for x_, hs in ((("U"), HH), (("D"), HH)) for h in hs]
                     + ["P0", "P1", "QT", "Y1", "MT", "N"] + [f"s{c}" for c in range(1, 8)] + ["mean", "var"])
        w_act = Steps("w_act", ["sw", "aa", "sq", "kkrt", "ec", "enc", "ecp", "gg", "tokB", "tokK", "rhs0", "rhs1"]
                      + [f"U{l}{h}" for l in LEV for h in HH] + ["P0", "Y1", "N", "ysq", "yrt"])
        w_dve = Steps("w_dve", ["kk0", "lw", "c", "cp", "ka", "kp", "max", "rec", "kk", "al", "ka2", "be", "kt", "rt",
                                "bh", "kh", "rkr", "tokA", "tokV"]
                      + [f"m{i}{h}" for h in HH for i in range(5)] + ["bon"]
                      + [f"D{l}{h}" for l in LEV for h in HH]
                      + ["P1", "QT", "MT", "s0"] + [f"s{c}" for c in range(1, 7)]
                      + ["y", "yc", "yrec", "yn", "yb", "yg", "out"])
        w_pool = Steps("w_pool", ["D0", "D1"] + [f"gb{l}{h}" for l in LEV for h in HH] + ["rhs0", "rhs1"])
        wlw, wc, wcp, waa, wkk, wsq, wrt, wkp = (tmp[:, j, :] for j in range(8))
        ec, enc, ecp, al, be, kt_, rt, bh, kh = (X_[:, j, :] for j in range(9))
        gg = enc
        tokA, tokB, tokK, tokV = (fsum[:, 2 * j, :].rearrange("p (j n) -> p j n", j=QT) for j in range(4))
        NN, YY, ST, bon, yc, ysq, yrs = wlw, wc, wcp, waa, wkk, wsq, wrt

        def hz(h, j):
            return rz[:, 11 * h + j, :].rearrange("p (j n) -> p j n", j=QT)
        MATS = [[hz(h, j) for j in range(5)] for h in HH]
        Dm, DTm, Um, Gb, RHS, PM = ([hz(h, j) for h in HH] for j in range(5, 11))
        QTt, MTt = rz[:, 22, :], rz[:, 23, :]

        def wide(m):
            return m.unsqueeze(1).broadcast_to([P, QT, P])

        def rwkv_pe(pe):
            for p in range(4):
                cp_ = slice(p * P, p * P + P)
                if p:
                    w_dve.wait(pe, "out", p - 1)
                else:
                    pe.wait_ge(ev_act, 3)
                w_pe.done(pe.matmul(pbank[0][:, :], wa_up[0:HD, cp_], zs[0:HD, 12, :], start=True, stop=True), "w")
                w_pe.done(pe.matmul(pbank[1][:, :], wa_up[HD:P, cp_], zs[HD:P, 12, :], start=True, stop=True), "a")
                w_pe.done(pe.matmul(pbank[2][:, :], g_up[:, cp_], zs[:, 13, :], start=True, stop=True), "g")
                w_act.wait(pe, "sq", p)
                w_pe.done(pe.matmul(pbank[3][:, :], bones, wsq, start=True, stop=True), "kk")
                w_dve.wait(pe, "rkr", p)
                w_pe.done(pe.matmul(pbank[4][:, :], bones, wsq, start=True, stop=True), "bonus")
                w_act.wait(pe, "gg", p)
                for name, src, b in (("t_al", al, 5), ("t_bh", bh, 6), ("t_kh", kh, 7), ("t_v", zs[:, 8 + p, :], 0)):
                    for j in range(QT):
                        ins = pe.transpose(pbank[b][:, j * P:j * P + P], src[:, j * P:j * P + P], ident[:, :])
                    w_pe.done(ins, name)
                w_act.wait(pe, "kkrt", p)
                k = 0
                for h in HH:
                    r = slice(h * HD, h * HD + HD)
                    for i, (l_, r_) in enumerate(((be, al), (be, rt), (kt_, al), (kt_, rt), (al, be))):
                        b = (1, 2, 3, 0, 5, 6, 7, 1, 2, 3)[k]
                        if b in (0, 5):
                            w_dve.wait(pe, "tokV", p)
                        if b in (6, 7):
                            w_act.wait(pe, "tokK", p)
                        if k >= 7:
                            w_dve.wait(pe, f"m{(k - 7) % 5}{(k - 7) // 5}", p)
                        for j in range(QT):
                            q = slice(j * P, j * P + P)
                            ins = pe.matmul(pbank[b][:, q], l_[r, q], r_[r, q], start=True, stop=True)
                        w_pe.done(ins, f"m{i}{h}")
                        k += 1
                w_dve.wait(pe, "bon", p)
                for h in HH:
                    for j in range(QT):
                        ins = pe.matmul(pbank[6 + h][:, j * HD:j * HD + HD], MATS[h][2][:, j, :],
                                        tokV[:, j, h * HD:h * HD + HD], start=True, stop=True)
                    w_pe.done(ins, f"rhs{h}")
                for l in LEV:
                    for h in HH:
                        w_pool.wait(pe, f"gb{l}{h}", p)
                        if l > 1:
                            w_dve.wait(pe, f"D{l - 1}{h}", p)
                        for j in range(QT):
                            ins = pe.matmul(pbank[h][:, j * P:j * P + P], Gb[h][:, j, :], Dm[h][:, j, :], start=True,
                                            stop=True)
                        w_pe.done(ins, f"U{l}{h}")
                    for h in HH:
                        w_act.wait(pe, f"U{l}{h}", p)
                        for j in range(QT):
                            q = slice(j * P, j * P + P)
                            if l < 5:
                                pe.matmul(pbank[2 + h][:, q], DTm[h][:, j, :], Um[h][:, j, :], start=True, stop=True)
                            ins = pe.matmul(pbank[4 + h][:, q], Um[h][:, j, :], DTm[h][:, j, :], start=True, stop=True)
                        w_pe.done(ins, f"D{l}{h}")
                for h in HH:
                    w_dve.wait(pe, f"D5{h}", p)
                    w_act.wait(pe, f"rhs{h}", p)
                    w_pool.wait(pe, f"rhs{h}", p)
                    for j in range(QT):
                        ins = pe.matmul(pbank[h][:, j * P:j * P + P], DTm[h][:, j, :], RHS[h][:, j, :], start=True,
                                        stop=True)
                    w_pe.done(ins, f"P{h}")
                w_act.wait(pe, "P0", p)
                w_dve.wait(pe, "P1", p)
                for h in HH:
                    for j in range(QT):
                        ins = pe.matmul(pbank[2][h * HD:h * HD + HD, j * P:j * P + P], PM[h][:, j, HD:P],
                                        MATS[h][1][:, j, :], start=True, stop=True)
                w_pe.done(ins, "QT")
                for h in HH:
                    for j in range(QT):
                        o_ = pbank[3][h * HD:h * HD + HD, j * P:j * P + P]
                        pe.matmul(o_, tokV[:, j, h * HD:h * HD + HD], MATS[h][3][:, j, :], start=True, stop=False)
                        ins = pe.matmul(o_, PM[h][:, j, 0:HD], MATS[h][1][:, j, :], start=False, stop=True)
                w_pe.done(ins, "Y1")
                for c in range(8):
                    rr_ = slice((c % 2) * HD, (c % 2) * HD + HD)
                    for h in HH:
                        r = slice(h * HD, h * HD + HD)
                        ins = pe.matmul(pbank[(4, 1)[c % 2]][r, c * HD:c * HD + HD], PM[h][rr_, c // 2, HD:P], tokB[rr_, c // 2, r],
                                        start=True, stop=True)
                w_pe.done(ins, "MT")
                for c in range(8):
                    rr_ = slice((c % 2) * HD, (c % 2) * HD + HD)
                    for h in HH:
                        r = slice(h * HD, h * HD + HD)
                        o_ = pbank[(5, 7)[c % 2]][r, c * HD:c * HD + HD]
                        pe.matmul(o_, tokB[rr_, c // 2, r], PM[h][rr_, c // 2, 0:HD], start=True, stop=False)
                        ins = pe.matmul(o_, tokK[rr_, c // 2, r], tokV[rr_, c // 2, r], start=False, stop=True)
                w_pe.done(ins, "N")
                w_dve.wait(pe, "MT", p)
                for c in range(1, 8):
                    w_dve.wait(pe, f"s{c - 1}", p)
                    st = ST[:, ((c - 1) % 2) * HD:((c - 1) % 2) * HD + HD]
                    for h in HH:
                        r = slice(h * HD, h * HD + HD)
                        q = slice(c * HD, c * HD + HD)
                        if c < 7:
                            pe.matmul(pbank[7][r, 0:HD], MTt[r, q], st[r, :], start=True, stop=True)
                        ins = pe.matmul(pbank[6][r, q], st[r, :], QTt[r, q], start=True, stop=True)
                    w_pe.done(ins, f"s{c}")
                w_dve.wait(pe, "y", p)
                w_pe.done(pe.matmul(pbank[0][:, :], bones, YY, start=True, stop=True), "mean")
                w_act.wait(pe, "ysq", p)
                w_pe.done(pe.matmul(pbank[1][:, :], bones, ysq, start=True, stop=True), "var")

        def rwkv_act(e):
            for p in range(4):
                def par_(j):
                    return gain(2, PVEC + 4 * j + p)
                if p:
                    w_dve.wait(e, "out", p - 1)
                w_pe.wait(e, "w", p)
                w_act.done(e.activation(wlw, pbank[0][:, :], ACT.Sigmoid, bias=par_(0)), "sw")
                w_pe.wait(e, "a", p)
                w_act.done(e.activation(waa, pbank[1][:, :], ACT.Sigmoid, bias=par_(1)), "aa")
                w_dve.wait(e, "kk0", p)
                w_act.done(e.activation(wsq, wkk, ACT.Square), "sq")
                w_pe.wait(e, "kk", p)
                w_act.done(e.activation(wrt, pbank[3][:, :], ACT.Sqrt), "kkrt")
                w_dve.wait(e, "cp", p)
                w_act.done(e.activation(ec, wc, ACT.Exp), "ec")
                w_act.done(e.activation(enc, wc, ACT.Exp, scale=-1.0), "enc")
                w_act.done(e.activation(ecp, wcp, ACT.Exp), "ecp")
                w_pe.wait(e, "g", p)
                w_dve.wait(e, "kt", p)
                w_act.done(e.activation(gg, pbank[2][:, :], ACT.Copy), "gg")
                for name, dst, b in (("tokB", tokB, 6), ("tokK", tokK, 7)):
                    w_pe.wait(e, {"tokB": "t_bh", "tokK": "t_kh"}[name], p)
                    w_act.done(e.activation(dst.rearrange("p j n -> p (j n)"), pbank[b][:, :], ACT.Copy), name)
                for h in HH:
                    w_pe.wait(e, f"rhs{h}", p)
                    w_act.done(e.activation(RHS[h][:, :, 0:HD], pbank[6 + h][:, 0:4 * HD].rearrange(
                        "p (j n) -> p j n", j=QT), ACT.Copy), f"rhs{h}")
                for l in LEV:
                    for h in HH:
                        w_pe.wait(e, f"U{l}{h}", p)
                        w_act.done(e.activation(Um[h].rearrange("p j n -> p (j n)"), pbank[h][:, :], ACT.Copy),
                                   f"U{l}{h}")
                w_pe.wait(e, "P0", p)
                w_act.done(e.activation(PM[0].rearrange("p j n -> p (j n)"), pbank[0][:, :], ACT.Copy), "P0")
                w_pe.wait(e, "Y1", p)
                w_act.done(e.activation(YY, pbank[3][:, :], ACT.Copy), "Y1")
                w_pe.wait(e, "N", p)
                for j in range(2):
                    ins = e.activation(*(m.rearrange("p (c j n) -> p j c n", j=2, n=HD)[:, j]
                                         for m in (NN, pbank[(5, 7)[j]][:, :])), ACT.Copy)
                w_act.done(ins, "N")
                w_dve.wait(e, "yc", p)
                w_act.done(e.activation(ysq, yc, ACT.Square), "ysq")
                w_pe.wait(e, "var", p)
                w_act.done(e.activation(yrs, pbank[1][:, :], ACT.Sqrt, bias=eps[:, 1:2], scale=1.0 / HD), "yrt")

        def rwkv_pool(e):
            for p in range(4):
                for h in HH:
                    w_dve.wait(e, f"m4{h}", p)
                    for src, dst in ((MATS[h][4], Dm[h]), (MATS[h][0], DTm[h])):
                        e.tensor_tensor(dst, src, wide(lmask[:, 0, :]), ALU.mult).then_inc(rw_own, 1)
                    e.wait_ge(rw_own, 4 * (2 * p + h) + 2)
                    for dst in (Dm[h], DTm[h]):
                        ins = e.tensor_tensor(dst, dst, wide(ident[:, :]), ALU.add)
                        ins.then_inc(rw_own, 1) if dst is Dm[h] else w_pool.done(ins, f"D{h}")
                    e.wait_ge(rw_own, 4 * (2 * p + h) + 3)
                    e.drain().then_inc(rw_own, 1)
                for l in LEV:
                    for h in HH:
                        if l > 1:
                            w_pe.wait(e, f"U{l - 1}{h}", p)
                        w_pool.done(e.tensor_tensor(Gb[h], MATS[h][0], wide(lmask[:, l, :]), ALU.mult), f"gb{l}{h}")
                for h in HH:
                    w_dve.wait(e, "tokA", p)
                    w_pool.done(e.tensor_copy(RHS[h][:, :, HD:P], tokA[:, :, h * HD:h * HD + HD]), f"rhs{h}")

        rw_own = sem("rw_own")

        def rwkv_dve(e):
            def do(ins, name, chain=True):
                w_dve.done(ins, name)
                if chain:
                    e.wait_ge(w_dve.sem, w_dve.n)
            for p in range(4):
                def par_(j):
                    return gain(2, PVEC + 4 * j + p)
                zr, zk, zv = zs[:, p, :], zs[:, 4 + p, :], zs[:, 8 + p, :]
                do(e.tensor_scalar(wkk, zk, par_(2), None, MUL), "kk0")
                w_act.wait(e, "sw", p)
                do(e.tensor_scalar(wlw, wlw, -math.exp(-0.5), None, MUL), "lw")
                do(e.tensor_tensor_scan(wc, cmask, wlw, 0.0, MUL, ALU.add), "c")
                do(e.tensor_tensor(wcp, wc, wlw, ALU.subtract), "cp", False)
                w_act.wait(e, "aa", p)
                do(e.tensor_scalar(wkp, waa, 1.0, par_(3), ALU.subtract, MUL), "ka")
                do(e.scalar_tensor_tensor(wkp, wkp, 1.0, zk, ALU.add, MUL), "kp", False)
                w_act.wait(e, "kkrt", p)
                do(e.tensor_scalar(wrt, wrt, 1e-12, None, ALU.max), "max")
                do(e.reciprocal(wrt, wrt), "rec")
                do(e.tensor_tensor(wkk, wkk, wrt, MUL), "kk")
                w_act.wait(e, "ecp", p)
                do(e.scalar_tensor_tensor(al, wkk, -1.0, ecp, MUL, MUL), "al", False)
                do(e.tensor_tensor(wrt, wkk, waa, MUL), "ka2")
                do(e.tensor_tensor(be, wrt, enc, MUL), "be", False)
                do(e.tensor_tensor(kt_, wkp, enc, MUL), "kt")
                do(e.tensor_tensor(rt, zr, ec, MUL), "rt")
                last = ec.rearrange("p (c t) -> p c t", t=RCH)[:, :, RCH - 1:RCH].broadcast_to([P, 8, RCH])
                for name, dst, src in (("bh", bh, be), ("kh", kh, kt_)):
                    do(e.tensor_tensor(dst.rearrange("p (c t) -> p c t", t=RCH),
                                       src.rearrange("p (c t) -> p c t", t=RCH), last, MUL), name, False)
                w_pe.wait(e, "kk", p)
                do(e.scalar_tensor_tensor(wsq, zr, par_(4), wkp, MUL, MUL), "rkr")
                for name, src, dst, b in (("tokA", "t_al", tokA, 5), ("tokV", "t_v", tokV, 0)):
                    w_pe.wait(e, src, p)
                    do(e.tensor_copy(dst.rearrange("p j n -> p (j n)"), pbank[b][:, :]), name, False)
                k = 0
                for h in HH:
                    for i in range(5):
                        b = (1, 2, 3, 0, 5, 6, 7, 1, 2, 3)[k]
                        m = (m_up, m_upd, m_up, m_upd, m_low)[i]
                        w_pe.wait(e, f"m{i}{h}", p)
                        do(e.tensor_tensor(MATS[h][i], pbank[b][:, :].rearrange("p (j n) -> p j n", j=QT), wide(m), MUL),
                           f"m{i}{h}", False)
                        k += 1
                do(e.tensor_tensor(bon, pbank[4][:, :], zv, MUL), "bon")
                for l in LEV:
                    for h in HH:
                        w_pool.wait(e, f"D{h}", p)
                        e.wait_ge(rw_own, 4 * (2 * p + h) + 4)
                        w_pe.wait(e, f"D{l}{h}", p)
                        if l < 5:
                            dfl = Dm[h].rearrange("p j n -> p (j n)")
                            e.tensor_tensor(dfl, dfl, pbank[2 + h][:, :], ALU.add)
                        dfl = DTm[h].rearrange("p j n -> p (j n)")
                        do(e.tensor_tensor(dfl, dfl, pbank[4 + h][:, :], ALU.add), f"D{l}{h}", False)
                w_pe.wait(e, "P1", p)
                do(e.tensor_copy(PM[1].rearrange("p j n -> p (j n)"), pbank[1][:, :]), "P1", False)
                w_pe.wait(e, "QT", p)
                do(e.tensor_tensor(QTt, pbank[2][:, :], rt, ALU.add), "QT", False)
                w_pe.wait(e, "MT", p)
                for c in range(8):
                    q = slice(c * HD, c * HD + HD)
                    ins = e.scalar_tensor_tensor(MTt[:, q], ident2, ec[:, c * HD + HD - 1:c * HD + HD],
                                                 pbank[(4, 1)[c % 2]][:, q],
                                                 MUL, ALU.add)
                do(ins, "MT", False)
                w_act.wait(e, "N", p)
                do(e.tensor_copy(ST[:, 0:HD], NN[:, 0:HD]), "s0", False)
                for c in range(1, 7):
                    w_pe.wait(e, f"s{c}", p)
                    o_ = ST[:, (c % 2) * HD:(c % 2) * HD + HD]
                    do(e.tensor_tensor(o_, pbank[7][:, 0:HD], NN[:, c * HD:c * HD + HD], ALU.add), f"s{c}", False)
                w_pe.wait(e, "s7", p)
                do(e.tensor_tensor(YY[:, HD:S], YY[:, HD:S], pbank[6][:, HD:S], ALU.add), "y")
                w_pe.wait(e, "mean", p)
                do(e.scalar_tensor_tensor(yc, pbank[0][:, :], -1.0 / HD, YY, MUL, ALU.add), "yc", False)
                w_act.wait(e, "yrt", p)
                do(e.reciprocal(yrs, yrs), "yrec")
                do(e.scalar_tensor_tensor(yc, yc, par_(5), yrs, MUL, MUL), "yn")
                do(e.scalar_tensor_tensor(yc, yc, par_(6), bon, ALU.add, ALU.add), "yb")
                do(e.tensor_tensor(yc, yc, gg, MUL), "yg")
                do(e.tensor_copy(zr, yc), "out")

        C_H = 4
        od_proj, od_dve, od_pe, od_act, od_pool = (sem("od_proj"), sem("od_dve"), sem("od_pe"), sem("od_act"),
                                                   sem("od_pool"))
        rdist = arena[:, 0:S]
        rdec = tiles(S, 4)
        rq, rk = tiles(5 * S, 2), tiles(7 * S, 2)
        rv = tiles(9 * S, QT)
        rg = tiles(13 * S, 4)
        rp = tmp
        ry = tiles(17 * S, 4)
        rsq = tiles(21 * S, 4)
        rrt = arena[:, 25 * S:26 * S]
        ryn = tiles(26 * S, 3)

        def pool_odd(e, chain):
            chain(e.iota(rdist, pattern=[[1, S]], base=0, channel_multiplier=-1,
                         allow_small_or_imprecise_dtypes=True))
            chain(e.tensor_scalar(rk[:, 0, :], rdist, 0.0, 2.0, ALU.min, MUL))
            chain(e.tensor_tensor(rdist, rk[:, 0, :], rdist, ALU.subtract))
            e.tensor_copy(rdist[:, 0:1], rdist[:, 0:1]).then_inc(od_pool, 1)
            e.wait_ge(od_act, C_H)
            for h in range(C_H):
                ins = e.memset(rdec[RCH:P, h, 0:RCH], 0.0)
            ins.then_inc(od_pool, 1)

        def pe_odd(pe):
            for h in range(C_H):
                n0 = where[f"odd{h}"]
                b0 = 16 * h

                def bank(t):
                    return pbank[t % 8]

                def free(t):
                    if t >= 8:
                        pe.wait_ge(od_proj, b0 + t - 7)
                    elif h:
                        pe.wait_ge(od_dve, 20 * h)
                for c in range(2):
                    pe_chunk(pe, n0 + c, KT, 2, h_hi, h_lo, lambda m: bank(2 * c + m)[:, :], lambda m: free(2 * c + m))
                for c in range(2):
                    pe_rows(pe, n0 + 2 + c, lambda m: bank(4 + 4 * c + m)[:, 0:256], lambda m: free(4 + 4 * c + m))
                for c in range(2):
                    pe_chunk(pe, n0 + 4 + c, KT, 2, h_hi, h_lo, lambda m: bank(12 + 2 * c + m)[:, :],
                             lambda m: free(12 + 2 * c + m))
                pe.wait_ge(od_proj, b0 + 16)
                for k in range(QT):
                    for j in range(2):
                        ins = pe.matmul(pbank[k][:, 0:S - k * P], rk[:, j, k * P:k * P + P], rq[:, j, k * P:S],
                                        start=j == 0, stop=j == 1)
                    ins.then_inc(od_pe, 1)
                for t in range(4):
                    for k in range(QT):
                        if t == 0:
                            pe.wait_ge(od_dve, 20 * h + k + 1)
                        ins = pe.matmul(pbank[4 + t][:, k * P:S], rv[:, k, t * P:t * P + P], rp[:, k, 0:S - k * P],
                                        start=k == 0, stop=k == QT - 1, skip_group_check=True)
                    ins.then_inc(od_pe, 1)
                for t in range(4):
                    pe.wait_ge(od_act, C_H + 10 * h + t + 1)
                    ins = pe.matmul(pbank[0][:, :], ones[:, :], rsq[:, t, :], start=t == 0, stop=t == 3)
                ins.then_inc(od_pe, 1)
                pe.wait_ge(od_dve, 20 * h + 12)
                for c in range(2):
                    pe_chunk(pe, n0 + 6 + c, 4, 4, u_hi, u_lo, lambda m: pbank[4 * c + m][:, :])

        def act_odd(e, chain):
            e.wait_ge(od_pool, 1)
            for h in range(C_H):
                e.activation(rdec[:, h, :], rdist, ACT.Exp, scale=-math.log(1.0 - 2.0 ** (-5.0 - h))).then_inc(od_act, 1)
            for h in range(C_H):
                n0 = where[f"odd{h}"]
                outs = [(rq[:, 0, :], 1.0), (rq[:, 1, :], 1.0), (rk[:, 0, :], 256 ** -0.5), (rk[:, 1, :], 256 ** -0.5)]
                outs += [(rv[:, j, 0:256], 1.0) for j in range(4)] + [(rv[:, j, 256:512], 1.0) for j in range(4)]
                t = 0
                for c in range(6):
                    for m in range(4 if c in (2, 3) else 2):
                        e.wait_ge(tiles_out, before[n0 + c] + m + 1)
                        if t == 0 and h:
                            e.wait_ge(od_dve, 20 * h)
                        if t < 12:
                            src = pbank[t % 8][:, 0:256] if t >= 4 else pbank[t % 8][:, :]
                            ins = e.activation(outs[t][0], src, ACT.Copy, scale=outs[t][1])
                        else:
                            ins = e.activation(rg[:, t - 12, :], pbank[t % 8][:, :], ACT.Silu)
                        ins.then_inc(od_proj, 1)
                        t += 1
                    act_hi(e, n0 + c + 2)
                for t in range(4):
                    e.wait_ge(od_pe, 9 * h + 4 + t + 1)
                    e.activation(rsq[:, t, :], pbank[4 + t][:, :], ACT.Square).then_inc(od_act, 1)
                e.wait_ge(od_pe, 9 * h + 9)
                e.activation(rrt, pbank[0][:, :], ACT.Sqrt, bias=eps[:, 0:1], scale=1.0 / 512).then_inc(od_act, 1)
                for t in range(4):
                    e.wait_ge(od_dve, 20 * h + 4 + t + 1)
                    e.activation(u_hi[:, t, :], ry[:, t, :], ACT.Copy).then_inc(od_act, 1)
                act_hi(e, n0 + 8)
                act_hi(e, n0 + 9)
                e.drain().then_inc(od_act, 1)

        def dve_odd(e, chain):
            e.wait_ge(od_pool, 2)
            for h in range(C_H):
                n0 = where[f"odd{h}"]
                for c in range(6):
                    dve_lo(e, n0 + c + 2)
                for k in range(QT):
                    e.wait_ge(od_pe, 9 * h + k + 1)
                    w = S - k * P
                    e.tensor_tensor(rp[:, k, 0:w], pbank[k][:, 0:w], rdec[:, h, 0:w], MUL).then_inc(od_dve, 1)
                e.wait_ge(od_act, C_H + 10 * h + 5)
                chain(e.reciprocal(rrt, rrt))
                for t in range(4):
                    chain(e.tensor_tensor(ry[:, t, :], pbank[4 + t][:, :], rrt, MUL))
                    e.tensor_tensor(ry[:, t, :], ry[:, t, :], rg[:, t, :], MUL).then_inc(od_dve, 1)
                for t in range(4):
                    e.wait_ge(od_act, C_H + 10 * h + 5 + t + 1)
                    e.tensor_tensor(u_lo[:, t, :], ry[:, t, :], u_hi[:, t, :].bitcast(F32), ALU.subtract)\
                        .then_inc(od_dve, 1)
                for c in range(2):
                    for m in range(4):
                        e.wait_ge(tiles_out, before[n0 + 6 + c] + m + 1)
                        t = 4 * c + m
                        if h == 0:
                            ins = e.tensor_copy(fsum[:, t, :], pbank[4 * c + m][:, :])
                        else:
                            ins = e.tensor_tensor(fsum[:, t, :], fsum[:, t, :], pbank[4 * c + m][:, :], ALU.add)
                        ins.then_inc(od_dve, 1)
                    dve_lo(e, n0 + 8 + c)

        block = ctx.enter_context(nc.Block())

        @block.sync
        def _(sp):
            sp_setup(sp)
            n = 0
            for stage, step in enumerate(PLAN):
                if step[0] == "ffn":
                    sp_ffn(sp, step[1])
                    n = where[step[1]] + FFN[step[1]]["groups"] * (FFN[step[1]]["gu"] + 1)
                while n < TOTAL and stream[n][0] is not None and n < ends[stage]:
                    load_chunk(sp, n, None, 0, 0)
                    n += 1
                if step[0] == "store":
                    sp_store(sp, stage)

        @block.gpsimd
        def _(pool):
            chain = Chain(pool, pool_step)
            for stage, step in enumerate(PLAN):
                enter(pool, stage)
                if step[0] == "setup":
                    pool_setup(pool, chain)
                elif step[0] == "rg":
                    pool_rg(pool)
                elif step[0] == "nsa":
                    pool_nsa(pool, chain)
                elif step[0] == "even":
                    pool_even(pool, chain)
                elif step[0] == "odd":
                    pool_odd(pool, chain)
                elif step[0] == "norm" and PLAN[stage + 1][0] == "ffn" and FFN[PLAN[stage + 1][1]]["swiglu"]:
                    pool.memset(fsum[:, :, :], 0.0)
                leave(pool, "pool")

        @block.scalar
        def _(act):
            chain = Chain(act, act_step)
            act_hi(act, 0)
            act_hi(act, 1)
            for stage, step in enumerate(PLAN):
                enter(act, stage)
                if step[0] == "norm":
                    act_norm(act, stage, step[1], True)
                elif step[0] == "norm_x":
                    act_norm(act, stage, x, False)
                elif step[0] == "post":
                    act_norm(act, stage, fsum, False)
                elif step[0] == "ffn":
                    act_ffn(act, step[1])
                elif step[0] == "rg":
                    act_rg(act, chain)
                elif step[0] == "nsa":
                    act_nsa(act, chain)
                elif step[0] == "even":
                    act_even(act, chain)
                elif step[0] == "odd":
                    act_odd(act, chain)
                leave(act, "act")

        @block.vector
        def _(dve):
            chain = Chain(dve, dve_step)
            dve_lo(dve, 0)
            dve_lo(dve, 1)
            for stage, step in enumerate(PLAN):
                enter(dve, stage)
                if step[0] == "setup":
                    dve_setup(dve)
                elif step[0] == "norm":
                    dve_norm(dve, stage, step[1], step[2], step[3], True, chain)
                elif step[0] == "norm_x":
                    dve_norm(dve, stage, x, step[1], step[2], False, chain)
                elif step[0] == "post":
                    dve_post(dve, stage, step[1], step[2], step[3], chain)
                elif step[0] == "ffn":
                    dve_ffn(dve, step[1])
                elif step[0] == "rg":
                    dve_rg(dve, chain)
                elif step[0] == "nsa":
                    dve_nsa(dve, chain)
                elif step[0] == "even":
                    dve_even(dve, chain)
                elif step[0] == "odd":
                    dve_odd(dve, chain)
                elif step[0] == "store":
                    dve_store(dve)
                leave(dve, "dve")

        @block.tensor
        def _(pe):
            for stage, step in enumerate(PLAN):
                enter(pe, stage)
                if step[0] == "setup":
                    pe_setup(pe)
                elif step[0] in ("norm", "norm_x", "post"):
                    pe_norm(pe, stage, None)
                elif step[0] == "ffn":
                    pe_ffn(pe, step[1])
                elif step[0] == "rg":
                    pe_rg(pe)
                elif step[0] == "nsa":
                    pe_nsa(pe)
                elif step[0] == "even":
                    pe_even(pe)
                elif step[0] == "odd":
                    pe_odd(pe)
                elif step[0] == "store":
                    pe_store(pe)
                leave(pe, "pe")


_INS = ["x", "norm_mix", "norm_ffn", "norm_final", "rg_w_in", "rg_conv_w", "rg_conv_b", "rg_w_a", "rg_b_a",
        "rg_w_x", "rg_b_x", "rg_lambda", "rg_w_out", "nsa_w_in", "nsa_b_gate", "nsa_pe_k", "nsa_pe_v",
        "nsa_w1_k", "nsa_w2_k", "nsa_w1_v", "nsa_w2_v", "nsa_w_out", "mlp_w_up", "mlp_w_down", "norms_2",
        "ffn_wgu_2", "ffn_wd_2", "even_w_in_2", "even_w_out_2", "diff_lam_2", "diff_subln_2", "rwkv_mu_2",
        "rwkv_vec_2", "rwkv_w_up_2", "rwkv_a_up_2", "rwkv_g_up_2", "odd_w_in_2", "odd_w_out_2"]


def kernel(**inputs):
    import numpy as _np
    import concourse.bacc as _bacc
    from concourse import mybir as _mybir
    from concourse.bass_utils import run_bass_kernel_spmd as _run

    nc = _bacc.Bacc("TRN2", target_bir_lowering=False, num_devices=1)
    arrays, args = {}, {}
    for name in _INS:
        a = _np.ascontiguousarray(inputs[name])
        arrays[f"in_{name}"] = a
        args[name] = nc.dram_tensor(f"in_{name}", a.shape, _mybir.dt.from_np(a.dtype), kind="ExternalInput").ap()
    out = nc.dram_tensor("out_x", (1, S, D), _mybir.dt.float32, kind="ExternalOutput").ap()
    build(nc, args, out)
    r = _run(nc, [arrays], core_ids=[0])
    return r.results[0]["out_x"]
```

```python
from contextlib import ExitStack
import math

import concourse.bass as bass
from concourse import mybir

F32 = mybir.dt.float32
F32R = mybir.dt.float32r
ACT = mybir.ActivationFunctionType
ALU = mybir.AluOpType
AX = mybir.AxisListType

P = 128
S = 512
D = 1024
KT = D // P
QT = S // P
CH = 2048
BIG = -1e30
EPS = 1e-6

HEADS, HD, GROUPS = 16, 64, 4
CMP_LEN, CMP_STRIDE = 32, 16
NC = S // CMP_STRIDE - 1
DFF = 4 * D
RG_C = 8.0
DFF2 = 2816
RCH = 64


def build(nc, a, out):
    ctx = ExitStack()
    with ctx:
        def sb(name, shape, dt=F32):
            return ctx.enter_context(nc.sbuf_tensor(name, shape, dt))

        def sem(name):
            return ctx.enter_context(nc.semaphore(name))

        x = sb("x", [P, KT, S])
        raw = sb("raw", [P, 2, CH])
        whi = sb("whi", [P, 2, CH], F32R)
        wlo = sb("wlo", [P, 2, CH], F32R)
        split_zone = sb("split_zone", [P, 24 * S])
        zone = nc.sbuf_base - 24 * S * 4
        h_hi = nc.alloc_sbuf_tensor_at("h_hi", [P, KT, S], F32R, offset=zone)
        h_lo = nc.alloc_sbuf_tensor_at("h_lo", [P, KT, S], F32R, offset=zone + 8 * S * 4)
        u_hi = nc.alloc_sbuf_tensor_at("u_hi", [P, 4, S], F32R, offset=zone + 16 * S * 4)
        u_lo = nc.alloc_sbuf_tensor_at("u_lo", [P, 4, S], F32R, offset=zone + 20 * S * 4)
        fsum = sb("fsum", [P, KT, S])
        tmp = sb("tmp", [P, 8, S])
        ident = sb("ident", [P, P])
        ones = sb("ones", [P, P])
        par = sb("par", [P, 3, P])
        eps = sb("eps", [P, 4])
        rstat = sb("rstat", [P, 2 * QT])
        AR = 14848
        arena = sb("arena", [P, AR])
        pbank = [ctx.enter_context(nc.psum_tensor(f"bank{i}", [P, S], F32)) for i in range(8)]

        def tiles(at, n, w=S):
            return arena[:, at:at + n * w].rearrange("p (t n) -> p t n", n=w)

        loaded = [sem("loaded0"), sem("loaded1")]
        hi_ready = sem("hi_ready")
        lo_ready = sem("lo_ready")
        tiles_out = sem("tiles_out")
        done = {k: sem(f"{k}_done") for k in ("pe", "act", "dve", "pool")}
        act_step = sem("act_step")
        dve_step = sem("dve_step")
        pool_step = sem("pool_step")
        const_in = sem("const_in")
        small_in = sem("small_in")
        stored = sem("stored")
        gate_done = sem("gate_done")
        prod_done = sem("prod_done")
        uhi_done = sem("uhi_done")
        ulo_done = sem("ulo_done")
        added = sem("added")
        n_sq = sem("n_sq")
        n_add = sem("n_add")
        n_sum = sem("n_sum")
        n_diag = sem("n_diag")
        n_rs = sem("n_rs")
        cleared = sem("cleared")
        n_rt = sem("n_rt")
        n_hn = sem("n_hn")
        n_hi = sem("n_hi")
        n_lo = sem("n_lo")
        s_pe = sem("s_pe")
        s_act = sem("s_act")
        s_dve = sem("s_dve")
        s_pool = sem("s_pool")

        def at(c, i, k):
            return c if i is None else i * k + c

        class Chain:

            def __init__(self, eng, own):
                self.eng, self.own, self.n = eng, own, 0

            def __call__(self, ins):
                ins.then_inc(self.own, 1)
                self.n += 1
                self.eng.wait_ge(self.own, self.n)

        stream = []
        where = {}

        def cols(w, c, n=256, kt=KT):
            return w.rearrange("(k p) n -> p k n", p=P)[:, :, c:c + n]

        def whole(k, n):
            return lambda slot: raw[:, slot, 0:k * n].rearrange("p (k n) -> p k n", k=k)

        def add_chunks(name, srcs, outs):
            where[name] = len(stream)
            for src in srcs:
                stream.append(([(whole(src.shape[1], src.shape[2]), src)], outs))

        def ffn_chunks(name, groups, gu):
            where[name] = len(stream)
            for g in range(groups):
                stream.extend([(None, 2)] * gu)
                if g > 0:
                    stream.append((None, 8))
            stream.append((None, 8))

        rg_in, rg_out = a["rg_w_in"][0], a["rg_w_out"][0]
        nsa_in, nsa_out = a["nsa_w_in"][0], a["nsa_w_out"][0]
        even_in, even_out = a["even_w_in_2"][0], a["even_w_out_2"][0]
        odd_in, odd_out = a["odd_w_in_2"][0], a["odd_w_out_2"][0]
        NG1 = DFF // 256
        NG2 = DFF2 // 256
        FFN = {}

        def mlp(i):
            up = a["mlp_w_up"][i].rearrange("(k p) (c n) -> c p k n", p=P, n=256)
            down = a["mlp_w_down"][i].rearrange("(c k p) n -> c p k n", k=2, p=P)
            return dict(gu=1, groups=NG1, w=[up], down=down, swiglu=False, dst=x)

        def swi(l, i):
            w = a["ffn_wgu_2"][l, i]
            g = w[:, 0:DFF2].rearrange("(k p) (c n) -> c p k n", p=P, n=256)
            u = w[:, DFF2:2 * DFF2].rearrange("(k p) (c n) -> c p k n", p=P, n=256)
            down = a["ffn_wd_2"][l, i].rearrange("(c k p) n -> c p k n", k=2, p=P)
            return dict(gu=2, groups=NG2, w=[g, u], down=down, swiglu=True, dst=fsum)

        PG = dict(mix=0, ffn=16, final=32, conv_w=40, conv_b=72, b_a=80, b_x=88, lam=96)
        PN2, PMU, PSUB, PVEC = 0, 96, 110, 0

        def gain(sec, i):
            return par[:, sec, i:i + 1]

        PLAN = [("setup",), ("norm", x, 0, PG["mix"]), ("rg",), ("norm", x, 0, PG["ffn"]), ("ffn", "f0")]
        FFN["f0"] = mlp(0)
        PLAN += [("norm", x, 0, PG["mix"] + KT), ("nsa",), ("norm", x, 0, PG["ffn"] + KT), ("ffn", "f1")]
        FFN["f1"] = mlp(1)
        PLAN += [("norm_x", 0, PG["final"])]
        for l in range(2):
            n2 = PN2 + l * 6 * KT
            for i in range(2):
                FFN[f"s{l}{i}"] = swi(l, i)
            PLAN += [("norm", x, 1, n2), ("ffn", f"s{l}0"), ("post", 1, n2 + KT, 0.5), ("norm", x, 1, n2 + 2 * KT),
                     (("even",), ("odd",))[l], ("post", 1, n2 + 3 * KT, 1.0), ("norm", x, 1, n2 + 4 * KT),
                     ("ffn", f"s{l}1"), ("post", 1, n2 + 5 * KT, 0.5)]
        PLAN += [("store",)]

        ends = []
        for step in PLAN:
            if step[0] == "rg":
                add_chunks("rg_in", [cols(rg_in, 256 * c) for c in range(8)], 2)
                where["rg_gates"] = len(stream)
                for w in (a["rg_w_a"][0], a["rg_w_x"][0]):
                    stream.append(([((lambda n: lambda slot: raw[:, slot, n * 512:(n + 1) * 512].rearrange(
                        "p (k n) -> p k n", k=2))(n), w[n].rearrange("(k p) n -> p k n", p=P)) for n in range(4)], 8))
                add_chunks("rg_out", [cols(rg_out, 256 * c) for c in range(4)], 2)
            elif step[0] == "ffn":
                ffn_chunks(step[1], FFN[step[1]]["groups"], FFN[step[1]]["gu"])
            elif step[0] == "nsa":
                q_src = nsa_in[:, 0:D].rearrange("(k p) (t h g d) -> t g p k h d", p=P, t=2, h=2, g=4)
                add_chunks("nsa_in", [cols(nsa_in, D), cols(nsa_in, D + 256)], 2)
                for c in range(4):
                    stream.append(([((lambda j: lambda slot: raw[:, slot, :].rearrange(
                        "p (k m h d) -> p k m h d", k=KT, m=2, h=2)[:, :, j // 2, j % 2])(j), q_src[c // 2, 2 * (c % 2) + j // 2][:, :, j % 2, :])
                        for j in range(4)], 2))
                for c in (2, 4):
                    stream.append(([(whole(8, 256), cols(nsa_in, D + 256 * c))], 2))
                for c in (3, 5):
                    stream.append(([(whole(8, 256), cols(nsa_in, D + 256 * c))], 4))
                add_chunks("nsa_out", [cols(nsa_out, 256 * c) for c in range(4)], 2)
            elif step[0] == "even":
                add_chunks("even_a", [cols(even_in, 256 * c) for c in range(4)], 2)
                add_chunks("even_v", [cols(even_in, 1024 + 256 * c) for c in range(2)], 4)
                add_chunks("even_b", [cols(even_in, 1536 + 256 * c) for c in range(7)], 2)
                add_chunks("even_out", [cols(even_out, 256 * c) for c in range(4)], 2)
            elif step[0] == "odd":
                def qk(h):
                    return [cols(odd_in, 256 * h), cols(odd_in, 1024 + 256 * h)]
                add_chunks("odd", qk(0), 2)
                for h in range(4):
                    for c in range(2):
                        stream.append(([(whole(8, 256), cols(odd_in, 2048 + 512 * h + 256 * c))], 4))
                    for c in range(2):
                        stream.append(([(whole(8, 256), cols(odd_in, 4096 + 512 * h + 256 * c))], 2))
                    if h < 3:
                        stream.extend(([(whole(8, 256), w)], 2) for w in qk(h + 1))
                    wo = odd_out.rearrange("(h k p) n -> h p k n", k=4, p=P)[h]
                    for c in range(2):
                        stream.append(([(whole(4, 512), wo[:, :, 512 * c:512 * c + 512])], 4))
            ends.append(len(stream))
        before = [0]
        landed = []
        for n, (parts, outs) in enumerate(stream):
            before.append(before[-1] + outs)
            landed.append((landed[n - 2] if n > 1 else 0) + 16 * (1 if parts is None else len(parts)))
        TOTAL = len(stream)
        ffn_base, k = {}, 0
        for step in PLAN:
            if step[0] == "ffn":
                ffn_base[step[1]] = k
                k += FFN[step[1]]["groups"]
        norm_base, k = {}, 0
        for i, step in enumerate(PLAN):
            if step[0] in ("norm", "norm_x", "post"):
                norm_base[i] = k
                k += KT

        def enter(e, stage, always=False):
            kinds = [s_[0] for s_ in PLAN]
            if stage and (always or (kinds[stage] not in ("norm", "norm_x", "post", "store")
                                     and kinds[stage - 1] != "norm")):
                for k in ("pe", "act", "dve", "pool"):
                    e.wait_ge(done[k], stage)

        def leave(e, k):
            e.drain().then_inc(done[k], 1)

        def load_chunk(e, n, i, dn, dt, src=None):
            parts = stream[n][0] if src is None else [(whole(src.shape[1], src.shape[2]), src)]
            if n >= 2:
                e.wait_ge(lo_ready, at(n - 1, i, dn))
            for dst, s in parts:
                e.dma_start(dst(n % 2), s).then_inc(loaded[n % 2], 16)

        def act_hi(e, n, i=None, dn=0, dt=0):
            if i is None and n >= TOTAL:
                return
            e.wait_ge(loaded[n % 2], at(landed[n], i, dn * 8))
            if n >= 2:
                e.wait_ge(tiles_out, at(before[n - 1], i, dt))
            e.activation(whi[:, n % 2, :], raw[:, n % 2, :], ACT.Copy).then_inc(hi_ready, 1)

        def dve_lo(e, n, i=None, dn=0, dt=0):
            if i is None and n >= TOTAL:
                return
            e.wait_ge(hi_ready, at(n + 1, i, dn))
            e.tensor_tensor(wlo[:, n % 2, :], raw[:, n % 2, :], whi[:, n % 2, :].bitcast(F32),
                            ALU.subtract).then_inc(lo_ready, 1)

        def three(pe, o, w_hi, w_lo, r_hi, r_lo, first, last):
            pe.matmul(o, w_hi, r_hi, start=first, stop=False)
            pe.matmul(o, w_hi, r_lo, start=False, stop=False)
            return pe.matmul(o, w_lo, r_hi, start=False, stop=last)

        def pe_chunk(pe, n, kt, mt, hi, lo, outs, free=None, i=None, dn=0, k0=0, first=True, last=True, off=0, ready=True):
            s = n % 2
            if ready:
                pe.wait_ge(lo_ready, at(n + 1, i, dn))
            for m in range(mt):
                if free:
                    free(m)
                for k in range(kt):
                    c = off + k * mt * P + m * P
                    ins = three(pe, outs(m), whi[:, s, c:c + P], wlo[:, s, c:c + P], hi[:, k0 + k, :], lo[:, k0 + k, :],
                                first and k == 0, last and k == kt - 1)
                ins.then_inc(tiles_out, 1)

        def pe_rows(pe, n, outs, free=None):
            s = n % 2
            pe.wait_ge(lo_ready, n + 1)
            for t in range(QT):
                if free:
                    free(t)
                for k in range(KT):
                    c = slice(k * 256, k * 256 + 256)
                    q = slice(t * P, t * P + P)
                    pe.matmul(outs(t), h_hi[:, k, q], whi[:, s, c], start=k == 0, stop=False)
                    pe.matmul(outs(t), h_hi[:, k, q], wlo[:, s, c], start=False, stop=False)
                    ins = pe.matmul(outs(t), h_lo[:, k, q], whi[:, s, c], start=False, stop=k == KT - 1)
                ins.then_inc(tiles_out, 1)

        def ffn_walk(e, name, gu, dn):
            f = FFN[name]
            G, per = f["groups"], f["gu"] + 1
            n0 = where[name]

            def n_gu(g):
                return n0 if g == 0 else n0 + f["gu"] + (g - 1) * per

            def n_dn(g):
                return n0 + f["gu"] + g * per + f["gu"] if g < G - 1 else n0 + G * per - 1
            turns = (G - 1) // 2
            if n0 + G * per == TOTAL and 2 * turns == G - 1:
                turns -= 1
            dt = 2 * (2 * f["gu"] + 8)
            gu(0, n_gu(0), None, 0, 0)
            with e.Fori(0, turns) as i:
                for g in (1, 2):
                    gu(g, n_gu(g), i, 2 * per, dt)
                    dn(g - 1, n_dn(g - 1), i, 2 * per, dt)
            for g in range(2 * turns + 1, G):
                gu(g, n_gu(g), None, 0, 0)
                dn(g - 1, n_dn(g - 1), None, 0, 0)
            dn(G - 1, n_dn(G - 1), None, 0, 0)

        def after_down(name, g):
            gu = FFN[name]["gu"]
            return before[where[name]] + 2 * gu * (g + 2) + 8 * (g + 1)

        def sp_ffn(e, name):
            f = FFN[name]

            def gu(g, n, i, dn, dt):
                for c, w in enumerate(f["w"]):
                    load_chunk(e, n + c, i, dn, dt, w[at(g, i, 2)])

            def down(g, n, i, dn, dt):
                load_chunk(e, n, i, dn, dt, f["down"][at(g, i, 2)])
            ffn_walk(e, name, gu, down)

        def pe_ffn(pe, name, stage):
            f, b = FFN[name], ffn_base[name]

            def gu(g, n, i, dn, dt):
                for c in range(f["gu"]):
                    def free(m):
                        if g > 0:
                            pe.wait_ge(prod_done, at(2 * (b + g - 1) + m + 1, i, 4))
                    if g == 0 and c == 0:
                        pe_first(pe, n, stage)
                        continue
                    pe_chunk(pe, n + c, KT, 2, h_hi, h_lo, lambda m: pbank[2 * c + m][:, :], free, i, dn)

            def down(g, n, i, dn, dt):
                pe.wait_ge(ulo_done, at(2 * (b + g) + 2, i, 4))

                def free(m):
                    pe.wait_ge(added, at(8 * (b + g) + m + 5, i, 16))
                pe_chunk(pe, n, 2, 8, u_hi, u_lo, lambda m: pbank[4 + m % 4][:, :], free, i, dn, k0=2 * (g % 2))
            ffn_walk(pe, name, gu, down)

        def act_ffn(e, name):
            f, b = FFN[name], ffn_base[name]

            def gu(g, n, i, dn, dt):
                for j in range(2):
                    e.wait_ge(tiles_out, at(before[n] + j + 1, i, dt))
                    if g > 0:
                        e.wait_ge(prod_done, at(2 * (b + g - 1) + j + 1, i, 4))
                    e.activation(tmp[:, j, :], pbank[j][:, :], ACT.Silu if f["swiglu"] else ACT.Relu)\
                        .then_inc(gate_done, 1)
                if f["swiglu"]:
                    act_hi(e, n + 2, i, dn, dt)
                for j in range(2):
                    e.wait_ge(prod_done, at(2 * (b + g) + j + 1, i, 4))
                    if g > 0:
                        e.wait_ge(tiles_out, at(after_down(name, g - 2), i, dt))
                    e.activation(u_hi[:, 2 * (g % 2) + j, :], tmp[:, 2 + j, :], ACT.Copy).then_inc(uhi_done, 1)
                act_hi(e, n + f["gu"] + 1, i, dn, dt)

            def down(g, n, i, dn, dt):
                if i is not None or g < f["groups"] - 1:
                    act_hi(e, n + 2, i, dn, dt)
            ffn_walk(e, name, gu, down)

        def dve_ffn(e, name, stage):
            f, b = FFN[name], ffn_base[name]
            dst = f["dst"]
            if f["swiglu"]:
                e.wait_ge(cleared, sum(s_[0] == "ffn" and FFN[s_[1]]["swiglu"] for s_ in PLAN[:stage]) + 1)

            def gu(g, n, i, dn, dt):
                if f["swiglu"]:
                    dve_lo(e, n + 2, i, dn, dt)
                for j in range(2):
                    e.wait_ge(gate_done, at(2 * (b + g) + j + 1, i, 4))
                    if f["swiglu"]:
                        e.wait_ge(tiles_out, at(before[n + 1] + j + 1, i, dt))
                    if g > 0:
                        e.wait_ge(ulo_done, at(2 * (b + g - 1) + j + 1, i, 4))
                    if f["swiglu"]:
                        ins = e.tensor_tensor(tmp[:, 2 + j, :], pbank[2 + j][:, :], tmp[:, j, :], ALU.mult)
                    else:
                        ins = e.scalar_tensor_tensor(tmp[:, 2 + j, :], pbank[j][:, :], 0.0, tmp[:, j, :],
                                                     ALU.max, ALU.mult)
                    ins.then_inc(prod_done, 1)
                for j in range(2):
                    e.wait_ge(uhi_done, at(2 * (b + g) + j + 1, i, 4))
                    u = 2 * (g % 2) + j
                    e.tensor_tensor(u_lo[:, u, :], tmp[:, 2 + j, :], u_hi[:, u, :].bitcast(F32),
                                    ALU.subtract).then_inc(ulo_done, 1)
                if g == 0:
                    dve_lo(e, n + f["gu"] + 1, i, dn, dt)

            def down(g, n, i, dn, dt):
                final = i is None and g == f["groups"] - 1
                for m in range(8):
                    if m == 4 and not final:
                        dve_lo(e, n + 1, i, dn, dt)
                    e.wait_ge(tiles_out, at(before[n] + m + 1, i, dt))
                    if b + g > 0 or i is not None:
                        e.wait_ge(added, at(8 * (b + g) + m + 1, i, 16))
                    e.tensor_tensor(dst[:, m, :], dst[:, m, :], pbank[4 + m % 4][:, :], ALU.add)\
                        .then_inc(added, 1)
                if not final:
                    dve_lo(e, n + 2, i, dn, dt)
            ffn_walk(e, name, gu, down)

        acc, diag = tmp[:, 7, :], tmp[:, 4, :]
        SUMS, SPREAD = pbank[3][:, 0:QT], pbank[2][:, :]

        def final(e, stage, k):
            kind = PLAN[stage - 1][0]
            if kind == "setup":
                e.wait_ge(added, k + 1)
            elif kind == "ffn":
                name = PLAN[stage - 1][1]
                e.wait_ge(added, 8 * (ffn_base[name] + FFN[name]["groups"]) + k + 1)
            elif kind in ("rg", "nsa", "even"):
                e.wait_ge(out_taken, KT * sum(s_[0] in ("rg", "nsa", "even") for s_ in PLAN[:stage - 1]) + k + 1)
            elif kind == "odd":
                e.wait_ge(od_dve, 20 * 3 + 12 + k + 1)
            else:
                e.wait_ge(n_hn, norm_base[stage - 1] + k + 1)

        def owes(stage):
            return PLAN[stage - 1][0] in ("ffn", "rg", "nsa", "even", "odd")

        def act_norm(e, stage, src, split):
            b = norm_base[stage]
            j = b // KT
            for k in range(KT):
                final(e, stage, k)
                if k >= 3:
                    e.wait_ge(n_add, 6 * j + max(1, k - 3))
                e.activation(tmp[:, 4 + k % 3, :], src[:, k, :], ACT.Square).then_inc(n_sq, 1)
            if owes(stage):
                act_hi(e, ends[stage - 1] + 1)
            e.wait_ge(n_sum, j + 1)
            e.activation(rstat[:, 0:QT], SUMS, ACT.Sqrt, bias=eps[:, 0:1], scale=1.0 / D).then_inc(n_rt, 1)
            if split:
                for k in range(KT):
                    e.wait_ge(n_hn, b + k + 1)
                    e.activation(h_hi[:, k, :], tmp[:, k % 4, :], ACT.Copy).then_inc(n_hi, 1)

        def pool_norm(e, stage):
            b = norm_base[stage]
            j = b // KT
            for k in range(1, KT - 1):
                e.wait_ge(n_sq, b + k + 1)
                if k > 1:
                    e.wait_ge(n_add, 6 * j + k - 1)
                e.tensor_tensor(acc, tmp[:, 4, :] if k == 1 else acc, tmp[:, 4 + k % 3, :], ALU.add).then_inc(n_add, 1)

        def pe_norm(pe, stage):
            j = norm_base[stage] // KT
            pe.wait_ge(n_add, 6 * j + 6)
            for q in range(QT):
                pe.matmul(SUMS[:, q:q + 1], acc[:, q * P:q * P + P], ones[:, 0:1], start=q == 0, stop=False,
                          skip_group_check=True)
            pe.wait_ge(n_sq, KT * j + KT)
            for q in range(QT):
                ins = pe.matmul(SUMS[:, q:q + 1], tmp[:, 5, q * P:q * P + P], ones[:, 0:1], start=False, stop=True,
                                skip_group_check=True)
            ins.then_inc(n_sum, 1)
            pe.wait_ge(n_diag, j + 1)
            pe.matmul(SPREAD, ones[:, :], diag, start=True, stop=True).then_inc(n_rs, 1)

        def dve_root(e, stage, chain):
            j = norm_base[stage] // KT
            e.wait_ge(n_rt, j + 1)
            chain(e.reciprocal(rstat[:, QT:2 * QT], rstat[:, 0:QT]))
            e.tensor_tensor(diag.rearrange("p (q n) -> p q n", q=QT), ident[:, :].unsqueeze(1).broadcast_to([P, QT, P]),
                            rstat[:, QT:2 * QT].unsqueeze(2).broadcast_to([P, QT, P]), ALU.mult).then_inc(n_diag, 1)
            if owes(stage):
                dve_lo(e, ends[stage - 1] + 1)
            e.wait_ge(n_rs, j + 1)

        def dve_norm(e, stage, src, sec, g0, split, chain):
            if stage == 1:
                e.wait_ge(setup_out, 1)
            dve_root(e, stage, chain)
            bs = b_split(stage)

            def lo(k):
                e.wait_ge(n_hi, bs + k + 1)
                e.tensor_tensor(h_lo[:, k, :], tmp[:, k % 4, :], h_hi[:, k, :].bitcast(F32), ALU.subtract)\
                    .then_inc(n_lo, 1)
            for k in range(KT):
                o = tmp[:, k % 4, :] if split else x[:, k, :]
                if split and k >= 4:
                    e.wait_ge(n_lo, bs + k - 3)
                e.scalar_tensor_tensor(o, src[:, k, :], gain(sec, g0 + k), SPREAD, ALU.mult, ALU.mult)\
                    .then_inc(n_hn, 1)
                if split and k > 0:
                    lo(k - 1)
            if split:
                lo(KT - 1)

        def b_split(stage):
            return KT * sum(1 for s_ in PLAN[:stage] if s_[0] == "norm")

        def dve_post(e, stage, sec, g0, scale, chain):
            dve_root(e, stage, chain)
            for k in range(KT):
                chain(e.scalar_tensor_tensor(tmp[:, k % 4, :], fsum[:, k, :], gain(sec, g0 + k), SPREAD,
                                             ALU.mult, ALU.mult))
                e.scalar_tensor_tensor(x[:, k, :], tmp[:, k % 4, :], scale, x[:, k, :], ALU.mult, ALU.add)\
                    .then_inc(n_hn, 1)

        def pe_first(pe, n, stage):
            s = n % 2
            pe.wait_ge(lo_ready, n + 1)
            for k in range(KT):
                pe.wait_ge(n_lo, b_split(stage) - KT + k + 1)
                for m in range(2):
                    c = k * 256 + m * P
                    ins = three(pe, pbank[m][:, :], whi[:, s, c:c + P], wlo[:, s, c:c + P], h_hi[:, k, :], h_lo[:, k, :],
                                k == 0, k == KT - 1)
                    if k == KT - 1:
                        ins.then_inc(tiles_out, 1)

        xrows = fsum[:, :, :].rearrange("p t n -> p (t n)").rearrange("p (q c) -> p q c", q=QT)
        prow = arena[:, 0:S].rearrange("p (r n) -> p r n", n=P)

        def vec(v, n):
            return v.rearrange("(r n) -> r n", n=P) if n == 1 else v.rearrange("l (r n) -> (l r) n", n=P)

        ROWS = [(0, PG["mix"], vec(a["norm_mix"], 2)), (0, PG["ffn"], vec(a["norm_ffn"], 2)),
                (0, PG["final"], vec(a["norm_final"], 1)), (0, PG["conv_w"], vec(a["rg_conv_w"][0], 2)),
                (0, PG["conv_b"], vec(a["rg_conv_b"][0], 1)), (0, PG["b_a"], vec(a["rg_b_a"][0], 1)),
                (0, PG["b_x"], vec(a["rg_b_x"][0], 1)), (0, PG["lam"], vec(a["rg_lambda"][0], 1)),
                (1, PN2, a["norms_2"].rearrange("l i (r n) -> (l i r) n", n=P)),
                (1, PMU, vec(a["rwkv_mu_2"][0], 1)), (1, PSUB, a["diff_subln_2"]),
                (2, PVEC, vec(a["rwkv_vec_2"][0], 2))]

        def sp_setup(e):
            for q in range(QT):
                e.dma_start(xrows[:, q, :], a["x"][0].rearrange("(q p) c -> q p c", p=P)[q]).then_inc(x_in[q], 16)
            e.wait_ge(pool_step, 1)
            for r, at0, src in ROWS:
                e.dma_start(prow[at0:at0 + src.shape[0], r, :], src).then_inc(const_in, 16)

        def pool_setup(e, chain):
            chain(e.memset(arena[:, 0:S], 0.0))
            chain(e.memset(ident[:, :], 0.0))
            chain(e.affine_select(out=ident[:, :], in_=ident[:, :], compare_op=ALU.not_equal, fill=1.0, base=0,
                                  pattern=[[-1, P]], channel_multiplier=1))
            e.memset(ones[:, :], 1.0)
            for j, v in enumerate((EPS, 64e-5, 1.0, 0.0)):
                e.memset(eps[:, j:j + 1], v)

        def pe_setup(pe):
            pe.wait_ge(pool_step, 3)
            for q in range(QT):
                pe.wait_ge(x_in[q], 16)
                for k in range(KT):
                    ins = pe.transpose(pbank[k][:, q * P:q * P + P], xrows[:, q, k * P:k * P + P], ident[:, :])
                    if q == QT - 1:
                        ins.then_inc(setup_pe, 1)
            pe.wait_ge(const_in, 16 * len(ROWS))
            pe.wait_ge(added, 1)
            for r in range(3):
                ins = pe.transpose(pbank[0][:, r * P:r * P + P], prow[:, r, :], ident[:, :])
            ins.then_inc(setup_par, 1)

        def dve_setup(e):
            for k in range(KT):
                e.wait_ge(setup_pe, k + 1)
                e.tensor_copy(x[:, k, :], pbank[k][:, :]).then_inc(added, 1)
            e.wait_ge(setup_par, 1)
            e.tensor_copy(par[:, :, :].rearrange("p r n -> p (r n)"), pbank[0][:, 0:3 * P]).then_inc(setup_out, 1)

        orows = tiles(0, QT, D)
        STORE_BANKS = ((4, 5, 6, 7), (0, 1, 3, 4))

        def pe_store(pe, stage):
            for half in range(2):
                for k in range(4):
                    final(pe, stage, 4 * half + k)
                    if half == 1 and k == 0:
                        pe.wait_ge(store_act, 1)
                    for q in range(QT):
                        ins = pe.transpose(pbank[STORE_BANKS[half][q]][:, k * P:k * P + P],
                                           x[:, 4 * half + k, q * P:q * P + P], ident[:, :])
                        if k == 3:
                            ins.then_inc(store_pe, 1)

        def take_store(e, half, q, signal):
            e.wait_ge(store_pe, 4 * half + q + 1)
            dst = orows[:, q, half * 512:half * 512 + 512]
            src = pbank[STORE_BANKS[half][q]][:, :]
            ins = e.activation(dst, src, ACT.Copy) if signal is store_act else e.tensor_copy(dst, src)
            ins.then_inc(signal, 1)

        def act_store(e):
            for half, q in [(0, q) for q in range(QT)] + [(1, 0), (1, 2)]:
                take_store(e, half, q, store_act)

        def dve_store(e):
            for q in (1, 3):
                take_store(e, 1, q, store_dve)
        def sp_store(e, stage):
            for half in range(2):
                for q in range(QT):
                    if half == 1 and q % 2:
                        e.wait_ge(store_dve, q // 2 + 1)
                    else:
                        e.wait_ge(store_act, 4 + q // 2 + 1 if half else q + 1)
                    c = slice(half * 512, half * 512 + 512)
                    e.dma_start(out.rearrange("b (q p) c -> (b q) p c", p=P)[q][:, c], orows[:, q, c]).then_inc(stored, 16)
            e.wait_ge(stored, 16 * 2 * QT)

        setup_par = sem("setup_par")
        setup_pe, setup_out = sem("setup_pe"), sem("setup_out")
        store_pe, store_dve, store_act = sem("store_pe"), sem("store_dve"), sem("store_act")
        x_in = [sem(f"x_in{q}") for q in range(QT)]

        def pe_out(pe, name):
            for c in range(4):
                pe_chunk(pe, where[name] + c, KT, 2, h_hi, h_lo, lambda m: pbank[2 * c + m][:, :])

        def act_out(e, name):
            for c in range(3):
                act_hi(e, where[name] + c + 2)

        def dve_out(e, name, add):
            n = where[name]
            for m in range(KT):
                e.wait_ge(tiles_out, before[n] + m + 1)
                if add:
                    ins = e.tensor_tensor(x[:, m, :], x[:, m, :], pbank[m][:, :], ALU.add)
                else:
                    ins = e.tensor_copy(fsum[:, m, :], pbank[m][:, :])
                ins.then_inc(out_taken, 1)
                if m % 2 and m < KT - 1:
                    dve_lo(e, n + m // 2 + 2)

        out_taken = sem("out_taken")

        rg_act, rg_dve, rg_pool = sem("rg_act"), sem("rg_dve"), sem("rg_pool")
        Y, XB, RR = tiles(0, KT), tiles(8 * S, KT), tiles(16 * S, KT)
        PX = tiles(24 * S, 2, S + 4)
        small = arena[:, 24 * S + 2 * (S + 4):AR]
        GI = fsum
        uz = nc.alloc_sbuf_tensor_at("uz", [P, 8, S], F32, offset=zone + 16 * S * 4)
        RA_XH, RA_R, RA_T, RA_SQ, RA_L, RA_I, RA_E = 16, 24, 32, 40, 48, 56, 64
        RD_RES, RD_END = 18, 34
        RA_EXP = [RA_E + 2 * (t + 1) + max(0, t - 3) for t in range(8)]
        RA_YH_OF = [RA_E + 2 * min(8, t + 4) + t + 1 for t in range(8)]

        def pe_rg(pe, stage):
            n0 = where["rg_in"]
            for c in range(8):
                def free(m):
                    if 2 * c + m >= 8:
                        pe.wait_ge(rg_act, 2 * c + m - 7)
                if c == 0:
                    pe_first(pe, n0, stage)
                    continue
                pe_chunk(pe, n0 + c, KT, 2, h_hi, h_lo, lambda m: pbank[(2 * c + m) % 8][:, :], free)
            for g in range(2):
                for b in range(4):
                    pe.wait_ge(rg_dve, 8 + 2 * b + 2)

                    def free(m):
                        if g:
                            pe.wait_ge(rg_act, RA_R + 2 * b + m + 1)
                    pe_chunk(pe, n0 + 8 + g, 2, 2, h_hi, h_lo, lambda m: pbank[2 * b + m][:, :], free, k0=2 * b,
                             off=512 * b)
            pe.wait_ge(rg_dve, RD_END)
            pe_out(pe, "rg_out")

        def act_rg(e, chain):
            n0 = where["rg_in"]
            c8 = small

            def high(t):
                e.wait_ge(rg_dve, RD_RES + max(1, 2 * t))
                e.activation(h_hi[:, t, :], Y[:, t, :], ACT.Copy).then_inc(rg_act, 1)
            lam = par[:, 0, PG["lam"]:PG["lam"] + KT]
            chain(e.activation(c8[:, 0:8], lam, ACT.Abs))
            chain(e.activation(c8[:, 8:16], c8[:, 0:8], ACT.Exp, scale=-1.0))
            chain(e.activation(c8[:, 16:24], c8[:, 8:16], ACT.Ln, bias=eps[:, 2:3]))
            chain(e.activation(c8[:, 24:32], lam, ACT.Relu, scale=-1.0))
            for c in range(8):
                for m in range(2):
                    t = 2 * c + m
                    e.wait_ge(tiles_out, before[n0 + c] + m + 1)
                    if t < 8:
                        e.activation(Y[:, t, :], pbank[t % 8][:, :], ACT.Gelu_apprx_tanh).then_inc(rg_act, 1)
                    else:
                        if t >= 10:
                            e.wait_ge(rg_dve, t - 9)
                        if t == 8:
                            e.wait_ge(rg_pool, 1)
                        e.activation(PX[:, t % 2, 3:3 + S], pbank[t % 8][:, :], ACT.Copy).then_inc(rg_act, 1)
                act_hi(e, n0 + c + 2)
            e.wait_ge(tiles_out, before[n0 + 8])
            for t in range(8):
                e.wait_ge(rg_dve, t + 1)
                e.activation(h_hi[:, t, :], XB[:, t, :], ACT.Copy).then_inc(rg_act, 1)
            def gates(g, o, b):
                for t in range(8):
                    e.wait_ge(tiles_out, before[n0 + 8 + g] + t + 1)
                    e.activation(o[:, t, :], pbank[t][:, :], ACT.Sigmoid, bias=gain(0, b + t)).then_inc(rg_act, 1)
                act_hi(e, n0 + 8 + g + 2)
            gates(0, RR, PG["b_a"])
            e.wait_ge(rg_dve, RD_RES)
            for t in range(8):
                e.wait_ge(rg_act, RA_R + t + 1)
                e.activation(tmp[:, t, :], RR[:, t, :], ACT.Tanh, scale=c8[:, 32 + t:33 + t]).then_inc(rg_act, 1)
            for t in range(8):
                e.wait_ge(rg_act, RA_T + t + 1)
                e.activation(uz[:, t, :], tmp[:, t, :], ACT.Sqrt, scale=2.0).then_inc(rg_act, 1)
            for t in range(8):
                e.activation(tmp[:, t, :], tmp[:, t, :], ACT.Ln, bias=eps[:, 2:3]).then_inc(rg_act, 1)
            gates(1, GI, PG["b_x"])
            for t in range(8):
                e.wait_ge(rg_act, RA_L + t + 1)
                e.activation(tmp[:, t, :], tmp[:, t, :], ACT.Exp, scale=-0.5).then_inc(rg_act, 1)
                e.activation(RR[:, t, :], RR[:, t, :], ACT.Exp, scale=c8[:, 40 + t:41 + t]).then_inc(rg_act, 1)
                if t > 2:
                    high(t - 3)
            for t in range(5, 8):
                high(t)
            act_out(e, "rg_out")

        def dve_rg(e, chain):
            n0 = where["rg_in"]
            c8 = small
            for c in range(4):
                dve_lo(e, n0 + c + 2)
            for t in range(8):
                px = PX[:, t % 2, :]
                e.wait_ge(rg_act, 8 + t + 1)
                w = [gain(0, PG["conv_w"] + 8 * j + t) for j in range(4)]
                chain(e.tensor_scalar(XB[:, t, :], px[:, 0:S], w[0], gain(0, PG["conv_b"] + t), ALU.mult, ALU.add))
                for j in (1, 2):
                    chain(e.scalar_tensor_tensor(XB[:, t, :], px[:, j:j + S], w[j], XB[:, t, :], ALU.mult, ALU.add))
                e.scalar_tensor_tensor(XB[:, t, :], px[:, 3:3 + S], w[3], XB[:, t, :], ALU.mult, ALU.add)\
                    .then_inc(rg_dve, 1)
                if t % 2:
                    dve_lo(e, n0 + 4 + t // 2 + 2)
            for t in range(8):
                e.wait_ge(rg_act, RA_XH + t + 1)
                e.tensor_tensor(h_lo[:, t, :], XB[:, t, :], h_hi[:, t, :].bitcast(F32), ALU.subtract)\
                    .then_inc(rg_dve, 1)
            e.wait_ge(act_step, 4)
            chain(e.tensor_tensor(c8[:, 16:24], c8[:, 16:24], c8[:, 24:32], ALU.add))
            e.tensor_scalar(c8[:, 32:40], c8[:, 16:24], RG_C, None, ALU.mult).then_inc(rg_dve, 1)
            e.tensor_scalar(c8[:, 40:48], c8[:, 16:24], -RG_C, None, ALU.mult).then_inc(rg_dve, 1)
            for g in range(2):
                dve_lo(e, n0 + 8 + g + 2)
            def low(t):
                e.wait_ge(rg_act, RA_YH_OF[t])
                e.tensor_tensor(h_lo[:, t, :], Y[:, t, :], h_hi[:, t, :].bitcast(F32), ALU.subtract)\
                    .then_inc(rg_dve, 1)
            for t in range(8):
                e.wait_ge(rg_pool, 9 + t + 1)
                e.wait_ge(rg_act, RA_EXP[t])
                chain(e.tensor_tensor(XB[:, t, :], GI[:, t, :], tmp[:, t, :], ALU.mult))
                chain(e.tensor_tensor_scan(tmp[:, t, :], RR[:, t, :], XB[:, t, :], 0.0, ALU.mult, ALU.add))
                e.tensor_tensor(Y[:, t, :], Y[:, t, :], tmp[:, t, :], ALU.mult).then_inc(rg_dve, 1)
                if t:
                    low(t - 1)
            low(7)
            dve_out(e, "rg_out", True)

        def pool_rg(e):
            for j in range(2):
                ins = e.memset(PX[:, j, 0:3], 0.0)
            ins.then_inc(rg_pool, 1)
            for t in range(8):
                e.wait_ge(rg_act, RA_I + t + 1)
                e.wait_ge(rg_dve, 8 + t + 1)
                e.tensor_tensor(GI[:, t, :], GI[:, t, :], XB[:, t, :], ALU.mult).then_inc(rg_pool, 1)
            for t in range(8):
                e.wait_ge(rg_pool, 1 + t + 1)
                e.wait_ge(rg_act, RA_SQ + t + 1)
                e.tensor_tensor(GI[:, t, :], GI[:, t, :], uz[:, t, :], ALU.mult).then_inc(rg_pool, 1)

        na_proj, na_act, na_dve, na_pool, na_pe = (sem("na_proj"), sem("na_act"), sem("na_dve"), sem("na_pool"),
                                                   sem("na_pe"))
        sc_pe, sc_dve, sc_act = sem("sc_pe"), sem("sc_dve"), sem("sc_act")
        tr_pe, tr_act = sem("tr_pe"), sem("tr_act")
        pv_pe, cb_dve = sem("pv_pe"), sem("cb_dve")
        cm_pe, cm_dve, cm_max, cm_act = sem("cm_pe"), sem("cm_dve"), sem("cm_max"), sem("cm_act")
        bias_pool = sem("bias_pool")
        o = 0
        qT = tiles(o, 8); o += 8 * S
        zc = tiles(o, 4); o += 4 * S
        ksT = tiles(o, 2); o += 2 * S
        kwT = tiles(o, 2); o += 2 * S
        vs = tiles(o, QT, 256); o += QT * 256
        vw = tiles(o, QT, 256); o += QT * 256
        gates = tiles(o, QT, 48); o += QT * 48
        gz = tiles(o, 2, NC + 1); o += 2 * (NC + 1)
        kcT = tiles(o, 2, NC + 1); o += 2 * (NC + 1)
        vcr = tiles(o, 2, P); o += 2 * P
        dist = arena[:, o:o + S]; o += S
        cdist = tiles(o, QT, NC + 1); o += QT * (NC + 1)
        gw = tiles(o, KT, 48); o += KT * 48
        w2bd = tiles(o, 2, P); o += 2 * P
        peT = tiles(o, 2, CMP_LEN); o += 2 * CMP_LEN
        negm = tiles(o, 2, 4); o += 8
        sums = tiles(o, 4, 4); o += 16
        rr = tiles(o, 2, 4); o += 8
        bias_h = tiles(o, 2); o += 2 * S
        cb_h = tiles(o, 2, QT * (NC + 1)); o += 2 * QT * (NC + 1)
        cs = tiles(o, QT, NC + 1); o += QT * (NC + 1)
        csT = arena[:, o:o + S]; o += S
        cmx = arena[:, o:o + QT]; o += QT
        csum = arena[:, o:o + QT]; o += QT
        cout = tiles(o, QT, HD); o += QT * HD
        perow = cout.rearrange("p t n -> p (t n)").rearrange("p (z n) -> p z n", z=2)
        bgate = arena[0:48, o:o + 1]; o += 1
        gT = csT[0:48, :]
        zadd = nc.alloc_sbuf_tensor_at("zadd", [P, 24, S], F32, offset=zone)
        zA, zB = (zadd[:, 17:19, :], zadd[:, 0:2, :]), (zadd[:, 21:23, :], zadd[:, 2:4, :])
        assert o <= AR
        w1bd = [fsum[:, :, :].rearrange("p t n -> p (t n)").rearrange("p (l e) -> p l e", e=P),
                tmp[:, :, :].rearrange("p t n -> p (t n)").rearrange("p (l e) -> p l e", e=P)]
        orow = xrows
        UNITS = HEADS * QT

        def pool_nsa(e, chain):
            c0 = chain.n
            chain(e.memset(fsum[:, :, :], 0.0))
            chain(e.memset(tmp[:, :, :], 0.0))
            chain(e.memset(w2bd[:, :, :], 0.0))
            for z, (w1, w2, pe_) in enumerate(((a["nsa_w1_k"], a["nsa_w2_k"], a["nsa_pe_k"]),
                                               (a["nsa_w1_v"], a["nsa_w2_v"], a["nsa_pe_v"]))):
                for h in range(2):
                    r = slice(h * HD, h * HD + HD)
                    e.dma_start(w1bd[z][r, :, r], w1[0].rearrange("(l d) e -> d l e", d=HD)).then_inc(small_in, 16)
                    e.dma_start(w2bd[r, z, r], w2[0]).then_inc(small_in, 16)
                    e.dma_start(perow[0:CMP_LEN, z, r], pe_[0]).then_inc(small_in, 16)
            e.dma_start(gw[:, :, :], cols(nsa_in, D + 6 * 256, 48)).then_inc(small_in, 16)
            e.dma_start(bgate, a["nsa_b_gate"].rearrange("o n -> n o")).then_inc(small_in, 16)
            chain(e.iota(dist, pattern=[[1, S]], base=-3 * P, channel_multiplier=-1,
                         allow_small_or_imprecise_dtypes=True))
            chain(e.affine_select(out=dist, in_=dist, compare_op=ALU.is_ge, fill=BIG, base=3 * P,
                                  pattern=[[-1, S]], channel_multiplier=1))
            chain(e.iota(cdist[:, :, 0:NC], pattern=[[-P, QT], [CMP_STRIDE, NC]], base=CMP_LEN - 1,
                         channel_multiplier=-1, allow_small_or_imprecise_dtypes=True))
            chain(e.affine_select(out=cdist[:, :, 0:NC], in_=cdist[:, :, 0:NC], compare_op=ALU.is_ge, fill=BIG,
                                  base=1 - CMP_LEN, pattern=[[P, QT], [-CMP_STRIDE, NC]], channel_multiplier=1))
            for h in range(HEADS):
                slope = 2.0 ** (-8.0 * (h + 1) / HEADS)
                if h >= 2:
                    e.wait_ge(sc_dve, 4 * (h - 1))
                    e.wait_ge(cm_dve, 3 * (h - 2) + 1)
                e.tensor_scalar(bias_h[:, h % 2, :], dist, slope, None, ALU.mult)
                e.tensor_scalar(cb_h[:, h % 2, :].rearrange("p (t n) -> p t n", t=QT)[:, :, 0:NC],
                                cdist[:, :, 0:NC], slope, None, ALU.mult).then_inc(bias_pool, 1)

        SMALL_NSA = 16 * 14

        def pe_nsa(pe, stage):
            n0 = where["nsa_in"]
            t = 0
            for c in range(10):
                def free(m):
                    if t + m >= 8:
                        pe.wait_ge(na_proj, t + m - 7)
                if c == 0:
                    pe_first(pe, n0, stage)
                    t += 2
                elif c < 8:
                    pe_chunk(pe, n0 + c, KT, 2, h_hi, h_lo, lambda m: pbank[(t + m) % 8][:, :], free)
                    t += 2
                else:
                    pe_rows(pe, n0 + c, lambda m: pbank[(t + m) % 8][:, 0:256], free)
                    t += 4
            pe.wait_ge(small_in, SMALL_NSA)
            pe.wait_ge(na_proj, 24)
            for z in range(2):
                ins = pe.transpose(pbank[1][:, z * 32:z * 32 + 32], perow[0:CMP_LEN, z, :], ident[0:32, 0:32])
            ins.then_inc(na_pe, 1)
            pe.wait_ge(na_dve, 1)
            for k in range(KT):
                gk = slice(k * 48, k * 48 + 48)
                ins = three(pe, pbank[0][0:48, :], u_hi[:, 0, gk], u_lo[:, 0, gk], h_hi[:, k, :], h_lo[:, k, :], k == 0,
                            k == KT - 1)
            ins.then_inc(na_pe, 1)
            for z in range(2):
                o62 = pbank[2 + z][:, 0:2 * NC].rearrange("p (t n) -> p t n", t=2)
                pe.wait_ge(na_dve, 2 + z)
                for l in range(CMP_LEN):
                    src = (zA, zB)[l // CMP_STRIDE][z]
                    ins = pe.matmul(o62, w1bd[z][:, l, :], src[:, :, l:l + CMP_STRIDE * (NC - 1) + 1:CMP_STRIDE],
                                    start=l == 0, stop=l == CMP_LEN - 1)
                ins.then_inc(na_pe, 1)
                if z == 0:
                    pe.wait_ge(na_act, 3)
                    for q in range(QT):
                        ins = pe.transpose(pbank[6][:, q * 48:q * 48 + 48], gT[:, q * P:q * P + P], ident[0:48, 0:48])
                    ins.then_inc(na_pe, 1)
                    pe.wait_ge(na_act, 4)
                    pe.matmul(pbank[4][:, 0:2 * NC].rearrange("p (t n) -> p t n", t=2), w2bd[:, 0, :],
                              gz[:, :, 0:NC], start=True, stop=True).then_inc(na_pe, 1)
                else:
                    pe.wait_ge(na_act, 6)
                    for t2 in range(2):
                        ins = pe.matmul(pbank[5][0:NC, t2 * P:t2 * P + P], gz[:, t2, 0:NC], w2bd[:, 1, :],
                                        start=True, stop=True)
                    ins.then_inc(na_pe, 1)
            pe.wait_ge(na_act, 8)

            def scores(u):
                h, q = u // QT, u % QT
                t2, half, g = h // 8, (h // 4) % 2, h % 4
                r = slice(half * HD, half * HD + HD)
                nk = (q + 1) * P
                lhs = qT[r, 4 * t2 + g, q * P:q * P + P]
                if u >= 2:
                    pe.wait_ge(sc_dve, u - 1)
                pe.matmul(pbank[u % 2][:, 0:nk], lhs, ksT[r, t2, 0:nk], start=True, stop=True)
                pe.matmul(pbank[2 + u % 2][:, 0:nk], lhs, kwT[r, t2, 0:nk], start=True, stop=True).then_inc(sc_pe, 1)

            def turn(u):
                q, p = u % QT, u % 2
                pe.wait_ge(sc_act, u + 1)
                if u >= 1:
                    pe.wait_ge(tr_act, u)
                for b in range(2):
                    for k in range(q + 1):
                        kk = slice(k * P, k * P + P)
                        ins = pe.transpose(pbank[4 + b][:, kk], tmp[:, 2 * b + p, kk], ident[:, :])
                ins.then_inc(tr_pe, 1)

            def values(u):
                h, q, p = u // QT, u % QT, u % 2
                t2, G = h // 8, h // 4
                pe.wait_ge(tr_act, u + 1)
                if u >= 1:
                    pe.wait_ge(cb_dve, u)
                for b, v in enumerate((vs, vw)):
                    for k in range(q + 1):
                        ins = pe.matmul(pbank[7][:, b * HD:b * HD + HD], tmp[:, 4 + 2 * b + p, k * P:k * P + P], v[:, k, G * HD:G * HD + HD],
                                        start=k == 0, stop=k == q)
                ins.then_inc(pv_pe, 1)
            def compressed(h, part):
                t2, half, g = h // 8, (h // 4) % 2, h % 4
                r = slice(half * HD, half * HD + HD)
                if part == 0:
                    if h:
                        pe.wait_ge(cm_dve, 3 * h)
                    for q in range(QT):
                        ins = pe.matmul(pbank[6][:, 32 * q:32 * q + NC], qT[r, 4 * t2 + g, q * P:q * P + P],
                                        kcT[r, t2, 0:NC], start=True, stop=True)
                elif part == 1:
                    pe.wait_ge(cm_dve, 3 * h + 1)
                    pe.wait_ge(cm_act, h + 1)
                    for q in range(QT):
                        ins = pe.transpose(pbank[6][0:NC, q * P:q * P + P], cs[:, q, 0:NC], ident[:, :])
                else:
                    pe.wait_ge(cm_dve, 3 * h + 2)
                    for q in range(QT):
                        ins = pe.matmul(pbank[6][:, q * HD:q * HD + HD], csT[0:NC, q * P:q * P + P],
                                        vcr[0:NC, t2, half * HD:half * HD + HD], start=True, stop=True)
                ins.then_inc(cm_pe, 1)
            for u in range(UNITS + 2):
                if u >= 5 and u % QT == 1:
                    compressed(u // QT - 1, 2)
                if u >= 4 and u % QT == 0:
                    compressed(u // QT - 1, 1)
                if u < UNITS:
                    scores(u)
                if u < UNITS and u % QT == 3:
                    compressed(u // QT, 0)
                if 1 <= u <= UNITS:
                    turn(u - 1)
                if u >= 2:
                    values(u - 2)
            pe.wait_ge(cb_dve, UNITS)
            pe.wait_ge(cm_dve, 3 * HEADS)
            for k in range(KT):
                for q in range(QT):
                    ins = pe.transpose(pbank[k][:, q * P:q * P + P], orow[:, q, k * P:k * P + P], ident[:, :])
                ins.then_inc(na_pe, 1)
            pe.wait_ge(na_dve, 3 + KT)
            pe_out(pe, "nsa_out")

        def act_nsa(e, chain):
            n0 = where["nsa_in"]
            dst = [zc[:, j, :] for j in range(4)] + [qT[:, j, :] for j in range(8)] + [ksT[:, 0, :], ksT[:, 1, :],
                   kwT[:, 0, :], kwT[:, 1, :]] + [vs[:, j, :] for j in range(4)] + [vw[:, j, :] for j in range(4)]
            t = 0
            for c in range(10):
                for m in range(2 if c < 8 else 4):
                    e.wait_ge(tiles_out, before[n0 + c] + m + 1)
                    e.activation(dst[t], pbank[t % 8][:, 0:256 if c >= 8 else S], ACT.Copy,
                                 scale=HD ** -0.5 if 4 <= t < 12 else 1.0).then_inc(na_proj, 1)
                    t += 1
                act_hi(e, n0 + c + 2)
            e.wait_ge(small_in, SMALL_NSA)
            e.activation(u_hi[:, 0, 0:KT * 48], gw[:, :, :].rearrange("p k n -> p (k n)"), ACT.Copy).then_inc(na_act, 1)
            e.wait_ge(na_pe, 1)
            e.activation(peT[:, :, :].rearrange("p z l -> p (z l)"), pbank[1][:, 0:64], ACT.Copy).then_inc(na_act, 1)
            e.wait_ge(na_pe, 2)
            e.activation(gT, pbank[0][0:48, :], ACT.Sigmoid, bias=bgate).then_inc(na_act, 1)
            for z in range(2):
                e.wait_ge(na_pe, 3 + 3 * z)
                e.activation(gz[:, :, 0:NC], pbank[2 + z][:, 0:2 * NC].rearrange("p (t n) -> p t n", t=2),
                             ACT.Gelu_apprx_tanh).then_inc(na_act, 1)
                if z == 0:
                    e.wait_ge(na_pe, 4)
                    e.activation(gates[:, :, :].rearrange("p q n -> p (q n)"), pbank[6][:, 0:QT * 48], ACT.Copy)\
                        .then_inc(na_act, 1)
            e.wait_ge(na_pe, 7)
            e.activation(kcT[:, :, 0:NC], pbank[4][:, 0:2 * NC].rearrange("p (t n) -> p t n", t=2), ACT.Copy)\
                .then_inc(na_act, 1)
            e.activation(vcr[0:NC, :, :].rearrange("p t n -> p (t n)"), pbank[5][0:NC, 0:2 * P], ACT.Copy)\
                .then_inc(na_act, 1)
            for u in range(UNITS + 1):
                if u < UNITS:
                    q, p = u % QT, u % 2
                    nk = (q + 1) * P
                    e.wait_ge(sc_dve, u + 1)
                    if u >= 4:
                        e.wait_ge(cb_dve, u - 3)
                    for b, s_ in enumerate((tmp[:, p, 0:nk], tmp[:, 2 + p, 0:nk])):
                        ins = e.activation(s_, s_, ACT.Exp, bias=negm[:, p, b:b + 1], scale=-1.0,
                                           accum_out=sums[:, u % 4, b:b + 1])
                    ins.then_inc(sc_act, 1)
                if u < UNITS and u % QT == 3:
                    h = u // QT
                    e.wait_ge(cm_max, h + 1)
                    e.activation(cs[:, :, 0:NC], cs[:, :, 0:NC], ACT.Exp).then_inc(cm_act, 1)
                if u >= 1:
                    v = u - 1
                    nk = (v % QT + 1) * P
                    e.wait_ge(tr_pe, v + 1)
                    if v >= 2:
                        e.wait_ge(pv_pe, v - 1)
                    e.activation(tmp[:, 4 + v % 2, 0:nk], pbank[4][:, 0:nk], ACT.Copy)
                    e.activation(tmp[:, 6 + v % 2, 0:nk], pbank[5][:, 0:nk], ACT.Copy).then_inc(tr_act, 1)
            for k in range(KT):
                e.wait_ge(na_pe, 8 + k)
                e.activation(h_hi[:, k, :], pbank[k][:, :], ACT.Copy).then_inc(na_act, 1)
            act_out(e, "nsa_out")

        def dve_nsa(e, chain):
            n0 = where["nsa_in"]
            for c in range(10):
                dve_lo(e, n0 + c + 2)
            e.wait_ge(na_act, 1)
            e.tensor_tensor(u_lo[:, 0, 0:KT * 48], gw[:, :, :].rearrange("p k n -> p (k n)"),
                            u_hi[:, 0, 0:KT * 48].bitcast(F32), ALU.subtract).then_inc(na_dve, 1)
            e.wait_ge(na_proj, 4)
            e.wait_ge(na_act, 2)
            for z in range(2):
                if z:
                    e.wait_ge(na_pe, 2)
                for half, dst in ((0, zA[z]), (1, zB[z])):
                    for t in range(2):
                        pos = peT[:, z, half * CMP_STRIDE:(half + 1) * CMP_STRIDE].unsqueeze(1)
                        ins = e.tensor_tensor(dst[:, t, :].rearrange("p (n l) -> p n l", l=CMP_STRIDE),
                                              zc[:, 2 * z + t, :].rearrange("p (n l) -> p n l", l=CMP_STRIDE),
                                              pos.broadcast_to([P, S // CMP_STRIDE, CMP_STRIDE]), ALU.add)
                ins.then_inc(na_dve, 1)

            def masked(u):
                h, q, p = u // QT, u % QT, u % 2
                nk = (q + 1) * P
                e.wait_ge(sc_pe, u + 1)
                e.wait_ge(bias_pool, h + 1)
                if u >= 2:
                    e.wait_ge(tr_pe, u - 1)
                for b, (dst, src, bias) in enumerate((
                        (tmp[:, p, 0:nk], pbank[p][:, 0:nk], bias_h[:, h % 2, S - nk:S]),
                        (tmp[:, 2 + p, 0:nk], pbank[2 + p][:, 0:nk], bias_h[:, h % 2, S - nk:S]))):
                    ins = e.tensor_tensor_reduce(dst, src, bias, -1.0, -BIG, ALU.add, ALU.min,
                                                 negm[:, p, b:b + 1])
                ins.then_inc(sc_dve, 1)

            def combine(v):
                h, q, p = v // QT, v % QT, v % 2
                e.wait_ge(sc_act, v + 1)
                chain(e.tensor_scalar(rr[:, p, 0:2], sums[:, v % 4, 0:2], 1e-30, None, ALU.max))
                chain(e.reciprocal(rr[:, p, 0:2], rr[:, p, 0:2]))
                chain(e.tensor_tensor(rr[:, p, 0:2], rr[:, p, 0:2], gates[:, q, 3 * h + 1:3 * h + 3], ALU.mult))
                e.wait_ge(pv_pe, v + 1)
                dst = orow[:, q, h * HD:h * HD + HD]
                chain(e.tensor_scalar(dst, pbank[7][:, 0:HD], rr[:, p, 0:1], None, ALU.mult))
                e.scalar_tensor_tensor(dst, pbank[7][:, HD:2 * HD], rr[:, p, 1:2], dst, ALU.mult, ALU.add)\
                    .then_inc(cb_dve, 1)

            def compressed(h, part):
                cb = cb_h[:, h % 2, :].rearrange("p (t n) -> p t n", t=QT)[:, :, 0:NC]
                c = cs[:, :, 0:NC]
                if part == 0:
                    e.wait_ge(cm_pe, 3 * h + 1)
                    e.tensor_tensor(c, pbank[6][:, 0:P].rearrange("p (q n) -> p q n", q=QT)[:, :, 0:NC], cb,
                                    ALU.add).then_inc(cm_dve, 1)
                    e.wait_ge(cm_dve, 3 * h + 1)
                    chain(e.tensor_reduce(cmx, c, AX.X, ALU.max))
                    chain(e.tensor_scalar(cmx, cmx, BIG * 1e-10, None, ALU.max))
                    e.tensor_tensor(c, c, cmx.unsqueeze(2).broadcast_to([P, QT, NC]), ALU.subtract)\
                        .then_inc(cm_max, 1)
                elif part == 1:
                    e.wait_ge(cm_pe, 3 * h + 2)
                    e.tensor_copy(csT[0:NC, :], pbank[6][0:NC, :]).then_inc(cm_dve, 1)
                    chain(e.tensor_reduce(csum, c, AX.X, ALU.add))
                    chain(e.tensor_scalar(csum, csum, 1e-30, None, ALU.max))
                    chain(e.reciprocal(csum, csum))
                    chain(e.tensor_tensor(csum, csum, gates[:, :, 3 * h], ALU.mult))
                else:
                    e.wait_ge(cm_pe, 3 * h + 3)
                    chain(e.tensor_tensor(cout, pbank[6][:, 0:QT * HD].rearrange("p (q n) -> p q n", q=QT),
                                          csum.unsqueeze(2).broadcast_to([P, QT, HD]), ALU.mult))
                    e.wait_ge(cb_dve, QT * h + QT)
                    dst = orow[:, :, h * HD:h * HD + HD]
                    e.tensor_tensor(dst, dst, cout, ALU.add).then_inc(cm_dve, 1)
            for u in range(UNITS + 3):
                if u >= 3:
                    combine(u - 3)
                if u < UNITS:
                    masked(u)
                if u >= 4 and u % QT == 0:
                    compressed(u // QT - 1, 1)
                if u >= 6 and u % QT == 2:
                    compressed(u // QT - 1, 2)
                if u < UNITS and u % QT == 3:
                    compressed(u // QT, 0)
            for k in range(KT):
                e.wait_ge(na_act, 9 + k)
                e.tensor_tensor(h_lo[:, k, :], pbank[k][:, :], h_hi[:, k, :].bitcast(F32), ALU.subtract)\
                    .then_inc(na_dve, 1)
            dve_out(e, "nsa_out", True)

        class Steps:

            def __init__(self, name, names):
                self.sem, self.names, self.n = sem(name), names, 0
                self.index = {s: i for i, s in enumerate(names)}

            def done(self, ins, s):
                assert self.names[self.n % len(self.names)] == s, (s, self.names[self.n % len(self.names)])
                self.n += 1
                ins.then_inc(self.sem, 1)

            def wait(self, e, s, turn=0):
                e.wait_ge(self.sem, turn * len(self.names) + self.index[s] + 1)

        A_H = 4
        ev_proj, ev_dve, ev_act, ev_pe = sem("ev_proj"), sem("ev_dve"), sem("ev_act"), sem("ev_pe")
        dsc_pe, dsc_dve, dsc_act = sem("dsc_pe"), sem("dsc_dve"), sem("dsc_act")
        dtr_pe, dtr_act, dtr_dve, dpv_pe, dcb_dve = (sem("dtr_pe"), sem("dtr_act"), sem("dtr_dve"), sem("dpv_pe"),
                                                     sem("dcb_dve"))
        dbias_pool = sem("dbias_pool")
        qa, ka, va = tiles(0, 4), tiles(4 * S, 4), tiles(8 * S, QT)
        ddist, dbias = arena[:, 12 * S:13 * S], tiles(13 * S, 4)
        lamv = arena[:, 17 * S:17 * S + 4 * HD]
        o = 17 * S + 4 * HD
        lams = arena[:, o:o + 8]; o += 8
        dnegm, dsums, drr = tiles(o, 2, 2), tiles(o + 4, 4, 2), tiles(o + 12, 2, 2); o += 16
        dss = arena[:, o:o + 16]; o += 16
        DUNITS = A_H * QT

        zs = tiles(0, 14)
        o = 14 * S
        wa_up, g_up = arena[:, o:o + S], arena[:, o + S:o + 2 * S]; o += 2 * S
        cmask = arena[:, o:o + S]; o += S
        m_up, m_upd, m_low = arena[:, o:o + P], arena[:, o + P:o + 2 * P], arena[:, o + 2 * P:o + 3 * P]; o += 3 * P
        lmask = tiles(o, 6, P); o += 6 * P
        bones = arena[:, o:o + P]; o += P
        ident2 = arena[:, o:o + HD]; o += HD
        PAD = o
        X_ = tiles(o, 9); o += 9 * S
        assert o <= AR, o
        rz = nc.alloc_sbuf_tensor_at("rz", [P, 24, S], F32, offset=zone)
        MUL = ALU.mult

        def padded(j):
            return arena[:, PAD + j * (S + 8):PAD + j * (S + 8) + S + 1]

        def pool_even(e, chain):
            e.dma_start(lamv, a["diff_lam_2"].rearrange("a l d -> a (l d)").broadcast_to([P, 4 * HD]))\
                .then_inc(small_in, 16)
            chain(e.iota(ddist, pattern=[[1, S]], base=-3 * P, channel_multiplier=-1,
                         allow_small_or_imprecise_dtypes=True))
            chain(e.tensor_scalar(dbias[:, 0, :], ddist, 0.0, 2.0, ALU.min, MUL))
            chain(e.tensor_tensor(ddist, dbias[:, 0, :], ddist, ALU.subtract))
            chain(e.memset(ddist[0:RCH, S - RCH:S], BIG))
            for h in range(A_H):
                e.tensor_scalar(dbias[:, h, :], ddist, 2.0 ** (-8.0 / A_H * (h + 1)), None, MUL)\
                    .then_inc(dbias_pool, 1)
            e.wait_ge(ev_dve, 2)
            e.wait_ge(ev_proj, 20)
            e.dma_start(wa_up[0:HD, :], a["rwkv_w_up_2"][0]).then_inc(small_in, 16)
            e.dma_start(wa_up[HD:P, :], a["rwkv_a_up_2"][0]).then_inc(small_in, 16)
            e.dma_start(g_up, a["rwkv_g_up_2"][0]).then_inc(small_in, 16)
            for j in range(2):
                chain(e.memset(padded(j)[:, 0:1], 0.0))
            chain(e.memset(cmask, 1.0))
            chain(e.memset(cmask.rearrange("p (c t) -> p c t", t=RCH)[:, :, 0:1], 0.0))

            def block_ones(m, b):
                v = m.rearrange("p (c f) -> p c f", f=b)
                chain(e.memset(m, 1.0))
                chain(e.affine_select(out=v, in_=v, compare_op=ALU.is_ge, fill=0.0, base=0,
                                      pattern=[[-b, P // b], [0, b]], channel_multiplier=1))
                chain(e.affine_select(out=v, in_=v, compare_op=ALU.is_ge, fill=0.0, base=b - 1,
                                      pattern=[[b, P // b], [0, b]], channel_multiplier=-1))
            block_ones(bones, RCH)
            for j in range(6):
                block_ones(lmask[:, j, :], 2 << j)
            for j in range(5, 0, -1):
                chain(e.tensor_tensor(lmask[:, j, :], lmask[:, j, :], lmask[:, j - 1, :], ALU.subtract))
            chain(e.tensor_tensor(lmask[:, 0, :], lmask[:, 0, :], ident[:, :], ALU.subtract))
            chain(e.affine_select(out=m_up, in_=bones, compare_op=ALU.is_gt, fill=0.0, base=0, pattern=[[1, P]],
                                  channel_multiplier=-1))
            chain(e.affine_select(out=m_upd, in_=bones, compare_op=ALU.is_ge, fill=0.0, base=0, pattern=[[1, P]],
                                  channel_multiplier=-1))
            chain(e.affine_select(out=m_low, in_=bones, compare_op=ALU.is_gt, fill=0.0, base=0, pattern=[[-1, P]],
                                  channel_multiplier=1))
            for j in range(2):
                chain(e.tensor_copy(ident2[j * HD:j * HD + HD, :], ident[j * HD:j * HD + HD, j * HD:j * HD + HD]))
            e.tensor_copy(ident2[:, 0:1], ident2[:, 0:1]).then_inc(dbias_pool, 1)
            rwkv_pool(e)

        EV_SMALL = (SMALL_NSA if any(s[0] == "nsa" for s in PLAN) else 0)

        def pe_even(pe, stage):
            n0 = where["even_a"]
            t = 0
            for c in range(6):
                def free(m):
                    if t + m >= 8:
                        pe.wait_ge(ev_proj, t + m - 7)
                if c == 0:
                    pe_first(pe, n0, stage)
                    t += 2
                elif c < 4:
                    pe_chunk(pe, n0 + c, KT, 2, h_hi, h_lo, lambda m: pbank[(t + m) % 8][:, :], free)
                    t += 2
                else:
                    pe_rows(pe, n0 + c, lambda m: pbank[(t + m) % 8][:, 0:256], free)
                    t += 4
            pe.wait_ge(ev_proj, 16)

            def scores(u):
                h, q = u // QT, u % QT
                nk = (q + 1) * P
                if u >= 2:
                    pe.wait_ge(dsc_dve, u - 1)
                for m in range(2):
                    r = slice(m * HD, m * HD + HD)
                    ins = pe.matmul(pbank[2 * m + u % 2][:, 0:nk], qa[r, h, q * P:q * P + P], ka[r, h, 0:nk],
                                    start=True, stop=True)
                ins.then_inc(dsc_pe, 1)

            def turn(u):
                q, p = u % QT, u % 2
                pe.wait_ge(dsc_act, u + 1)
                if u >= 1:
                    pe.wait_ge(dtr_act, u)
                    pe.wait_ge(dtr_dve, u)
                for b in range(2):
                    for k in range(q + 1):
                        kk = slice(k * P, k * P + P)
                        ins = pe.transpose(pbank[4 + b][:, kk], tmp[:, 2 * b + p, kk], ident[:, :])
                ins.then_inc(dtr_pe, 1)

            def values(u):
                h, q, p = u // QT, u % QT, u % 2
                pe.wait_ge(dtr_act, u + 1)
                pe.wait_ge(dtr_dve, u + 1)
                if u >= 1:
                    pe.wait_ge(dcb_dve, u)
                for b in range(2):
                    for k in range(q + 1):
                        ins = pe.matmul(pbank[7][:, b * P:b * P + P], tmp[:, 4 + 2 * b + p, k * P:k * P + P],
                                        va[:, k, h * P:h * P + P], start=k == 0, stop=k == q)
                ins.then_inc(dpv_pe, 1)
            for u in range(DUNITS + 2):
                if u < DUNITS:
                    scores(u)
                if 1 <= u <= DUNITS:
                    turn(u - 1)
                if u >= 2:
                    values(u - 2)
            pe.wait_ge(ev_dve, 1)
            for h in range(A_H):
                for q in range(QT):
                    ins = pe.transpose(pbank[h][:, q * P:q * P + P], xrows[:, q, h * P:h * P + P], ident[:, :])
                ins.then_inc(ev_pe, 1)
            n1 = where["even_b"]
            for c in range(7):
                def free(m):
                    t = 2 * c + m
                    if t < 4:
                        pe.wait_ge(ev_proj, 17 + t)
                    if t >= 8:
                        pe.wait_ge(ev_proj, 20 + t - 7)
                pe_chunk(pe, n1 + c, KT, 2, h_hi, h_lo, lambda m: pbank[(2 * c + m) % 8][:, :], free)
            pe.wait_ge(small_in, EV_SMALL + 64)
            pe.wait_ge(dbias_pool, 5)
            pe.wait_ge(ev_proj, 34)
            rwkv_pe(pe)
            pe.wait_ge(ev_dve, 2 + 14 + KT)
            pe_out(pe, "even_out")

        def act_even(e, chain):
            n0 = where["even_a"]
            dst = [qa[:, j, :] for j in range(4)] + [ka[:, j, :] for j in range(4)] + \
                [va[:, j, 0:256] for j in range(4)] + [va[:, j, 256:512] for j in range(4)]
            t = 0
            for c in range(6):
                for m in range(2 if c < 4 else 4):
                    e.wait_ge(tiles_out, before[n0 + c] + m + 1)
                    e.activation(dst[t], pbank[t % 8][:, 0:256 if c >= 4 else S], ACT.Copy,
                                 scale=HD ** -0.5 if t < 4 else 1.0).then_inc(ev_proj, 1)
                    t += 1
                act_hi(e, n0 + c + 2)
            e.wait_ge(dve_even_l.sem, dve_even_l.index["dots"] + 1)
            e.activation(lams[:, 2:4], lams[:, 0:2], ACT.Exp).then_inc(ev_act, 1)
            for u in range(DUNITS + 1):
                if u < DUNITS:
                    q, p = u % QT, u % 2
                    nk = (q + 1) * P
                    e.wait_ge(dsc_dve, u + 1)
                    if u >= 4:
                        e.wait_ge(dcb_dve, u - 3)
                    for b in range(2):
                        s_ = tmp[:, 2 * b + p, 0:nk]
                        ins = e.activation(s_, s_, ACT.Exp, bias=dnegm[:, p, b:b + 1], scale=-1.0,
                                           accum_out=dsums[:, u % 4, b:b + 1])
                    ins.then_inc(dsc_act, 1)
                if u >= 1:
                    v = u - 1
                    nk = (v % QT + 1) * P
                    e.wait_ge(dtr_pe, v + 1)
                    if v >= 2:
                        e.wait_ge(dpv_pe, v - 1)
                    e.activation(tmp[:, 4 + v % 2, 0:nk], pbank[4][:, 0:nk], ACT.Copy).then_inc(dtr_act, 1)
            e.wait_ge(dcb_dve, DUNITS)
            e.activation(dss, dss, ACT.Sqrt, bias=eps[:, 0:1], scale=1.0 / P).then_inc(ev_act, 1)
            for h in range(A_H):
                e.wait_ge(ev_pe, h + 1)
                e.activation(fsum[:, 2 * h + 1, :], pbank[h][:, :], ACT.Copy, scale=lams[:, 6:7]).then_inc(ev_proj, 1)
            n1 = where["even_b"]
            for c in range(7):
                for m in range(2):
                    t = 2 * c + m
                    e.wait_ge(tiles_out, before[n1 + c] + m + 1)
                    if t < 2:
                        e.wait_ge(dbias_pool, 5)
                    else:
                        e.wait_ge(ev_dve, 2 + t - 1)
                    e.activation(padded(t % 2)[:, 1:S + 1], pbank[t % 8][:, :], ACT.Copy).then_inc(ev_proj, 1)
                act_hi(e, n1 + c + 2)
            e.wait_ge(ev_dve, 2 + 14)
            e.activation(zs[0:HD, 12, :], zs[0:HD, 12, :], ACT.Tanh)
            e.activation(zs[:, 13, :], zs[:, 13, :], ACT.Sigmoid).then_inc(ev_act, 1)
            rwkv_act(e)
            w_dve.wait(e, "out", 3)
            for k in range(KT):
                src = fsum[:, 2 * k + 1, :] if k < 4 else zs[:, k - 4, :]
                e.activation(h_hi[:, k, :], src, ACT.Copy).then_inc(ev_act, 1)
            act_out(e, "even_out")

        dve_even_l = Steps("lam_dots", ["dots", "lam"])

        def dve_even(e, chain):
            n0 = where["even_a"]
            e.wait_ge(small_in, EV_SMALL + 16)
            for j in range(2):
                ins = e.tensor_tensor_reduce(lamv[:, 2 * j * HD:2 * j * HD + HD], lamv[:, 2 * j * HD:2 * j * HD + HD],
                                             lamv[:, (2 * j + 1) * HD:(2 * j + 2) * HD], 1.0, 0.0, ALU.mult, ALU.add,
                                             lams[:, j:j + 1])
            dve_even_l.done(ins, "dots")
            for c in range(6):
                dve_lo(e, n0 + c + 2)
            e.wait_ge(ev_act, 1)
            chain(e.tensor_tensor(lams[:, 4:5], lams[:, 3:4], lams[:, 2:3], ALU.subtract))
            chain(e.tensor_scalar(lams[:, 5:6], lams[:, 4:5], -(0.8 - 0.6), None, ALU.add))
            dve_even_l.done(e.tensor_scalar(lams[:, 6:7], gain(1, PSUB), 1.0 - (0.8 - 0.6), None, ALU.mult), "lam")

            def masked(u):
                h, q, p = u // QT, u % QT, u % 2
                nk = (q + 1) * P
                e.wait_ge(dsc_pe, u + 1)
                e.wait_ge(dbias_pool, h + 1)
                if u >= 2:
                    e.wait_ge(dtr_pe, u - 1)
                for b in range(2):
                    ins = e.tensor_tensor_reduce(tmp[:, 2 * b + p, 0:nk], pbank[2 * b + p][:, 0:nk],
                                                 dbias[:, h, S - nk:S], -1.0, -BIG, ALU.add, ALU.min,
                                                 dnegm[:, p, b:b + 1])
                ins.then_inc(dsc_dve, 1)

            def take(v):
                q, p = v % QT, v % 2
                nk = (q + 1) * P
                e.wait_ge(dtr_pe, v + 1)
                if v >= 2:
                    e.wait_ge(dpv_pe, v - 1)
                e.tensor_copy(tmp[:, 6 + p, 0:nk], pbank[5][:, 0:nk]).then_inc(dtr_dve, 1)

            def combine(v):
                h, q, p = v // QT, v % QT, v % 2
                e.wait_ge(dsc_act, v + 1)
                chain(e.reciprocal(drr[:, p, :], dsums[:, v % 4, :]))
                chain(e.tensor_tensor(drr[:, p, 1:2], drr[:, p, 1:2], lams[:, 5:6], ALU.mult))
                e.wait_ge(dpv_pe, v + 1)
                dst = xrows[:, q, h * P:h * P + P]
                chain(e.tensor_scalar(dst, pbank[7][:, 0:P], drr[:, p, 0:1], None, ALU.mult))
                chain(e.scalar_tensor_tensor(dst, pbank[7][:, P:2 * P], drr[:, p, 1:2], dst, ALU.mult, ALU.add))
                chain(e.tensor_tensor(xrows[:, q, 512 + h * P:512 + h * P + P], dst, dst, ALU.mult))
                e.tensor_reduce(dss[:, v:v + 1], xrows[:, q, 512 + h * P:512 + h * P + P], AX.X, ALU.add)\
                    .then_inc(dcb_dve, 1)
            for u in range(DUNITS + 3):
                if u >= 3:
                    combine(u - 3)
                if u < DUNITS:
                    masked(u)
                if 1 <= u <= DUNITS:
                    take(u - 1)
            e.wait_ge(ev_act, 2)
            chain(e.reciprocal(dss, dss))
            for v in range(DUNITS):
                dst = xrows[:, v % QT, (v // QT) * P:(v // QT) * P + P]
                ins = e.tensor_scalar(dst, dst, dss[:, v:v + 1], None, ALU.mult)
            ins.then_inc(ev_dve, 1)
            e.wait_ge(ev_pe, A_H)
            e.drain().then_inc(ev_dve, 1)
            n1 = where["even_b"]
            for t in range(14):
                z = padded(t % 2)
                e.wait_ge(ev_proj, 21 + t)
                chain(e.tensor_tensor(tmp[:, t % 2, :], z[:, 0:S], z[:, 1:S + 1], ALU.subtract))
                e.scalar_tensor_tensor(zs[:, t, :], tmp[:, t % 2, :], gain(1, PMU + t), z[:, 1:S + 1],
                                       ALU.mult, ALU.add).then_inc(ev_dve, 1)
                if t % 2:
                    dve_lo(e, n1 + t // 2 + 2)
            rwkv_dve(e)
            for k in range(KT):
                src = fsum[:, 2 * k + 1, :] if k < 4 else zs[:, k - 4, :]
                e.wait_ge(ev_act, 3 + k + 1)
                e.tensor_tensor(h_lo[:, k, :], src, h_hi[:, k, :].bitcast(F32), ALU.subtract).then_inc(ev_dve, 1)
            dve_out(e, "even_out", False)

        LEV = range(1, 6)
        HH = range(2)
        w_pe = Steps("w_pe", ["w", "a", "g", "kk", "bonus", "t_al", "t_bh", "t_kh", "t_v"]
                     + [f"m{i}{h}" for h in HH for i in range(5)]
                     + ["rhs0", "rhs1"]
                     + [f"{x_}{l}{h}" for l in LEV for x_, hs in ((("U"), HH), (("D"), HH)) for h in hs]
                     + ["P0", "P1", "QT", "Y1", "MT", "N"] + [f"s{c}" for c in range(1, 8)] + ["mean", "var"])
        w_act = Steps("w_act", ["sw", "aa", "sq", "kkrt", "ec", "enc", "ecp", "gg", "tokB", "tokK", "rhs0", "rhs1"]
                      + [f"U{l}{h}" for l in LEV for h in HH] + ["P0", "Y1", "N", "ysq", "yrt"])
        w_dve = Steps("w_dve", ["kk0", "lw", "c", "cp", "ka", "kp", "max", "rec", "kk", "al", "ka2", "be", "kt", "rt",
                                "bh", "kh", "rkr", "tokA", "tokV"]
                      + [f"m{i}{h}" for h in HH for i in range(5)] + ["bon"]
                      + [f"D{l}{h}" for l in LEV for h in HH]
                      + ["P1", "QT", "MT", "s0"] + [f"s{c}" for c in range(1, 7)]
                      + ["y", "yc", "yrec", "yn", "yb", "yg", "out"])
        w_pool = Steps("w_pool", ["D0", "D1"] + [f"gb{l}{h}" for l in LEV for h in HH] + ["rhs0", "rhs1"])
        wlw, wc, wcp, waa, wkk, wsq, wrt, wkp = (tmp[:, j, :] for j in range(8))
        ec, enc, ecp, al, be, kt_, rt, bh, kh = (X_[:, j, :] for j in range(9))
        gg = enc
        tokA, tokB, tokK, tokV = (fsum[:, 2 * j, :].rearrange("p (j n) -> p j n", j=QT) for j in range(4))
        NN, YY, ST, bon, yc, ysq, yrs = wlw, wc, wcp, waa, wkk, wsq, wrt

        def hz(h, j):
            return rz[:, 11 * h + j, :].rearrange("p (j n) -> p j n", j=QT)
        MATS = [[hz(h, j) for j in range(5)] for h in HH]
        Dm, DTm, Um, Gb, RHS, PM = ([hz(h, j) for h in HH] for j in range(5, 11))
        QTt, MTt = rz[:, 22, :], rz[:, 23, :]

        def wide(m):
            return m.unsqueeze(1).broadcast_to([P, QT, P])

        def rwkv_pe(pe):
            for p in range(4):
                cp_ = slice(p * P, p * P + P)
                if p:
                    w_dve.wait(pe, "out", p - 1)
                else:
                    pe.wait_ge(ev_act, 3)
                w_pe.done(pe.matmul(pbank[0][:, :], wa_up[0:HD, cp_], zs[0:HD, 12, :], start=True, stop=True), "w")
                w_pe.done(pe.matmul(pbank[1][:, :], wa_up[HD:P, cp_], zs[HD:P, 12, :], start=True, stop=True), "a")
                w_pe.done(pe.matmul(pbank[2][:, :], g_up[:, cp_], zs[:, 13, :], start=True, stop=True), "g")
                w_act.wait(pe, "sq", p)
                w_pe.done(pe.matmul(pbank[3][:, :], bones, wsq, start=True, stop=True), "kk")
                w_dve.wait(pe, "rkr", p)
                w_pe.done(pe.matmul(pbank[4][:, :], bones, wsq, start=True, stop=True), "bonus")
                w_act.wait(pe, "gg", p)
                for name, src, b in (("t_al", al, 5), ("t_bh", bh, 6), ("t_kh", kh, 7), ("t_v", zs[:, 8 + p, :], 0)):
                    for j in range(QT):
                        ins = pe.transpose(pbank[b][:, j * P:j * P + P], src[:, j * P:j * P + P], ident[:, :])
                    w_pe.done(ins, name)
                w_act.wait(pe, "kkrt", p)
                k = 0
                for h in HH:
                    r = slice(h * HD, h * HD + HD)
                    for i, (l_, r_) in enumerate(((be, al), (be, rt), (kt_, al), (kt_, rt), (al, be))):
                        b = (1, 2, 3, 0, 5, 6, 7, 1, 2, 3)[k]
                        if b in (0, 5):
                            w_dve.wait(pe, "tokV", p)
                        if b in (6, 7):
                            w_act.wait(pe, "tokK", p)
                        if k >= 7:
                            w_dve.wait(pe, f"m{(k - 7) % 5}{(k - 7) // 5}", p)
                        for j in range(QT):
                            q = slice(j * P, j * P + P)
                            ins = pe.matmul(pbank[b][:, q], l_[r, q], r_[r, q], start=True, stop=True)
                        w_pe.done(ins, f"m{i}{h}")
                        k += 1
                w_dve.wait(pe, "bon", p)
                for h in HH:
                    for j in range(QT):
                        ins = pe.matmul(pbank[6 + h][:, j * HD:j * HD + HD], MATS[h][2][:, j, :],
                                        tokV[:, j, h * HD:h * HD + HD], start=True, stop=True)
                    w_pe.done(ins, f"rhs{h}")
                for l in LEV:
                    for h in HH:
                        w_pool.wait(pe, f"gb{l}{h}", p)
                        if l > 1:
                            w_dve.wait(pe, f"D{l - 1}{h}", p)
                        for j in range(QT):
                            ins = pe.matmul(pbank[h][:, j * P:j * P + P], Gb[h][:, j, :], Dm[h][:, j, :], start=True,
                                            stop=True)
                        w_pe.done(ins, f"U{l}{h}")
                    for h in HH:
                        w_act.wait(pe, f"U{l}{h}", p)
                        for j in range(QT):
                            q = slice(j * P, j * P + P)
                            if l < 5:
                                pe.matmul(pbank[2 + h][:, q], DTm[h][:, j, :], Um[h][:, j, :], start=True, stop=True)
                            ins = pe.matmul(pbank[4 + h][:, q], Um[h][:, j, :], DTm[h][:, j, :], start=True, stop=True)
                        w_pe.done(ins, f"D{l}{h}")
                for h in HH:
                    w_dve.wait(pe, f"D5{h}", p)
                    w_act.wait(pe, f"rhs{h}", p)
                    w_pool.wait(pe, f"rhs{h}", p)
                    for j in range(QT):
                        ins = pe.matmul(pbank[h][:, j * P:j * P + P], DTm[h][:, j, :], RHS[h][:, j, :], start=True,
                                        stop=True)
                    w_pe.done(ins, f"P{h}")
                w_act.wait(pe, "P0", p)
                w_dve.wait(pe, "P1", p)
                for h in HH:
                    for j in range(QT):
                        ins = pe.matmul(pbank[2][h * HD:h * HD + HD, j * P:j * P + P], PM[h][:, j, HD:P],
                                        MATS[h][1][:, j, :], start=True, stop=True)
                w_pe.done(ins, "QT")
                for h in HH:
                    for j in range(QT):
                        o_ = pbank[3][h * HD:h * HD + HD, j * P:j * P + P]
                        pe.matmul(o_, tokV[:, j, h * HD:h * HD + HD], MATS[h][3][:, j, :], start=True, stop=False)
                        ins = pe.matmul(o_, PM[h][:, j, 0:HD], MATS[h][1][:, j, :], start=False, stop=True)
                w_pe.done(ins, "Y1")
                for c in range(8):
                    rr_ = slice((c % 2) * HD, (c % 2) * HD + HD)
                    for h in HH:
                        r = slice(h * HD, h * HD + HD)
                        ins = pe.matmul(pbank[(4, 1)[c % 2]][r, c * HD:c * HD + HD], PM[h][rr_, c // 2, HD:P], tokB[rr_, c // 2, r],
                                        start=True, stop=True)
                w_pe.done(ins, "MT")
                for c in range(8):
                    rr_ = slice((c % 2) * HD, (c % 2) * HD + HD)
                    for h in HH:
                        r = slice(h * HD, h * HD + HD)
                        o_ = pbank[(5, 7)[c % 2]][r, c * HD:c * HD + HD]
                        pe.matmul(o_, tokB[rr_, c // 2, r], PM[h][rr_, c // 2, 0:HD], start=True, stop=False)
                        ins = pe.matmul(o_, tokK[rr_, c // 2, r], tokV[rr_, c // 2, r], start=False, stop=True)
                w_pe.done(ins, "N")
                w_dve.wait(pe, "MT", p)
                for c in range(1, 8):
                    w_dve.wait(pe, f"s{c - 1}", p)
                    st = ST[:, ((c - 1) % 2) * HD:((c - 1) % 2) * HD + HD]
                    for h in HH:
                        r = slice(h * HD, h * HD + HD)
                        q = slice(c * HD, c * HD + HD)
                        if c < 7:
                            pe.matmul(pbank[7][r, 0:HD], MTt[r, q], st[r, :], start=True, stop=True)
                        ins = pe.matmul(pbank[6][r, q], st[r, :], QTt[r, q], start=True, stop=True)
                    w_pe.done(ins, f"s{c}")
                w_dve.wait(pe, "y", p)
                w_pe.done(pe.matmul(pbank[0][:, :], bones, YY, start=True, stop=True), "mean")
                w_act.wait(pe, "ysq", p)
                w_pe.done(pe.matmul(pbank[1][:, :], bones, ysq, start=True, stop=True), "var")

        def rwkv_act(e):
            for p in range(4):
                def par_(j):
                    return gain(2, PVEC + 4 * j + p)
                if p:
                    w_dve.wait(e, "out", p - 1)
                w_pe.wait(e, "w", p)
                w_act.done(e.activation(wlw, pbank[0][:, :], ACT.Sigmoid, bias=par_(0)), "sw")
                w_pe.wait(e, "a", p)
                w_act.done(e.activation(waa, pbank[1][:, :], ACT.Sigmoid, bias=par_(1)), "aa")
                w_dve.wait(e, "kk0", p)
                w_act.done(e.activation(wsq, wkk, ACT.Square), "sq")
                w_pe.wait(e, "kk", p)
                w_act.done(e.activation(wrt, pbank[3][:, :], ACT.Sqrt), "kkrt")
                w_dve.wait(e, "cp", p)
                w_act.done(e.activation(ec, wc, ACT.Exp), "ec")
                w_act.done(e.activation(enc, wc, ACT.Exp, scale=-1.0), "enc")
                w_act.done(e.activation(ecp, wcp, ACT.Exp), "ecp")
                w_pe.wait(e, "g", p)
                w_dve.wait(e, "kt", p)
                w_act.done(e.activation(gg, pbank[2][:, :], ACT.Copy), "gg")
                for name, dst, b in (("tokB", tokB, 6), ("tokK", tokK, 7)):
                    w_pe.wait(e, {"tokB": "t_bh", "tokK": "t_kh"}[name], p)
                    w_act.done(e.activation(dst.rearrange("p j n -> p (j n)"), pbank[b][:, :], ACT.Copy), name)
                for h in HH:
                    w_pe.wait(e, f"rhs{h}", p)
                    w_act.done(e.activation(RHS[h][:, :, 0:HD], pbank[6 + h][:, 0:4 * HD].rearrange(
                        "p (j n) -> p j n", j=QT), ACT.Copy), f"rhs{h}")
                for l in LEV:
                    for h in HH:
                        w_pe.wait(e, f"U{l}{h}", p)
                        w_act.done(e.activation(Um[h].rearrange("p j n -> p (j n)"), pbank[h][:, :], ACT.Copy),
                                   f"U{l}{h}")
                w_pe.wait(e, "P0", p)
                w_act.done(e.activation(PM[0].rearrange("p j n -> p (j n)"), pbank[0][:, :], ACT.Copy), "P0")
                w_pe.wait(e, "Y1", p)
                w_act.done(e.activation(YY, pbank[3][:, :], ACT.Copy), "Y1")
                w_pe.wait(e, "N", p)
                for j in range(2):
                    ins = e.activation(*(m.rearrange("p (c j n) -> p j c n", j=2, n=HD)[:, j]
                                         for m in (NN, pbank[(5, 7)[j]][:, :])), ACT.Copy)
                w_act.done(ins, "N")
                w_dve.wait(e, "yc", p)
                w_act.done(e.activation(ysq, yc, ACT.Square), "ysq")
                w_pe.wait(e, "var", p)
                w_act.done(e.activation(yrs, pbank[1][:, :], ACT.Sqrt, bias=eps[:, 1:2], scale=1.0 / HD), "yrt")

        def rwkv_pool(e):
            for p in range(4):
                for h in HH:
                    w_dve.wait(e, f"m4{h}", p)
                    for src, dst in ((MATS[h][4], Dm[h]), (MATS[h][0], DTm[h])):
                        e.tensor_tensor(dst, src, wide(lmask[:, 0, :]), ALU.mult).then_inc(rw_own, 1)
                    e.wait_ge(rw_own, 4 * (2 * p + h) + 2)
                    for dst in (Dm[h], DTm[h]):
                        ins = e.tensor_tensor(dst, dst, wide(ident[:, :]), ALU.add)
                        ins.then_inc(rw_own, 1) if dst is Dm[h] else w_pool.done(ins, f"D{h}")
                    e.wait_ge(rw_own, 4 * (2 * p + h) + 3)
                    e.drain().then_inc(rw_own, 1)
                for l in LEV:
                    for h in HH:
                        if l > 1:
                            w_pe.wait(e, f"U{l - 1}{h}", p)
                        w_pool.done(e.tensor_tensor(Gb[h], MATS[h][0], wide(lmask[:, l, :]), ALU.mult), f"gb{l}{h}")
                for h in HH:
                    w_dve.wait(e, "tokA", p)
                    w_pool.done(e.tensor_copy(RHS[h][:, :, HD:P], tokA[:, :, h * HD:h * HD + HD]), f"rhs{h}")

        rw_own = sem("rw_own")

        def rwkv_dve(e):
            def do(ins, name, chain=True):
                w_dve.done(ins, name)
                if chain:
                    e.wait_ge(w_dve.sem, w_dve.n)
            for p in range(4):
                def par_(j):
                    return gain(2, PVEC + 4 * j + p)
                zr, zk, zv = zs[:, p, :], zs[:, 4 + p, :], zs[:, 8 + p, :]
                do(e.tensor_scalar(wkk, zk, par_(2), None, MUL), "kk0")
                w_act.wait(e, "sw", p)
                do(e.tensor_scalar(wlw, wlw, -math.exp(-0.5), None, MUL), "lw")
                do(e.tensor_tensor_scan(wc, cmask, wlw, 0.0, MUL, ALU.add), "c")
                do(e.tensor_tensor(wcp, wc, wlw, ALU.subtract), "cp", False)
                w_act.wait(e, "aa", p)
                do(e.tensor_scalar(wkp, waa, 1.0, par_(3), ALU.subtract, MUL), "ka")
                do(e.scalar_tensor_tensor(wkp, wkp, 1.0, zk, ALU.add, MUL), "kp", False)
                w_act.wait(e, "kkrt", p)
                do(e.tensor_scalar(wrt, wrt, 1e-12, None, ALU.max), "max")
                do(e.reciprocal(wrt, wrt), "rec")
                do(e.tensor_tensor(wkk, wkk, wrt, MUL), "kk")
                w_act.wait(e, "ecp", p)
                do(e.scalar_tensor_tensor(al, wkk, -1.0, ecp, MUL, MUL), "al", False)
                do(e.tensor_tensor(wrt, wkk, waa, MUL), "ka2")
                do(e.tensor_tensor(be, wrt, enc, MUL), "be", False)
                do(e.tensor_tensor(kt_, wkp, enc, MUL), "kt")
                do(e.tensor_tensor(rt, zr, ec, MUL), "rt")
                last = ec.rearrange("p (c t) -> p c t", t=RCH)[:, :, RCH - 1:RCH].broadcast_to([P, 8, RCH])
                for name, dst, src in (("bh", bh, be), ("kh", kh, kt_)):
                    do(e.tensor_tensor(dst.rearrange("p (c t) -> p c t", t=RCH),
                                       src.rearrange("p (c t) -> p c t", t=RCH), last, MUL), name, False)
                w_pe.wait(e, "kk", p)
                do(e.scalar_tensor_tensor(wsq, zr, par_(4), wkp, MUL, MUL), "rkr")
                for name, src, dst, b in (("tokA", "t_al", tokA, 5), ("tokV", "t_v", tokV, 0)):
                    w_pe.wait(e, src, p)
                    do(e.tensor_copy(dst.rearrange("p j n -> p (j n)"), pbank[b][:, :]), name, False)
                k = 0
                for h in HH:
                    for i in range(5):
                        b = (1, 2, 3, 0, 5, 6, 7, 1, 2, 3)[k]
                        m = (m_up, m_upd, m_up, m_upd, m_low)[i]
                        w_pe.wait(e, f"m{i}{h}", p)
                        do(e.tensor_tensor(MATS[h][i], pbank[b][:, :].rearrange("p (j n) -> p j n", j=QT), wide(m), MUL),
                           f"m{i}{h}", False)
                        k += 1
                do(e.tensor_tensor(bon, pbank[4][:, :], zv, MUL), "bon")
                for l in LEV:
                    for h in HH:
                        w_pool.wait(e, f"D{h}", p)
                        e.wait_ge(rw_own, 4 * (2 * p + h) + 4)
                        w_pe.wait(e, f"D{l}{h}", p)
                        if l < 5:
                            dfl = Dm[h].rearrange("p j n -> p (j n)")
                            e.tensor_tensor(dfl, dfl, pbank[2 + h][:, :], ALU.add)
                        dfl = DTm[h].rearrange("p j n -> p (j n)")
                        do(e.tensor_tensor(dfl, dfl, pbank[4 + h][:, :], ALU.add), f"D{l}{h}", False)
                w_pe.wait(e, "P1", p)
                do(e.tensor_copy(PM[1].rearrange("p j n -> p (j n)"), pbank[1][:, :]), "P1", False)
                w_pe.wait(e, "QT", p)
                do(e.tensor_tensor(QTt, pbank[2][:, :], rt, ALU.add), "QT", False)
                w_pe.wait(e, "MT", p)
                for c in range(8):
                    q = slice(c * HD, c * HD + HD)
                    ins = e.scalar_tensor_tensor(MTt[:, q], ident2, ec[:, c * HD + HD - 1:c * HD + HD],
                                                 pbank[(4, 1)[c % 2]][:, q],
                                                 MUL, ALU.add)
                do(ins, "MT", False)
                w_act.wait(e, "N", p)
                do(e.tensor_copy(ST[:, 0:HD], NN[:, 0:HD]), "s0", False)
                for c in range(1, 7):
                    w_pe.wait(e, f"s{c}", p)
                    o_ = ST[:, (c % 2) * HD:(c % 2) * HD + HD]
                    do(e.tensor_tensor(o_, pbank[7][:, 0:HD], NN[:, c * HD:c * HD + HD], ALU.add), f"s{c}", False)
                w_pe.wait(e, "s7", p)
                do(e.tensor_tensor(YY[:, HD:S], YY[:, HD:S], pbank[6][:, HD:S], ALU.add), "y")
                w_pe.wait(e, "mean", p)
                do(e.scalar_tensor_tensor(yc, pbank[0][:, :], -1.0 / HD, YY, MUL, ALU.add), "yc", False)
                w_act.wait(e, "yrt", p)
                do(e.reciprocal(yrs, yrs), "yrec")
                do(e.scalar_tensor_tensor(yc, yc, par_(5), yrs, MUL, MUL), "yn")
                do(e.scalar_tensor_tensor(yc, yc, par_(6), bon, ALU.add, ALU.add), "yb")
                do(e.tensor_tensor(yc, yc, gg, MUL), "yg")
                do(e.tensor_copy(zr, yc), "out")

        C_H = 4
        od_proj, od_dve, od_pe, od_act, od_pool = (sem("od_proj"), sem("od_dve"), sem("od_pe"), sem("od_act"),
                                                   sem("od_pool"))
        rdist = arena[:, 0:S]
        rdec = tiles(S, 4)
        rq, rk = tiles(5 * S, 2), tiles(7 * S, 2)
        rv = tiles(9 * S, QT)
        rg = tiles(13 * S, 4)
        rp = tmp
        ry = tiles(17 * S, 4)
        rsq = tiles(21 * S, 4)
        rrt = arena[:, 25 * S:26 * S]
        ryn = tiles(26 * S, 3)

        def pool_odd(e, chain):
            chain(e.iota(rdist, pattern=[[1, S]], base=0, channel_multiplier=-1,
                         allow_small_or_imprecise_dtypes=True))
            chain(e.tensor_scalar(rk[:, 0, :], rdist, 0.0, 2.0, ALU.min, MUL))
            chain(e.tensor_tensor(rdist, rk[:, 0, :], rdist, ALU.subtract))
            e.tensor_copy(rdist[:, 0:1], rdist[:, 0:1]).then_inc(od_pool, 1)
            e.wait_ge(od_act, C_H)
            for h in range(C_H):
                ins = e.memset(rdec[RCH:P, h, 0:RCH], 0.0)
            ins.then_inc(od_pool, 1)

        def odd_chunks(h):
            n = where["odd"] + 2 + 8 * h
            return range(n, n + 4), range(n + 4, n + 6 if h < C_H - 1 else n + 4), \
                range(n + 6, n + 8) if h < C_H - 1 else range(n + 4, n + 6)

        QK_BANK = (1, 2, 3, 0)

        def pe_odd(pe, stage):
            pe_first(pe, where["odd"], stage)
            pe_chunk(pe, where["odd"] + 1, KT, 2, h_hi, h_lo, lambda m: pbank[2 + m][:, :])
            for h in range(C_H):
                vg, qk, wo = odd_chunks(h)
                b0 = 4 + 16 * h

                def free_v(m):
                    if h:
                        pe.wait_ge(od_dve, 20 * (h - 1) + 12 + m + 1)
                    elif m < 4:
                        pe.wait_ge(od_proj, m + 1)
                for c in range(2):
                    pe_rows(pe, vg[c], lambda m: pbank[4 * c + m][:, 0:256], lambda m: free_v(4 * c + m))
                pe_chunk(pe, vg[2], KT, 2, h_hi, h_lo, lambda m: pbank[4 + m][:, :],
                         lambda m: pe.wait_ge(od_proj, b0 + 4 + m + 1))
                for k in range(QT):
                    for j in range(2):
                        ins = pe.matmul(pbank[k][:, 0:S - k * P], rk[:, j, k * P:k * P + P], rq[:, j, k * P:S],
                                        start=j == 0, stop=j == 1)
                    ins.then_inc(od_pe, 1)
                pe_chunk(pe, vg[3], KT, 2, h_hi, h_lo, lambda m: pbank[6 + m][:, :],
                         lambda m: pe.wait_ge(od_proj, b0 + 6 + m + 1))
                for t in range(4):
                    pe.wait_ge(od_proj, b0 + 8 + t + 1)
                    for k in range(QT):
                        if t == 0:
                            pe.wait_ge(od_dve, 20 * h + k + 1)
                        ins = pe.matmul(pbank[4 + t][:, k * P:S], rv[:, k, t * P:t * P + P], rp[:, k, 0:S - k * P],
                                        start=k == 0, stop=k == QT - 1, skip_group_check=True)
                    ins.then_inc(od_pe, 1)
                for t in range(4):
                    pe.wait_ge(od_act, C_H + 10 * h + t + 1)
                    ins = pe.matmul(pbank[0][:, :], ones[:, :], rsq[:, t, :], start=t == 0, stop=t == 3)
                ins.then_inc(od_pe, 1)
                for c, n in enumerate(qk):
                    def free_qk(m):
                        if 2 * c + m == 3:
                            pe.wait_ge(od_act, C_H + 10 * h + 5)
                    pe_chunk(pe, n, KT, 2, h_hi, h_lo, lambda m: pbank[QK_BANK[2 * c + m]][:, :], free_qk)
                if h < C_H - 1:
                    pe.wait_ge(od_proj, b0 + 16)
                pe.wait_ge(od_dve, 20 * h + 12)
                for c, n in enumerate(wo):
                    pe_chunk(pe, n, 4, 4, u_hi, u_lo, lambda m: pbank[4 * c + m][:, :])

        def act_odd(e, chain):
            e.wait_ge(od_pool, 1)
            for h in range(C_H):
                e.activation(rdec[:, h, :], rdist, ACT.Exp, scale=-math.log(1.0 - 2.0 ** (-5.0 - h))).then_inc(od_act, 1)

            def take_qk(n, c, banks):
                for m in range(2):
                    t = 2 * c + m
                    e.wait_ge(tiles_out, before[n] + m + 1)
                    e.activation((rq, rk)[c][:, m, :], pbank[banks[t]][:, :], ACT.Copy, scale=(1.0, 256 ** -0.5)[c])\
                        .then_inc(od_proj, 1)
                act_hi(e, n + 2)
            for c in range(2):
                take_qk(where["odd"] + c, c, range(4))
            for h in range(C_H):
                vg, qk, wo = odd_chunks(h)
                if h:
                    e.wait_ge(od_dve, 20 * h)
                for c in range(2):
                    for m in range(QT):
                        e.wait_ge(tiles_out, before[vg[c]] + m + 1)
                        e.activation(rv[:, m, 256 * c:256 * c + 256], pbank[4 * c + m][:, 0:256], ACT.Copy)\
                            .then_inc(od_proj, 1)
                    act_hi(e, vg[c] + 2)
                for t in range(4):
                    n = vg[2 + t // 2]
                    e.wait_ge(tiles_out, before[n] + t % 2 + 1)
                    e.activation(rg[:, t, :], pbank[4 + t][:, :], ACT.Silu).then_inc(od_proj, 1)
                    if t % 2:
                        act_hi(e, n + 2)
                for t in range(4):
                    e.wait_ge(od_pe, 9 * h + 4 + t + 1)
                    e.activation(rsq[:, t, :], pbank[4 + t][:, :], ACT.Square).then_inc(od_act, 1)
                e.wait_ge(od_pe, 9 * h + 9)
                e.activation(rrt, pbank[0][:, :], ACT.Sqrt, bias=eps[:, 0:1], scale=1.0 / 512).then_inc(od_act, 1)
                for t in range(4):
                    e.wait_ge(od_dve, 20 * h + 4 + t + 1)
                    e.activation(u_hi[:, t, :], ry[:, t, :], ACT.Copy).then_inc(od_act, 1)
                for c, n in enumerate(qk):
                    take_qk(n, c, QK_BANK)
                act_hi(e, wo[0] + 2)
                if h < C_H - 1:
                    act_hi(e, wo[1] + 2)
                e.drain().then_inc(od_act, 1)

        def dve_odd(e, chain):
            for c in range(2):
                dve_lo(e, where["odd"] + c + 2)
            e.wait_ge(od_pool, 2)
            for h in range(C_H):
                vg, qk, wo = odd_chunks(h)
                for c in range(3):
                    dve_lo(e, vg[c] + 2)
                for k in range(QT):
                    e.wait_ge(od_pe, 9 * h + k + 1)
                    w = S - k * P
                    e.tensor_tensor(rp[:, k, 0:w], pbank[k][:, 0:w], rdec[:, h, 0:w], MUL).then_inc(od_dve, 1)
                dve_lo(e, vg[3] + 2)
                e.wait_ge(od_act, C_H + 10 * h + 5)
                chain(e.reciprocal(rrt, rrt))
                for t in range(4):
                    chain(e.tensor_tensor(ry[:, t, :], pbank[4 + t][:, :], rrt, MUL))
                    e.tensor_tensor(ry[:, t, :], ry[:, t, :], rg[:, t, :], MUL).then_inc(od_dve, 1)
                for t in range(4):
                    e.wait_ge(od_act, C_H + 10 * h + 5 + t + 1)
                    e.tensor_tensor(u_lo[:, t, :], ry[:, t, :], u_hi[:, t, :].bitcast(F32), ALU.subtract)\
                        .then_inc(od_dve, 1)
                for n in qk:
                    dve_lo(e, n + 2)
                for c, n in enumerate(wo):
                    for m in range(4):
                        e.wait_ge(tiles_out, before[n] + m + 1)
                        t = 4 * c + m
                        if h == 0:
                            ins = e.tensor_copy(fsum[:, t, :], pbank[t][:, :])
                        else:
                            ins = e.tensor_tensor(fsum[:, t, :], fsum[:, t, :], pbank[t][:, :], ALU.add)
                        ins.then_inc(od_dve, 1)
                    if c == 0 or h < C_H - 1:
                        dve_lo(e, n + 2)

        block = ctx.enter_context(nc.Block())

        @block.sync
        def _(sp):
            sp_setup(sp)
            n = 0
            for stage, step in enumerate(PLAN):
                if step[0] == "ffn":
                    sp_ffn(sp, step[1])
                    n = where[step[1]] + FFN[step[1]]["groups"] * (FFN[step[1]]["gu"] + 1)
                while n < TOTAL and stream[n][0] is not None and n < ends[stage]:
                    load_chunk(sp, n, None, 0, 0)
                    n += 1
                if step[0] == "store":
                    sp_store(sp, stage)

        @block.gpsimd
        def _(pool):
            chain = Chain(pool, pool_step)
            for stage, step in enumerate(PLAN):
                enter(pool, stage, step[0] in ("rg", "nsa", "even", "odd"))
                if step[0] == "setup":
                    pool_setup(pool, chain)
                elif step[0] == "rg":
                    pool_rg(pool)
                elif step[0] == "nsa":
                    pool_nsa(pool, chain)
                elif step[0] == "even":
                    pool_even(pool, chain)
                elif step[0] == "odd":
                    pool_odd(pool, chain)
                elif step[0] in ("norm", "norm_x", "post"):
                    pool_norm(pool, stage)
                    if step[0] == "norm" and PLAN[stage + 1][0] == "ffn" and FFN[PLAN[stage + 1][1]]["swiglu"]:
                        if PLAN[stage - 1][0] == "post":
                            pool.wait_ge(n_hn, norm_base[stage - 1] + KT)
                        pool.memset(fsum[:, :, :], 0.0).then_inc(cleared, 1)
                leave(pool, "pool")

        @block.scalar
        def _(act):
            chain = Chain(act, act_step)
            act_hi(act, 0)
            act_hi(act, 1)
            for stage, step in enumerate(PLAN):
                enter(act, stage)
                if step[0] == "norm":
                    act_norm(act, stage, step[1], True)
                elif step[0] == "norm_x":
                    act_norm(act, stage, x, False)
                elif step[0] == "post":
                    act_norm(act, stage, fsum, False)
                elif step[0] == "ffn":
                    act_ffn(act, step[1])
                elif step[0] == "rg":
                    act_rg(act, chain)
                elif step[0] == "nsa":
                    act_nsa(act, chain)
                elif step[0] == "even":
                    act_even(act, chain)
                elif step[0] == "odd":
                    act_odd(act, chain)
                elif step[0] == "store":
                    act_store(act)
                leave(act, "act")

        @block.vector
        def _(dve):
            chain = Chain(dve, dve_step)
            dve_lo(dve, 0)
            dve_lo(dve, 1)
            for stage, step in enumerate(PLAN):
                enter(dve, stage)
                if step[0] == "setup":
                    dve_setup(dve)
                elif step[0] == "norm":
                    dve_norm(dve, stage, step[1], step[2], step[3], True, chain)
                elif step[0] == "norm_x":
                    dve_norm(dve, stage, x, step[1], step[2], False, chain)
                elif step[0] == "post":
                    dve_post(dve, stage, step[1], step[2], step[3], chain)
                elif step[0] == "ffn":
                    dve_ffn(dve, step[1], stage)
                elif step[0] == "rg":
                    dve_rg(dve, chain)
                elif step[0] == "nsa":
                    dve_nsa(dve, chain)
                elif step[0] == "even":
                    dve_even(dve, chain)
                elif step[0] == "odd":
                    dve_odd(dve, chain)
                elif step[0] == "store":
                    dve_store(dve)
                leave(dve, "dve")

        @block.tensor
        def _(pe):
            for stage, step in enumerate(PLAN):
                enter(pe, stage)
                if step[0] == "setup":
                    pe_setup(pe)
                elif step[0] in ("norm", "norm_x", "post"):
                    pe_norm(pe, stage)
                elif step[0] == "ffn":
                    pe_ffn(pe, step[1], stage)
                elif step[0] == "rg":
                    pe_rg(pe, stage)
                elif step[0] == "nsa":
                    pe_nsa(pe, stage)
                elif step[0] == "even":
                    pe_even(pe, stage)
                elif step[0] == "odd":
                    pe_odd(pe, stage)
                elif step[0] == "store":
                    pe_store(pe, stage)
                leave(pe, "pe")


_INS = ["x", "norm_mix", "norm_ffn", "norm_final", "rg_w_in", "rg_conv_w", "rg_conv_b", "rg_w_a", "rg_b_a",
        "rg_w_x", "rg_b_x", "rg_lambda", "rg_w_out", "nsa_w_in", "nsa_b_gate", "nsa_pe_k", "nsa_pe_v",
        "nsa_w1_k", "nsa_w2_k", "nsa_w1_v", "nsa_w2_v", "nsa_w_out", "mlp_w_up", "mlp_w_down", "norms_2",
        "ffn_wgu_2", "ffn_wd_2", "even_w_in_2", "even_w_out_2", "diff_lam_2", "diff_subln_2", "rwkv_mu_2",
        "rwkv_vec_2", "rwkv_w_up_2", "rwkv_a_up_2", "rwkv_g_up_2", "odd_w_in_2", "odd_w_out_2"]


def kernel(**inputs):
    import numpy as _np
    import concourse.bacc as _bacc
    from concourse import mybir as _mybir
    from concourse.bass_utils import run_bass_kernel_spmd as _run

    nc = _bacc.Bacc("TRN2", target_bir_lowering=False, num_devices=1)
    arrays, args = {}, {}
    for name in _INS:
        a = _np.ascontiguousarray(inputs[name])
        arrays[f"in_{name}"] = a
        args[name] = nc.dram_tensor(f"in_{name}", a.shape, _mybir.dt.from_np(a.dtype), kind="ExternalInput").ap()
    out = nc.dram_tensor("out_x", (1, S, D), _mybir.dt.float32, kind="ExternalOutput").ap()
    build(nc, args, out)
    r = _run(nc, [arrays], core_ids=[0])
    return r.results[0]["out_x"]
```
